# Optimizing a Trainium2 kernel written in Bass

```python
import jax, jax.numpy as jnp
from jax import lax
import numpy as np
import math

D_MODEL = 1024
BATCH = 1
SEQ = 512
DEPTH = 1

CONV_DIM = 1024
CONV_KERNEL = 31
CONV_PAD = (CONV_KERNEL - 1) // 2
N_HEADS = 16
N_KV_HEADS = 4
HEAD_DIM = 64
ATTN_DIM = N_HEADS * HEAD_DIM
KV_DIM = N_KV_HEADS * HEAD_DIM
WINDOW = 128
BLOCK = 128
NEG_INF = -1e30
N_BRANCH = 2
IN_DIM = 2 * CONV_DIM + ATTN_DIM + 2 * KV_DIM + N_BRANCH * D_MODEL
PEER_HEADS = 8
PEER_KEY_DIM = 256
PEER_HALF = PEER_KEY_DIM // 2
N_KEYS = 128
N_EXPERTS = N_KEYS * N_KEYS
PEER_TOPK = 16
TOKEN_CHUNK = 128
EPS = 1e-6


def rmsnorm(x, g):
    xf = x.astype(jnp.float32)
    y = xf * lax.rsqrt(jnp.mean(xf * xf, axis=-1, keepdims=True) + EPS)
    return (y * g.astype(jnp.float32)).astype(x.dtype)

def layernorm(x, g, b):
    xf = x.astype(jnp.float32)
    mu = jnp.mean(xf, axis=-1, keepdims=True)
    var = jnp.mean(jnp.square(xf - mu), axis=-1, keepdims=True)
    y = (xf - mu) * lax.rsqrt(var + EPS)
    return (y * g.astype(jnp.float32) + b.astype(jnp.float32)).astype(x.dtype)

def conformer_conv(a_in, dw_w, dw_b, ln_g, ln_b, w_pw):
    u = a_in[..., :CONV_DIM] * jax.nn.sigmoid(a_in[..., CONV_DIM:])
    u = lax.conv_general_dilated(
        u, dw_w[:, None, :], window_strides=(1,), padding=[(CONV_PAD, CONV_PAD)],
        dimension_numbers=('NWC', 'WIO', 'NWC'), feature_group_count=CONV_DIM) + dw_b
    u = layernorm(u, ln_g, ln_b)
    u = jax.nn.silu(u)
    return u @ w_pw

def windowed_gqa(q, k, v, sink):
    b, s = q.shape[0], q.shape[1]
    nb = s // BLOCK
    grp = N_HEADS // N_KV_HEADS
    span = BLOCK + 2 * WINDOW
    kp = jnp.pad(k, ((0, 0), (WINDOW, WINDOW), (0, 0), (0, 0)))
    vp = jnp.pad(v, ((0, 0), (WINDOW, WINDOW), (0, 0), (0, 0)))
    qb = q.reshape(b, nb, BLOCK, N_KV_HEADS, grp, HEAD_DIM).transpose(1, 0, 2, 3, 4, 5)
    slopes = jnp.exp2(-8.0 * jnp.arange(1, N_HEADS + 1, dtype=jnp.float32) / N_HEADS)
    slopes = slopes.reshape(N_KV_HEADS, grp)
    r = jnp.arange(BLOCK)[:, None]
    c = jnp.arange(span)[None, :]
    dist = jnp.abs(r + WINDOW - c)
    bias = -slopes[:, :, None, None] * dist.astype(jnp.float32)[None, None]
    in_window = dist <= WINDOW
    sink_f = sink.astype(jnp.float32).reshape(N_KV_HEADS, grp)[None, :, :, None]
    scale = HEAD_DIM ** -0.5

    def block_fn(args):
        i, qi = args
        start = i * BLOCK
        ks = lax.dynamic_slice_in_dim(kp, start, span, axis=1)
        vs = lax.dynamic_slice_in_dim(vp, start, span, axis=1)
        key_pos = start - WINDOW + jnp.arange(span)
        valid = in_window & ((key_pos >= 0) & (key_pos < s))[None, :]
        logits = jnp.einsum('bqkgd,bskd->bkgqs', qi, ks).astype(jnp.float32) * scale + bias
        logits = jnp.where(valid, logits, NEG_INF)
        m = jnp.maximum(logits.max(-1), sink_f)
        p = jnp.exp(logits - m[..., None])
        denom = p.sum(-1) + jnp.exp(sink_f - m)
        o = jnp.einsum('bkgqs,bskd->bqkgd', p, vs.astype(jnp.float32))
        o = o / denom.transpose(0, 3, 1, 2)[..., None]
        return o.astype(q.dtype)

    out = lax.map(block_fn, (jnp.arange(nb), qb))
    return out.transpose(1, 0, 2, 3, 4, 5).reshape(b, s, ATTN_DIM)

def peer_ffn(h, w_query, sub_keys, expert_u, expert_v):
    b, s, d = h.shape
    hc_all = h.reshape((b * s) // TOKEN_CHUNK, TOKEN_CHUNK, d)

    def chunk_fn(hc):
        q = (hc @ w_query).reshape(TOKEN_CHUNK, PEER_HEADS, 2, PEER_HALF)
        sc = jnp.einsum('thpd,pnd->thpn', q, sub_keys).astype(jnp.float32)
        vals, idx = lax.top_k(sc, PEER_TOPK)
        cand = vals[:, :, 0, :, None] + vals[:, :, 1, None, :]
        cand_idx = idx[:, :, 0, :, None] * N_KEYS + idx[:, :, 1, None, :]
        cand = cand.reshape(TOKEN_CHUNK, PEER_HEADS, PEER_TOPK * PEER_TOPK)
        cand_idx = cand_idx.reshape(TOKEN_CHUNK, PEER_HEADS, PEER_TOPK * PEER_TOPK)
        top_s, pos = lax.top_k(cand, PEER_TOPK)
        expert_idx = jnp.take_along_axis(cand_idx, pos, axis=-1)
        gate = jax.nn.softmax(top_s, axis=-1)
        u = expert_u[expert_idx]
        act = jax.nn.gelu(jnp.einsum('thkd,td->thk', u, hc).astype(jnp.float32), approximate=False)
        vv = expert_v[expert_idx]
        return jnp.einsum('thk,thkd->td', (gate * act).astype(hc.dtype), vv)

    return lax.map(chunk_fn, hc_all).reshape(b, s, d)

def first_inputs(seed: int = 0) -> dict:
    key = jax.random.key(seed)
    ks = jax.random.split(key, 18)
    f32 = jnp.float32
    nrm = lambda k, shape, sc: jax.random.normal(k, shape, f32) * sc
    return {
        "x": nrm(ks[0], (BATCH, SEQ, D_MODEL), 1.0),
        "norm1_g": 1.0 + nrm(ks[1], (DEPTH, D_MODEL), 0.02),
        "w_in": nrm(ks[2], (DEPTH, D_MODEL, IN_DIM), D_MODEL ** -0.5),
        "conv_dw_w": nrm(ks[3], (DEPTH, CONV_KERNEL, CONV_DIM), CONV_KERNEL ** -0.5),
        "conv_dw_b": nrm(ks[4], (DEPTH, CONV_DIM), 0.02),
        "conv_ln_g": 1.0 + nrm(ks[5], (DEPTH, CONV_DIM), 0.02),
        "conv_ln_b": nrm(ks[6], (DEPTH, CONV_DIM), 0.02),
        "conv_w_pw": nrm(ks[7], (DEPTH, CONV_DIM, D_MODEL), CONV_DIM ** -0.5),
        "attn_sink": nrm(ks[8], (DEPTH, N_HEADS), 0.5),
        "attn_w_o": nrm(ks[9], (DEPTH, ATTN_DIM, D_MODEL), ATTN_DIM ** -0.5),
        "w_out": nrm(ks[10], (DEPTH, D_MODEL, D_MODEL), D_MODEL ** -0.5),
        "norm2_g": 1.0 + nrm(ks[11], (DEPTH, D_MODEL), 0.02),
        "peer_w_query": nrm(ks[12], (DEPTH, D_MODEL, PEER_HEADS * PEER_KEY_DIM), D_MODEL ** -0.5),
        "peer_sub_keys": nrm(ks[13], (DEPTH, 2, N_KEYS, PEER_HALF), PEER_HALF ** -0.5),
        "peer_u": nrm(ks[14], (DEPTH, N_EXPERTS, D_MODEL), D_MODEL ** -0.5),
        "peer_v": nrm(ks[15], (DEPTH, N_EXPERTS, D_MODEL), 0.25),
        "final_g": 1.0 + nrm(ks[16], (D_MODEL,), 0.02),
    }

def first_block(x, norm1_g, w_in, conv_dw_w, conv_dw_b, conv_ln_g, conv_ln_b, conv_w_pw,
              attn_sink, attn_w_o, w_out, norm2_g, peer_w_query, peer_sub_keys,
              peer_u, peer_v, final_g):
    b, s, d = x.shape
    o_conv = 2 * CONV_DIM
    o_q = o_conv + ATTN_DIM
    o_k = o_q + KV_DIM
    o_v = o_k + KV_DIM
    for l in range(DEPTH):
        h = rmsnorm(x, norm1_g[l])
        z = h @ w_in[l]
        conv_in = z[..., :o_conv]
        q = z[..., o_conv:o_q].reshape(b, s, N_HEADS, HEAD_DIM)
        k = z[..., o_q:o_k].reshape(b, s, N_KV_HEADS, HEAD_DIM)
        v = z[..., o_k:o_v].reshape(b, s, N_KV_HEADS, HEAD_DIM)
        gates = jax.nn.sigmoid(z[..., o_v:].astype(jnp.float32)).astype(x.dtype)
        gates = gates.reshape(b, s, N_BRANCH, d)
        conv_out = conformer_conv(conv_in, conv_dw_w[l], conv_dw_b[l], conv_ln_g[l],
                                  conv_ln_b[l], conv_w_pw[l])
        attn_out = windowed_gqa(q, k, v, attn_sink[l]) @ attn_w_o[l]
        merged = gates[:, :, 0, :] * conv_out + gates[:, :, 1, :] * attn_out
        x = x + merged @ w_out[l]
        h2 = rmsnorm(x, norm2_g[l])
        x = x + peer_ffn(h2, peer_w_query[l], peer_sub_keys[l], peer_u[l], peer_v[l])
    return rmsnorm(x, final_g)


MEM_LEN = 256
RMS_EPS = 1e-6
RW_HEADS = 8
RW_HEAD_DIM = 64
RW_WIDTH = RW_HEADS * RW_HEAD_DIM
DECAY_LORA = 64
AAA_LORA = 64
LNX_EPS = 64e-5
L2_EPS = 1e-12
SW_HEADS = 8
SW_KV_HEADS = 2
SW_GROUP = SW_HEADS // SW_KV_HEADS
SW_HEAD_DIM = 64
SW_WIDTH = SW_HEADS * SW_HEAD_DIM
SW_KV_WIDTH = SW_KV_HEADS * SW_HEAD_DIM
ROPE_THETA = 10000.0
NEG_INF_2 = -1e30
X_HEADS = 4
X_HEAD_DIM = 128
X_WIDTH = X_HEADS * X_HEAD_DIM
N_BRANCHES = 3

IN_SPLITS = (RW_WIDTH, RW_WIDTH, RW_WIDTH, DECAY_LORA, AAA_LORA, RW_WIDTH,
             SW_WIDTH, SW_KV_WIDTH, SW_KV_WIDTH, SW_WIDTH,
             X_WIDTH, X_WIDTH,
             N_BRANCHES * D_MODEL)
IN_WIDTH = sum(IN_SPLITS)


def rms_norm(x, g):
    xf = x.astype(jnp.float32)
    y = xf * lax.rsqrt(jnp.mean(xf * xf, axis=-1, keepdims=True) + RMS_EPS)
    return (y * g.astype(jnp.float32)).astype(x.dtype)

def token_shift_mix(u, mu):
    prev = jnp.pad(u, ((0, 0), (1, 0), (0, 0)))[:, :-1]
    return u + (prev - u) * mu

def rope(x, pos):
    d = x.shape[-1]
    half = d // 2
    inv = ROPE_THETA ** (-jnp.arange(half, dtype=jnp.float32) / half)
    ang = pos.astype(jnp.float32)[..., None] * inv
    cos = jnp.cos(ang)[:, :, None, :]
    sin = jnp.sin(ang)[:, :, None, :]
    xf = x.astype(jnp.float32)
    x1, x2 = xf[..., :half], xf[..., half:]
    return jnp.concatenate([x1 * cos - x2 * sin, x2 * cos + x1 * sin], axis=-1).astype(x.dtype)

def rwkv7_scan(r, w, k, v, a, b):
    def step(S, inp):
        r_t, w_t, k_t, v_t, a_t, b_t = inp
        sa = jnp.einsum('bhvk,bhk->bhv', S, a_t)
        S = S * w_t[:, :, None, :] + sa[..., None] * b_t[:, :, None, :] + v_t[..., None] * k_t[:, :, None, :]
        y = jnp.einsum('bhvk,bhk->bhv', S, r_t)
        return S, y
    bsz, _, h, n = r.shape
    xs = tuple(jnp.moveaxis(t, 1, 0) for t in (r, w, k, v, a, b))
    s0 = jnp.zeros((bsz, h, n, n), jnp.float32)
    _, y = lax.scan(step, s0, xs)
    return jnp.moveaxis(y, 0, 1)

def rwkv7_mix(p_r, p_k, p_v, p_w, p_a, mu_rkv, mu_wa, w0, w2, a0, a2, k_k, k_a, r_k, lnx_g, lnx_b):
    f32 = jnp.float32
    bsz, t, _ = p_r.shape
    r = token_shift_mix(p_r, mu_rkv[0]).astype(f32)
    k = token_shift_mix(p_k, mu_rkv[1]).astype(f32)
    v = token_shift_mix(p_v, mu_rkv[2]).astype(f32)
    lw = token_shift_mix(p_w, mu_wa[0]).astype(f32)
    la = token_shift_mix(p_a, mu_wa[1]).astype(f32)
    w_log = -jax.nn.softplus(-(w0.astype(f32) + jnp.tanh(lw) @ w2.astype(f32))) - 0.5
    decay = jnp.exp(-jnp.exp(w_log))
    a = jax.nn.sigmoid(a0.astype(f32) + la @ a2.astype(f32))
    heads = lambda u: u.reshape(bsz, t, RW_HEADS, RW_HEAD_DIM)
    kk = heads(k * k_k.astype(f32))
    kk = kk / jnp.maximum(jnp.linalg.norm(kk, axis=-1, keepdims=True), L2_EPS)
    k = k * (1.0 + (a - 1.0) * k_a.astype(f32))
    rh, kh, vh, ah = heads(r), heads(k), heads(v), heads(a)
    y = rwkv7_scan(rh, heads(decay), kh, vh, -kk, kk * ah)
    mean = jnp.mean(y, axis=-1, keepdims=True)
    var = jnp.mean(jnp.square(y - mean), axis=-1, keepdims=True)
    y = ((y - mean) * lax.rsqrt(var + LNX_EPS)).reshape(bsz, t, RW_WIDTH) * lnx_g.astype(f32) + lnx_b.astype(f32)
    bonus = jnp.sum(rh * kh * r_k.astype(f32), axis=-1, keepdims=True) * vh
    return y + bonus.reshape(bsz, t, RW_WIDTH)

def sliding_window_sink_attn(q, k, v, pos, q_g, k_g, sinks):
    bsz, t, _ = q.shape
    nb = t // BLOCK
    q = rope(rms_norm(q.reshape(bsz, t, SW_HEADS, SW_HEAD_DIM), q_g), pos)
    k = rope(rms_norm(k.reshape(bsz, t, SW_KV_HEADS, SW_HEAD_DIM), k_g), pos)
    v = v.reshape(bsz, t, SW_KV_HEADS, SW_HEAD_DIM)
    qb = q.reshape(bsz, nb, BLOCK, SW_KV_HEADS, SW_GROUP, SW_HEAD_DIM)
    def band(u):
        ub = u.reshape(bsz, nb, BLOCK, SW_KV_HEADS, SW_HEAD_DIM)
        prev = jnp.pad(ub, ((0, 0), (1, 0), (0, 0), (0, 0), (0, 0)))[:, :-1]
        return jnp.concatenate([prev, ub], axis=2)
    kband, vband = band(k), band(v)
    scale = SW_HEAD_DIM ** -0.5
    s = jnp.einsum('bnqhgd,bnkhd->bnhgqk', qb, kband).astype(jnp.float32) * scale
    qi = jnp.arange(BLOCK)[:, None]
    kj = jnp.arange(2 * BLOCK)[None, :]
    rel = qi - kj + BLOCK
    allowed = (rel >= 0) & (rel < WINDOW)
    not_pad = (jnp.arange(nb)[:, None, None] > 0) | (kj >= BLOCK)[None]
    mask = allowed[None] & not_pad
    s = jnp.where(mask[None, :, None, None], s, NEG_INF_2)
    sink = jnp.broadcast_to(sinks.astype(jnp.float32).reshape(SW_KV_HEADS, SW_GROUP)[None, None, :, :, None, None],
                            s.shape[:-1] + (1,))
    p = jax.nn.softmax(jnp.concatenate([s, sink], axis=-1), axis=-1)[..., :-1]
    o = jnp.einsum('bnhgqk,bnkhd->bnqhgd', p.astype(v.dtype), vband)
    return o.reshape(bsz, t, SW_WIDTH)

def memory_cross_attn(q, mem, mem_norm_g, w_mem_kv, xq_g, xk_g):
    bsz, t, _ = q.shape
    m = mem.shape[1]
    q = rms_norm(q.reshape(bsz, t, X_HEADS, X_HEAD_DIM), xq_g)
    kv = rms_norm(mem, mem_norm_g) @ w_mem_kv
    km, vm = kv[..., :X_WIDTH], kv[..., X_WIDTH:]
    km = rms_norm(km.reshape(bsz, m, X_HEADS, X_HEAD_DIM), xk_g)
    vm = vm.reshape(bsz, m, X_HEADS, X_HEAD_DIM)
    s = jnp.einsum('bthd,bmhd->bhtm', q, km).astype(jnp.float32) * (X_HEAD_DIM ** -0.5)
    p = jax.nn.softmax(s, axis=-1)
    o = jnp.einsum('bhtm,bmhd->bthd', p.astype(vm.dtype), vm)
    return o.reshape(bsz, t, X_WIDTH)

def second_inputs(seed: int = 0) -> dict:
    key = jax.random.key(seed)
    ks = iter(jax.random.split(key, 40))
    f32 = jnp.float32
    def nrm(shape, scale):
        return jax.random.normal(next(ks), shape, f32) * scale
    L = DEPTH
    x = jax.random.normal(next(ks), (BATCH, SEQ, D_MODEL), f32)
    mem = jax.random.normal(next(ks), (BATCH, MEM_LEN, D_MODEL), f32)
    offset = jax.random.randint(next(ks), (BATCH, 1), 0, 4096, dtype=jnp.int32)
    positions = jnp.arange(SEQ, dtype=jnp.int32)[None, :] + offset
    return {
        'x': x,
        'mem': mem,
        'positions': positions,
        'norm_g': 1.0 + nrm((L, D_MODEL), 0.05),
        'mem_norm_g': 1.0 + nrm((L, D_MODEL), 0.05),
        'w_in': nrm((L, D_MODEL, IN_WIDTH), D_MODEL ** -0.5),
        'mu_rkv': jax.random.uniform(next(ks), (L, 3, RW_WIDTH), f32),
        'mu_wa': jax.random.uniform(next(ks), (L, 2, DECAY_LORA), f32),
        'w0': jnp.linspace(-6.0, -1.0, RW_WIDTH, dtype=f32)[None, :] + nrm((L, RW_WIDTH), 0.1),
        'w2': nrm((L, DECAY_LORA, RW_WIDTH), 0.5 * DECAY_LORA ** -0.5),
        'a0': nrm((L, RW_WIDTH), 0.1),
        'a2': nrm((L, AAA_LORA, RW_WIDTH), 0.5 * AAA_LORA ** -0.5),
        'k_k': 0.85 + nrm((L, RW_WIDTH), 0.05),
        'k_a': 1.0 + nrm((L, RW_WIDTH), 0.05),
        'r_k': nrm((L, RW_HEADS, RW_HEAD_DIM), 0.1),
        'lnx_g': 1.0 + nrm((L, RW_WIDTH), 0.05),
        'lnx_b': nrm((L, RW_WIDTH), 0.01),
        'q_norm_g': 1.0 + nrm((L, SW_HEAD_DIM), 0.05),
        'k_norm_g': 1.0 + nrm((L, SW_HEAD_DIM), 0.05),
        'sinks': nrm((L, SW_HEADS), 1.0),
        'xq_norm_g': 1.0 + nrm((L, X_HEAD_DIM), 0.05),
        'xk_norm_g': 1.0 + nrm((L, X_HEAD_DIM), 0.05),
        'w_mem_kv': nrm((L, D_MODEL, 2 * X_WIDTH), D_MODEL ** -0.5),
        'w_proj_a': nrm((L, RW_WIDTH, D_MODEL), RW_WIDTH ** -0.5),
        'w_proj_b': nrm((L, SW_WIDTH, D_MODEL), SW_WIDTH ** -0.5),
        'w_proj_c': nrm((L, X_WIDTH, D_MODEL), X_WIDTH ** -0.5),
        'w_out': nrm((L, D_MODEL, D_MODEL), D_MODEL ** -0.5),
    }

def second_block(x, mem, positions, norm_g, mem_norm_g, w_in, mu_rkv, mu_wa, w0, w2, a0, a2, k_k, k_a, r_k,
              lnx_g, lnx_b, q_norm_g, k_norm_g, sinks, xq_norm_g, xk_norm_g, w_mem_kv,
              w_proj_a, w_proj_b, w_proj_c, w_out):
    bsz, t, _ = x.shape
    split_points = [int(i) for i in np.cumsum(IN_SPLITS)[:-1]]
    for l in range(DEPTH):
        h = rms_norm(x, norm_g[l])
        p = h @ w_in[l]
        (p_r, p_k, p_v, p_w, p_a, z_a,
         p_q, p_sk, p_sv, z_b,
         p_xq, z_c, p_gate) = jnp.split(p, split_points, axis=-1)
        y_a = rwkv7_mix(p_r, p_k, p_v, p_w, p_a, mu_rkv[l], mu_wa[l], w0[l], w2[l], a0[l], a2[l],
                        k_k[l], k_a[l], r_k[l], lnx_g[l], lnx_b[l]).astype(x.dtype) * jax.nn.silu(z_a)
        y_b = sliding_window_sink_attn(p_q, p_sk, p_sv, positions, q_norm_g[l], k_norm_g[l],
                                       sinks[l]) * jax.nn.silu(z_b)
        y_c = memory_cross_attn(p_xq, mem, mem_norm_g[l], w_mem_kv[l], xq_norm_g[l],
                                xk_norm_g[l]) * jax.nn.silu(z_c)
        gates = jax.nn.sigmoid(p_gate.astype(jnp.float32)).reshape(bsz, t, N_BRANCHES, D_MODEL)
        merged = (gates[:, :, 0] * (y_a @ w_proj_a[l]) + gates[:, :, 1] * (y_b @ w_proj_b[l])
                  + gates[:, :, 2] * (y_c @ w_proj_c[l]))
        x = x + (merged.astype(x.dtype) @ w_out[l]).astype(x.dtype)
    return x


def setup_inputs(seed=0):
    out = dict(first_inputs(seed))
    for name, value in second_inputs(seed + 1).items():
        if name != "x":
            out[name + "_2"] = value
    return out


def reference(
    x, norm1_g, w_in, conv_dw_w, conv_dw_b, conv_ln_g, conv_ln_b, conv_w_pw, attn_sink,
    attn_w_o, w_out, norm2_g, peer_w_query, peer_sub_keys, peer_u, peer_v, final_g, mem_2,
    positions_2, norm_g_2, mem_norm_g_2, w_in_2, mu_rkv_2, mu_wa_2, w0_2, w2_2, a0_2, a2_2,
    k_k_2, k_a_2, r_k_2, lnx_g_2, lnx_b_2, q_norm_g_2, k_norm_g_2, sinks_2, xq_norm_g_2,
    xk_norm_g_2, w_mem_kv_2, w_proj_a_2, w_proj_b_2, w_proj_c_2, w_out_2,
):
    x = first_block(
        x, norm1_g, w_in, conv_dw_w, conv_dw_b, conv_ln_g, conv_ln_b, conv_w_pw, attn_sink,
        attn_w_o, w_out, norm2_g, peer_w_query, peer_sub_keys, peer_u, peer_v, final_g,
    )
    return second_block(
        x, mem_2, positions_2, norm_g_2, mem_norm_g_2, w_in_2, mu_rkv_2, mu_wa_2, w0_2, w2_2,
        a0_2, a2_2, k_k_2, k_a_2, r_k_2, lnx_g_2, lnx_b_2, q_norm_g_2, k_norm_g_2, sinks_2,
        xq_norm_g_2, xk_norm_g_2, w_mem_kv_2, w_proj_a_2, w_proj_b_2, w_proj_c_2, w_out_2,
    )


_drawn_inputs = setup_inputs


def setup_inputs(seed=0):
    import zlib

    import numpy as np

    out = dict(_drawn_inputs(seed))
    spreads = {}
    factors = {'norm1_g': 3.339,
     'conv_ln_g': 3.606,
     'conv_ln_b': 3.997,
     'attn_sink': 40.536,
     'norm2_g': 2.754,
     'mem_norm_g_2': 8.0,
     'w2_2': 4.456,
     'a0_2': 3.966,
     'k_k_2': 15.091,
     'k_a_2': 3.148,
     'lnx_g_2': 10.707,
     'lnx_b_2': 49.207,
     'q_norm_g_2': 23.892,
     'k_norm_g_2': 23.555,
     'sinks_2': 200.0,
     'xq_norm_g_2': 8.0,
     'xk_norm_g_2': 8.0}
    for name, (base, spread) in spreads.items():
        noise = np.random.default_rng([zlib.crc32(name.encode()), seed]).standard_normal(out[name].shape)
        drawn = base * np.exp(spread * noise) if base else spread * noise
        out[name] = __import__('jax').numpy.asarray(drawn.astype(out[name].dtype))
    for name, factor in factors.items():
        out[name] = (out[name] * factor).astype(out[name].dtype)
    return out
```

```python
from contextlib import ExitStack, contextmanager

import numpy as np

import concourse.bass as bass
from concourse import mybir

F32 = mybir.dt.float32
U32 = mybir.dt.uint32
I32 = mybir.dt.int32
ALU = mybir.AluOpType
ACT = mybir.ActivationFunctionType
AXX = mybir.AxisListType.X

P = 128
T = 512
TT = T // P
D = 1024
DT = D // P
TAPS = 31
PAD = TAPS // 2
EPS = 1e-6
RING = 4

H1, KV1, HD = 16, 4, 64
SLOPES = [2.0 ** (-8.0 * (h + 1) / H1) for h in range(H1)]
FAR = 1e33
PH, TOPK, NKEYS = 8, 16, 128
PICKS = PH * TOPK

MEM = 256
LNX_EPS = 64e-5
DECAY = float(np.exp(-0.5))
CH = 64
LEVELS = 6

HEADS1 = [[4 * (2 * (i // 4) + e) + i % 4 for e in range(2)] for i in range(8)]
HEADS2 = [[i, 4 + i] for i in range(4)]

COLS1 = dict(norm1=8, conv_w=TAPS * 8, conv_b=8, ln_g=8, ln_b=8, sink=16)
COLS2 = dict(norm=8, memnorm=8, mu=13, a0=4, k_k=4, k_a=4, r_k=4, lnx_g=4, lnx_b=4, q_g=1, k_g=1,
             xq_g=1, xk_g=1, inv=1, sinks=8)
CONST1 = dict(ident=P, ones=P, dist=3 * P, iota=TOPK * TOPK)
CONST2 = dict(ident=P, ones=P, halves=P, swap=P, band=2 * P, strict=P, incl=P, level=LEVELS * P, eye2=CH)

UNITS = [("z1", 44), ("co", 16), ("wout1", 8), ("query", 16), ("rwkv", 17), ("sw", 10), ("mem", 8),
         ("xq", 8), ("merge", 36), ("wout2", 8)]


def first_unit(name):
    at = 0
    for n, count in UNITS:
        if n == name:
            return at
        at += count
    return at


def offsets(widths):
    at, out = 0, {}
    for name, w in widths.items():
        out[name] = (at, at + w)
        at += w
    return out, at


class Columns:

    def __init__(self, tensor, widths):
        self.tensor, (self.at, self.width) = tensor, offsets(widths)

    def __call__(self, name, i=0, n=1):
        a = self.at[name][0] + i
        return self.tensor[:, a:a + n]

    def whole(self, name):
        a, b = self.at[name]
        return self.tensor[:, a:b]


class Chain:

    def __init__(self, eng, sem):
        self.eng, self.sem, self.count = eng, sem, 0

    def __call__(self, ins):
        self.count += 1
        ins.then_inc(self.sem, 1)
        self.eng.wait_ge(self.sem, self.count)


class Weights:

    def __init__(self, nc, ctx, dram):
        self.dram = dram
        self.ring = ctx.enter_context(nc.sbuf_tensor("weight_ring", [P, RING, DT, P], F32))
        self.arrived = [ctx.enter_context(nc.semaphore(f"weights_arrived{s}")) for s in range(RING)]
        self.done = ctx.enter_context(nc.semaphore("unit_done"))
        self.issued = 0

    def load(self, sp, upto):
        def one(u, i, j):
            slot = (u + j) % RING
            if u + j >= RING:
                sp.wait_ge(self.done, RING * i + (u + j - RING + 1))
            sp.dma_start(self.ring[:, slot], self.dram[u + j + RING * i]).then_inc(self.arrived[slot], 16)

        u, n = self.issued, upto - self.issued
        while u < RING and n > 0:
            one(u, 0, 0)
            u, n = u + 1, n - 1
        if n >= 2 * RING:
            with sp.Fori(0, n // RING) as i:
                for j in range(RING):
                    one(u, i, j)
            u, n = u + n // RING * RING, n % RING
        for j in range(n):
            one(u, 0, j)
        self.issued = upto

    def wait(self, pe, u, i=0):
        pe.wait_ge(self.arrived[u % RING], 16 * i + 16 * (u // RING + 1))
        return self.ring[:, u % RING]


def rounds(eng, n, body):
    body(0, True)
    if n > 1:
        with eng.Fori(1, n) as i:
            body(i, False)


class Stage:

    owner, free = None, []

    def __init__(self, nc, name):
        self.nc, self.name, self.ctx, self.sems = nc, name, ExitStack(), []
        if Stage.owner is not nc:
            Stage.owner, Stage.free = nc, list(nc.free_semaphores)

    def __enter__(self):
        self.ctx.__enter__()
        return self

    def __exit__(self, *e):
        if self.sems:
            numbers = [s.num for s in self.sems]
            self.nc.clear_and_free_semaphores(self.sems)
            Stage.free += numbers
        return self.ctx.__exit__(*e)

    def sb(self, name, shape, dt=F32):
        return self.ctx.enter_context(self.nc.sbuf_tensor(f"{self.name}_{name}", shape, dt))

    def sem(self, name):
        self.sems.append(self.nc.alloc_semaphore(name=f"{self.name}_{name}", num=Stage.free.pop(0)))
        return self.sems[-1]

    def block(self):
        return self.nc.Block()


def norm_to_T(nc, w, bank, name, x, tiles, gain, ident, xT, prefetch, scaled=None, row_gain=None):
    with Stage(nc, name) as st:
        junk = st.sb("junk", [P, D])
        ss = st.sb("ss", [P, tiles])
        ms = st.sb("ms", [P, tiles])
        rms = st.sb("rms", [P, tiles])
        rstd = st.sb("rstd", [P, tiles])
        xn = scaled if scaled is not None else st.sb("xn", [P, tiles, D])
        squared, mean_ready, root_ready = st.sem("squared"), st.sem("mean_ready"), st.sem("root_ready")
        rstd_ready, normed, turned, kept = st.sem("rstd_ready"), st.sem("normed"), st.sem("turned"), st.sem("kept")
        with st.block() as block:
            @block.sync
            def _(sp):
                w.load(sp, prefetch)

            @block.scalar
            def _(act):
                for t in range(tiles):
                    if t:
                        act.wait_ge(squared, t)
                    nc.scalar.activation(junk[:], x[:, t], ACT.Square, accum_out=ss[:, t:t + 1]).then_inc(squared, 1)
                act.wait_ge(mean_ready, 1)
                nc.scalar.activation(rms[:], ms[:], ACT.Sqrt).then_inc(root_ready, 1)
                for f in range(DT):
                    act.wait_ge(turned, f + 1)
                    scale = 1.0 if gain is None else gain[:, f:f + 1]
                    nc.scalar.activation(xT[:, f], bank[f][:, 0:tiles * P], ACT.Copy, scale=scale).then_inc(kept, 1)

            @block.vector
            def _(dve):
                dve.wait_ge(squared, tiles)
                nc.vector.tensor_scalar(ms[:], ss[:], 1.0 / D, EPS, ALU.mult, ALU.add).then_inc(mean_ready, 1)
                dve.wait_ge(root_ready, 1)
                nc.vector.reciprocal(rstd[:], rms[:]).then_inc(rstd_ready, 1)
                dve.wait_ge(rstd_ready, 1)
                for t in range(tiles):
                    if row_gain is None:
                        nc.vector.tensor_scalar(xn[:, t], x[:, t], rstd[:, t:t + 1], None, ALU.mult).then_inc(normed, 1)
                    else:
                        nc.vector.scalar_tensor_tensor(xn[:, t], x[:, t], rstd[:, t:t + 1], row_gain, ALU.mult,
                                                       ALU.mult).then_inc(normed, 1)

            @block.tensor
            def _(pe):
                if xT is None:
                    return
                pe.wait_ge(normed, tiles)
                for f in range(DT):
                    for t in range(tiles):
                        mm = nc.tensor.transpose(bank[f][:, t * P:(t + 1) * P], xn[:, t, f * P:(f + 1) * P], ident)
                    mm.then_inc(turned, 1)


def attention(nc, w, bank, name, units, prefetch, *, scale, sink, ident, out, group, dim):
    n = len(units)
    width = max(u["k"].shape[-1] for u in units)
    per = P // dim
    with Stage(nc, name) as st:
        logit = st.sb("logit", [P, 2, width])
        prob = st.sb("prob", [P, 2, width])
        probT = st.sb("probT", [P, 2, width])
        diag = st.sb("diag", [P, 2, P])
        top = st.sb("top", [P, 2])
        negtop = st.sb("negtop", [P, 2])
        total = st.sb("total", [P, 2])
        sinkexp = st.sb("sinkexp", [P, 2])
        full = st.sb("full", [P, 2])
        recip = st.sb("recip", [P, 2])
        scores_ready, biased, top_ready = st.sem("scores_ready"), st.sem("biased"), st.sem("top_ready")
        negtop_ready, exp_ready, full_ready = st.sem("negtop_ready"), st.sem("exp_ready"), st.sem("full_ready")
        recip_ready, diag_ready, turned = st.sem("recip_ready"), st.sem("diag_ready"), st.sem("turned")
        turned_kept, out_ready, out_kept = st.sem("turned_kept"), st.sem("out_ready"), st.sem("out_kept")
        has_bias, has_sink = units[0]["bias"] is not None, sink is not None
        with st.block() as block:
            @block.sync
            def _(sp):
                w.load(sp, prefetch)

            @block.tensor
            def _(pe):
                def scores(i):
                    if i >= 2:
                        pe.wait_ge(biased if has_bias else exp_ready, i - 1)
                        if not has_bias:
                            pe.wait_ge(top_ready, i - 1)
                    u = units[i]
                    nc.tensor.matmul(bank[i % 2][:, 0:u["k"].shape[-1]], u["q"], u["k"], start=True,
                                     stop=True).then_inc(scores_ready, 1)

                def turn(i):
                    pe.wait_ge(exp_ready, i + 1)
                    pe.wait_ge(diag_ready, i + 1)
                    if i >= 2:
                        pe.wait_ge(turned_kept, i - 1)
                    for c in range(len(units[i]["v"])):
                        mm = nc.tensor.matmul(bank[2 + i % 2][:, c * P:(c + 1) * P], prob[:, i % 2, c * P:(c + 1) * P],
                                              diag[:, i % 2], start=True, stop=True)
                    mm.then_inc(turned, 1)

                def values(i):
                    u, g = units[i], i // group
                    pe.wait_ge(turned_kept, i + 1)
                    if g >= 2:
                        pe.wait_ge(out_kept, g - 1)
                    at = u["half"] * dim
                    col = (i % group) // per * P
                    for c, v in enumerate(u["v"]):
                        mm = nc.tensor.matmul(bank[4 + g % 2][at:at + dim, col:col + P], v,
                                              probT[:, i % 2, c * P:(c + 1) * P], start=(c == 0),
                                              stop=(c == len(u["v"]) - 1))
                    mm.then_inc(out_ready, 1)

                for i in range(n + 2):
                    if i < n:
                        scores(i)
                    if 1 <= i <= n:
                        turn(i - 1)
                    if i >= 2:
                        values(i - 2)

            @block.vector
            def _(dve):
                def maximum(i):
                    u, b = units[i], i % 2
                    k = u["k"].shape[-1]
                    dve.wait_ge(scores_ready, i + 1)
                    if i >= 2:
                        dve.wait_ge(exp_ready, i - 1)
                    src = bank[b][:, 0:k]
                    if has_bias:
                        tile, coef = u["bias"]
                        nc.vector.scalar_tensor_tensor(logit[:, b, 0:k], tile, coef, src, ALU.mult,
                                                       ALU.add).then_inc(biased, 1)
                        dve.wait_ge(biased, i + 1)
                        src = logit[:, b, 0:k]
                    nc.vector.tensor_reduce(top[:, b:b + 1], src, AXX, ALU.max).then_inc(top_ready, 1)
                    dve.wait_ge(top_ready, i + 1)
                    if has_sink:
                        nc.vector.tensor_scalar(negtop[:, b:b + 1], top[:, b:b + 1], u["sink_scaled"], -scale, ALU.max,
                                                ALU.mult).then_inc(negtop_ready, 1)
                    else:
                        nc.vector.tensor_scalar(negtop[:, b:b + 1], top[:, b:b + 1], -scale, None,
                                                ALU.mult).then_inc(negtop_ready, 1)

                def divisor(i):
                    b = i % 2
                    dve.wait_ge(exp_ready, i + 1)
                    src = total[:, b:b + 1]
                    if has_sink:
                        nc.vector.tensor_tensor(full[:, b:b + 1], src, sinkexp[:, b:b + 1], ALU.add).then_inc(full_ready, 1)
                        dve.wait_ge(full_ready, i + 1)
                        src = full[:, b:b + 1]
                    nc.vector.reciprocal(recip[:, b:b + 1], src).then_inc(recip_ready, 1)
                    dve.wait_ge(recip_ready, i + 1)
                    if i >= 2:
                        dve.wait_ge(turned, i - 1)
                    nc.vector.tensor_scalar(diag[:, b], ident, recip[:, b:b + 1], None, ALU.mult).then_inc(diag_ready, 1)

                def keep(g):
                    dve.wait_ge(out_ready, group * (g + 1))
                    nc.vector.tensor_copy(out(g), bank[4 + g % 2][:].rearrange("p (a t) -> p a t", t=P)[:, 0:group // per]
                                          ).then_inc(out_kept, 1)

                for i in range(n + 4):
                    if i < n:
                        maximum(i)
                    if 1 <= i <= n:
                        divisor(i - 1)
                    if i >= 3 and (i - 3) % group == group - 1:
                        keep((i - 3) // group)

            @block.scalar
            def _(act):
                def exps(i):
                    u, b = units[i], i % 2
                    k = u["k"].shape[-1]
                    act.wait_ge(negtop_ready, i + 1)
                    if i >= 2:
                        act.wait_ge(turned, i - 1)
                        act.wait_ge(recip_ready, i - 1)
                    if has_sink:
                        nc.scalar.activation(sinkexp[:, b:b + 1], u["sink"], ACT.Exp, bias=negtop[:, b:b + 1])
                    nc.scalar.activation(prob[:, b, 0:k], logit[:, b, 0:k] if has_bias else bank[b][:, 0:k], ACT.Exp,
                                         bias=negtop[:, b:b + 1], scale=scale,
                                         accum_out=total[:, b:b + 1]).then_inc(exp_ready, 1)

                def keep(i):
                    k = units[i]["k"].shape[-1]
                    act.wait_ge(turned, i + 1)
                    if i >= 2:
                        act.wait_ge(out_ready, i - 1)
                    nc.scalar.activation(probT[:, i % 2, 0:k], bank[2 + i % 2][:, 0:k], ACT.Copy).then_inc(turned_kept, 1)

                for i in range(n + 1):
                    if i < n:
                        exps(i)
                    if i >= 1:
                        keep(i - 1)


def turn_tiles(nc, w, bank, name, pairs, ident, prefetch):
    with Stage(nc, name) as st:
        turned, kept = st.sem("turned"), st.sem("kept")
        with st.block() as block:
            @block.sync
            def _(sp):
                w.load(sp, prefetch)

            @block.tensor
            def _(pe):
                for n, (sources, _) in enumerate(pairs):
                    if n >= 8:
                        pe.wait_ge(kept, n - 7)
                    for j, s in enumerate(sources):
                        mm = nc.tensor.transpose(bank[n % 8][:, j * P:(j + 1) * P], s, ident)
                    mm.then_inc(turned, 1)

            @block.scalar
            def _(act):
                for n, (sources, to) in enumerate(pairs):
                    act.wait_ge(turned, n + 1)
                    if n:
                        act.wait_ge(kept, n)
                    src = bank[n % 8][:, 0:len(sources) * P]
                    if len(to.shape) == 3:
                        src = src.rearrange("p (a t) -> p a t", a=to.shape[1])
                    nc.scalar.activation(to, src, ACT.Copy).then_inc(kept, 1)


def first_block(nc, w, bank, cols, const, rows, subkeys, peer_u, peer_v, x, dump):
    ident, ones = const.whole("ident"), const.whole("ones")
    with ExitStack() as outer:
        attnT = outer.enter_context(nc.sbuf_tensor("attnT", [P, DT, T], F32))
        convT = outer.enter_context(nc.sbuf_tensor("convT", [P, DT, T], F32))
        gateT = outer.enter_context(nc.sbuf_tensor("gateT", [P, 16, T], F32))
        with ExitStack() as inner:
            qkvT = inner.enter_context(nc.sbuf_tensor("qkvT", [P, 12, T], F32))
            with nc.sbuf_tensor("hT", [P, DT, T], F32) as hT:
                norm_to_T(nc, w, bank, "norm1", x, TT, cols.whole("norm1"), ident, hT, first_unit("z1") + RING)
                project_first(nc, w, bank, cols, hT, qkvT, gateT, convT)
            dump("conv", convT)
            dump("qkv", qkvT)
            dump("gate", gateT)
            conv_norm(nc, w, bank, cols, ones, convT)
            dump("convn", convT)
            v_tok = inner.enter_context(nc.sbuf_tensor("v_tok", [P, TT, KV1 * HD], F32))
            sink8 = inner.enter_context(nc.sbuf_tensor("sink8", [P, H1], F32))
            with Stage(nc, "sink") as st, st.block() as block:
                @block.vector
                def _(dve):
                    nc.vector.tensor_scalar(sink8[:], cols.whole("sink"), float(HD ** 0.5), None, ALU.mult)
            turn_tiles(nc, w, bank, "turn_v",
                       [([qkvT[:, 10 + a, t * P:(t + 1) * P] for a in range(2)], v_tok[:, t]) for t in range(TT)],
                       ident, first_unit("co") + RING)
            units = []
            for b in range(TT):
                lo, hi = max(b - 1, 0), min(b + 2, TT)
                for i in range(8):
                    for e in range(2):
                        h = HEADS1[i][e]
                        a, part = i // 4, slice(e * HD, (e + 1) * HD)
                        kv = 2 * a + e
                        units.append(dict(
                            q=qkvT[part, i, b * P:(b + 1) * P], k=qkvT[part, 8 + a, lo * P:hi * P],
                            bias=(const.whole("dist")[:, (lo - b + 1) * P:(hi - b + 1) * P], -SLOPES[h] * HD ** 0.5),
                            v=[v_tok[:, c, kv * HD:(kv + 1) * HD] for c in range(lo, hi)],
                            sink=cols("sink", h), sink_scaled=sink8[:, h:h + 1], half=e))
            attention(nc, w, bank, "attn1", units, first_unit("co") + RING, scale=HD ** -0.5, sink=True, ident=ident,
                      out=lambda g: attnT[:, 4 * (g % 2):4 * (g % 2) + 4, (g // 2) * P:(g // 2 + 1) * P],
                      group=8, dim=HD)
        dump("attn", attnT)
        with nc.sbuf_tensor("mergedT", [P, DT, T], F32) as mergedT:
            merge_first(nc, w, bank, convT, attnT, gateT, mergedT)
            out_residual(nc, w, bank, "wout1", mergedT, x, first_unit("query") + RING)
    dump("x1", x)
    with ExitStack() as inner:
        h2 = inner.enter_context(nc.sbuf_tensor("h2", [P, TT, D], F32))
        scores = inner.enter_context(nc.sbuf_tensor("scores", [P, TT, 2 * PH, NKEYS], F32))
        with nc.sbuf_tensor("h2T", [P, DT, T], F32) as h2T:
            norm_to_T(nc, w, bank, "norm2", x, TT, None, ident, h2T, first_unit("query") + RING, scaled=h2,
                      row_gain=rows[:, 0:D])
            query_scores(nc, w, bank, h2T, subkeys, scores)
        dump("scores", scores)
        experts(nc, w, bank, const, ident, scores, h2, peer_u, peer_v, x)
    dump("x2", x)
    final_norm(nc, w, x, rows[:, D:2 * D])
    dump("y", x)


def project_first(nc, w, bank, cols, hT, qkvT, gateT, convT):
    with Stage(nc, "z1") as st:
        sig = st.sb("sig", [P, 2, T])
        u = st.sb("u", [P, DT, T + 2 * PAD])
        sig_ready, z_kept = st.sem("sig_ready"), st.sem("z_kept")
        u0 = first_unit("z1")
        u_zero, gated, tap_done = st.sem("u_zero"), st.sem("gated"), st.sem("tap_done")
        with st.block() as block:
            @block.sync
            def _(sp):
                w.load(sp, first_unit("co") + RING)

            @block.gpsimd
            def _(pool):
                nc.gpsimd.memset(u[:, :, 0:PAD], 0.0).then_inc(u_zero, 1)
                nc.gpsimd.memset(u[:, :, T + PAD:T + 2 * PAD], 0.0).then_inc(u_zero, 1)

            @block.tensor
            def _(pe):
                def four_tiles(i, taken):
                    for j in range(RING):
                        ring = w.wait(pe, u0 + j, i)
                        if taken is gated:
                            pe.wait_ge(gated, 2 * i + (j // 2 - 1))
                        elif taken is z_kept:
                            pe.wait_ge(z_kept, i * RING + (j - RING + 1 - 2 * DT))
                        for k in range(DT):
                            mm = nc.tensor.matmul(bank[j][:], ring[:, k], hT[:, k], start=(k == 0), stop=(k == DT - 1))
                        mm.then_inc(w.done, 1)
                four_tiles(0, None)
                with pe.Fori(1, 5) as i:
                    four_tiles(i, gated)
                with pe.Fori(5, 44 // RING) as i:
                    four_tiles(i, z_kept)

            @block.scalar
            def _(act):
                def conv_gates(i, first):
                    for j in range(2):
                        act.wait_ge(w.done, i * RING + (u0 + 2 * j + 1))
                        if not first:
                            act.wait_ge(gated, 2 * i + (j - 1))
                        nc.scalar.activation(sig[:, j], bank[2 * j][:], ACT.Sigmoid).then_inc(sig_ready, 1)
                rounds(act, 4, conv_gates)
                for n in range(16, 28):
                    act.wait_ge(w.done, u0 + n + 1)
                    nc.scalar.activation(qkvT[:, n - 16], bank[n % RING][:], ACT.Copy).then_inc(z_kept, 1)
                for n in range(28, 44):
                    act.wait_ge(w.done, u0 + n + 1)
                    nc.scalar.activation(gateT[:, n - 28], bank[n % RING][:], ACT.Sigmoid).then_inc(z_kept, 1)

            @block.vector
            def _(dve):
                dve.wait_ge(u_zero, 2)
                for c in range(DT):
                    j = c % 2
                    dve.wait_ge(w.done, u0 + 2 * c + 2)
                    dve.wait_ge(sig_ready, c + 1)
                    nc.vector.tensor_tensor(u[:, c, PAD:PAD + T], bank[2 * j + 1][:], sig[:, j], ALU.mult).then_inc(gated, 1)
                for c in range(DT):
                    dve.wait_ge(gated, c + 1)
                    nc.vector.tensor_scalar(convT[:, c], u[:, c, 0:T], cols("conv_w", c), cols("conv_b", c), ALU.mult,
                                            ALU.add).then_inc(tap_done, 1)
                    for k in range(1, TAPS):
                        dve.wait_ge(tap_done, TAPS * c + k)
                        nc.vector.scalar_tensor_tensor(convT[:, c], u[:, c, k:k + T], cols("conv_w", k * DT + c),
                                                       convT[:, c], ALU.mult, ALU.add).then_inc(tap_done, 1)


def conv_norm(nc, w, bank, cols, ones, convT):
    with Stage(nc, "convnorm") as st:
        mean = st.sb("mean", [P, T])
        sq = st.sb("sq", [P, DT, T])
        var = st.sb("var", [P, T])
        std = st.sb("std", [P, T])
        rstd = st.sb("rstd", [P, T])
        sum_ready, mean_ready, centred, squared = st.sem("sum_ready"), st.sem("mean_ready"), st.sem("centred"), st.sem("squared")
        var_ready, std_ready, rstd_ready, scaled, done = st.sem("var_ready"), st.sem("std_ready"), st.sem("rstd_ready"), st.sem("scaled"), st.sem("done")
        with st.block() as block:
            @block.tensor
            def _(pe):
                for c in range(DT):
                    mm = nc.tensor.matmul(bank[0][:], ones, convT[:, c], start=(c == 0), stop=(c == DT - 1))
                mm.then_inc(sum_ready, 1)
                for c in range(DT):
                    pe.wait_ge(squared, c + 1)
                    mm = nc.tensor.matmul(bank[1][:], ones, sq[:, c], start=(c == 0), stop=(c == DT - 1))
                mm.then_inc(sum_ready, 1)

            @block.vector
            def _(dve):
                dve.wait_ge(sum_ready, 1)
                nc.vector.tensor_scalar(mean[:], bank[0][:], 1.0 / D, None, ALU.mult).then_inc(mean_ready, 1)
                dve.wait_ge(mean_ready, 1)
                for c in range(DT):
                    nc.vector.tensor_tensor(convT[:, c], convT[:, c], mean[:], ALU.subtract).then_inc(centred, 1)
                dve.wait_ge(sum_ready, 2)
                nc.vector.tensor_scalar(var[:], bank[1][:], 1.0 / D, EPS, ALU.mult, ALU.add).then_inc(var_ready, 1)
                dve.wait_ge(std_ready, 1)
                nc.vector.reciprocal(rstd[:], std[:]).then_inc(rstd_ready, 1)
                dve.wait_ge(rstd_ready, 1)
                for c in range(DT):
                    nc.vector.tensor_tensor(convT[:, c], convT[:, c], rstd[:], ALU.mult).then_inc(scaled, 1)

            @block.scalar
            def _(act):
                for c in range(DT):
                    act.wait_ge(centred, c + 1)
                    nc.scalar.activation(sq[:, c], convT[:, c], ACT.Square).then_inc(squared, 1)
                act.wait_ge(var_ready, 1)
                nc.scalar.activation(std[:], var[:], ACT.Sqrt).then_inc(std_ready, 1)
                for c in range(DT):
                    act.wait_ge(scaled, c + 1)
                    nc.scalar.activation(convT[:, c], convT[:, c], ACT.Silu, bias=cols("ln_b", c),
                                         scale=cols("ln_g", c)).then_inc(done, 1)


def merge_first(nc, w, bank, convT, attnT, gateT, mergedT):
    with Stage(nc, "merge1") as st:
        part = st.sb("part", [P, 2, 2, T])
        gated, merged = st.sem("gated"), st.sem("merged")
        u0 = first_unit("co")
        with st.block() as block:
            @block.sync
            def _(sp):
                w.load(sp, first_unit("wout1") + RING)

            @block.tensor
            def _(pe):
                for n in range(16):
                    j = n % RING
                    ring = w.wait(pe, u0 + n)
                    if n >= RING:
                        pe.wait_ge(gated, n - RING + 1)
                    src = attnT if n % 2 else convT
                    for k in range(DT):
                        mm = nc.tensor.matmul(bank[j][:], ring[:, k], src[:, k], start=(k == 0), stop=(k == DT - 1))
                    mm.then_inc(w.done, 1)

            @block.vector
            def _(dve):
                for f in range(DT):
                    if f >= 2:
                        dve.wait_ge(merged, f - 1)
                    for e in range(2):
                        dve.wait_ge(w.done, u0 + 2 * f + e + 1)
                        nc.vector.tensor_tensor(part[:, f % 2, e], bank[(2 * f + e) % RING][:], gateT[:, e * DT + f],
                                                ALU.mult).then_inc(gated, 1)
                    dve.wait_ge(gated, 2 * f + 2)
                    nc.vector.tensor_tensor(mergedT[:, f], part[:, f % 2, 0], part[:, f % 2, 1], ALU.add).then_inc(merged, 1)


def out_residual(nc, w, bank, name, mergedT, x, prefetch, store=None):
    with Stage(nc, name) as st:
        ready, added, stored = st.sem("ready"), st.sem("added"), st.sem("stored")
        u0 = first_unit(name)
        with st.block() as block:
            @block.sync
            def _(sp):
                w.load(sp, prefetch)
                if store is not None:
                    for t in range(TT):
                        sp.wait_ge(added, 2 * t + 2)
                        sp.dma_start(store[t * P:(t + 1) * P, :], x[:, t]).then_inc(stored, 16)
                    sp.wait_ge(stored, 16 * TT)

            @block.tensor
            def _(pe):
                for k in range(DT):
                    ring = w.wait(pe, u0 + k).rearrange("p a b -> p (a b)")
                    for t in range(TT):
                        for e in range(2):
                            mm = nc.tensor.matmul(bank[2 * t + e][:], mergedT[:, k, t * P:(t + 1) * P],
                                                  ring[:, e * 512:(e + 1) * 512], start=(k == 0), stop=(k == DT - 1))
                            if k == DT - 1 and (t, e) != (TT - 1, 1):
                                mm.then_inc(ready, 1)
                    mm.then_inc(w.done, 1)

            @block.vector
            def _(dve):
                for n in range(2 * TT):
                    t, e = n // 2, n % 2
                    if n < 2 * TT - 1:
                        dve.wait_ge(ready, n + 1)
                    else:
                        dve.wait_ge(w.done, u0 + DT)
                    nc.vector.tensor_tensor(x[:, t, e * 512:(e + 1) * 512], bank[n][:], x[:, t, e * 512:(e + 1) * 512],
                                            ALU.add).then_inc(added, 1)


def query_scores(nc, w, bank, h2T, subkeys, scores):
    with Stage(nc, "query") as st:
        queryT = st.sb("queryT", [P, RING, T])
        query_kept = st.sem("query_kept")
        u0 = first_unit("query")
        scored, score_kept = st.sem("scored"), st.sem("score_kept")
        with st.block() as block:
            @block.sync
            def _(sp):
                w.load(sp, first_unit("rwkv") + RING)

            @block.tensor
            def _(pe):
                def four_tiles(i, first):
                    for j in range(RING):
                        ring = w.wait(pe, u0 + j, i)
                        if not first:
                            pe.wait_ge(query_kept, i * RING + (j - RING + 1))
                        for k in range(DT):
                            mm = nc.tensor.matmul(bank[j][:], ring[:, k], h2T[:, k], start=(k == 0), stop=(k == DT - 1))
                        mm.then_inc(w.done, 1)
                    for j in range(RING):
                        pe.wait_ge(query_kept, i * RING + (j + 1))
                        if not first:
                            pe.wait_ge(score_kept, i * RING + (j - RING + 1))
                        for t in range(TT):
                            mm = nc.tensor.matmul(bank[4 + j][:, t * P:(t + 1) * P], queryT[:, j, t * P:(t + 1) * P],
                                                  subkeys[:, j % 2], start=True, stop=True)
                        mm.then_inc(scored, 1)
                rounds(pe, 4, four_tiles)

            @block.scalar
            def _(act):
                def four_tiles(i, first):
                    for j in range(RING):
                        act.wait_ge(w.done, i * RING + (u0 + j + 1))
                        if not first:
                            act.wait_ge(scored, i * RING + (j - RING + 1))
                        nc.scalar.activation(queryT[:, j], bank[j][:], ACT.Copy).then_inc(query_kept, 1)
                rounds(act, 4, four_tiles)

            @block.vector
            def _(dve):
                for n in range(16):
                    dve.wait_ge(scored, n + 1)
                    nc.vector.tensor_copy(scores[:, :, n], bank[4 + n % RING][:].rearrange("p (t n) -> p t n", t=TT)
                                          ).then_inc(score_kept, 1)


HEADS = TT * PH
GROUP = 4


def is_first(n, bound=1):
    return isinstance(n, int) and n < bound


def head_rounds(eng, body):
    def pair(i):
        for b in range(2):
            body(2 * i + b, b)
    pair(0)
    with eng.Fori(1, HEADS // 2 - 1) as i:
        pair(i)
    pair(HEADS // 2 - 1)


def experts(nc, w, bank, const, ident, scores, h2, peer_u, peer_v, x):
    HALF = TOPK // 2
    with Stage(nc, "peer") as st:
        ubuf = st.sb("ubuf", [P, 2 * GROUP, D])
        vbuf = st.sb("vbuf", [P, TOPK, D])
        junk = st.sb("junk", [P, D])
        sc = st.sb("sc", [P, 2, 2, NKEYS])
        index = st.sb("index", [P, 2, TOPK], I32)
        dots, gelu, weight = (st.sb(n, [P, TOPK]) for n in ("dots", "gelu", "weight"))
        diag = st.sb("diag", [P, TOPK, P])
        best, wheref, rcf, key = (st.sb(n, [P, 2, TOPK]) for n in ("best", "wheref", "rcf", "key"))
        where, rc = (st.sb(n, [P, 2, TOPK], U32) for n in ("where", "rc"))
        left = st.sb("left", [P, NKEYS])
        hot = st.sb("hot", [P, 2, TOPK, TOPK])
        pair, pairleft = hot[:, 0], hot[:, 1].rearrange("p a b -> p (a b)")
        top = st.sb("top", [P, TOPK])
        pos = st.sb("pos", [P, TOPK], U32)
        e, s, r = st.sb("e", [P, 2, TOPK]), st.sb("s", [P, 2]), st.sb("r", [P, 2])
        choice_open = st.sem("choice_open")
        scores_ready, step_done, index_ready = st.sem("scores_ready"), st.sem("step_done"), st.sem("index_ready")
        shifted, exped, recip_ready, gathers_open = (st.sem(n) for n in ("shifted", "exped", "recip_ready", "gathers_open"))
        u_arrived = [st.sem(f"u_arrived{q}") for q in range(2)]
        v_arrived = [st.sem(f"v_arrived{q}") for q in range(2)]
        dot_done, gelu_done, weight_ready = st.sem("dot_done"), st.sem("gelu_done"), st.sem("weight_ready")
        diag_ready, summed, added = st.sem("diag_ready"), st.sem("summed"), st.sem("added")
        iota = const.whole("iota").rearrange("p (a b) -> p a b", a=TOPK)
        score_heads = scores[:].rearrange("p t (h e) k -> p (t h) e k", e=2)

        with st.block() as block:
            @block.gpsimd
            def _(pool):
                def head(n, b):
                    pool.wait_ge(index_ready, n + 1)
                    for half in range(2):
                        for q in (2 * half, 2 * half + 1):
                            if not (is_first(n) and q < 2):
                                pool.wait_ge(dot_done, TOPK * n + GROUP * (q - 1))
                            pool.sem_inc(gathers_open, 1)
                            for k in range(GROUP):
                                col = index[:, b, q * GROUP + k:q * GROUP + k + 1]
                                pool.indirect_dma_start(ubuf[:, q % 2 * GROUP + k], None, peer_u,
                                                        bass.IndirectOffsetOnAxis(col, 0)).then_inc(u_arrived[q % 2], 16)
                        if not is_first(n):
                            pool.wait_ge(summed, 2 * n + (half - 1))
                        pool.sem_inc(gathers_open, 1)
                        for k in range(half * HALF, (half + 1) * HALF):
                            pool.indirect_dma_start(vbuf[:, k], None, peer_v,
                                                    bass.IndirectOffsetOnAxis(index[:, b, k:k + 1], 0)
                                                    ).then_inc(v_arrived[half], 16)
                head_rounds(pool, head)

            @block.vector
            def _(dve):
                def choose(n, b):
                    count = 0

                    def do(ins):
                        nonlocal count
                        count += 1
                        ins.then_inc(step_done, 1)
                        dve.wait_ge(step_done, count)

                    def top16(src, rest, vals, idx):
                        do(nc.vector.max(vals[:, 0:8], src))
                        do(nc.vector.max_index(idx[:, 0:8], vals[:, 0:8], src))
                        do(nc.vector.match_replace(rest, vals[:, 0:8], src, -3.0e38))
                        do(nc.vector.max(vals[:, 8:16], rest))
                        do(nc.vector.max_index(idx[:, 8:16], vals[:, 8:16], rest))

                    wide = [P, 2, TOPK, TOPK]
                    dve.wait_ge(scores_ready, n + 1)
                    dve.sem_inc(choice_open, 1)
                    dve.sem_clear(step_done)
                    for half in range(2):
                        top16(sc[:, b, half], left[:], best[:, half], where[:, half])
                    do(nc.vector.tensor_tensor(pair, best[:, 0].unsqueeze(2).broadcast_to([P, TOPK, TOPK]),
                                               best[:, 1].unsqueeze(1).broadcast_to([P, TOPK, TOPK]), ALU.add))
                    top16(pair.rearrange("p a b -> p (a b)"), pairleft, top[:], pos[:])
                    nc.vector.tensor_scalar(rc[:, 0], pos[:], 4, None, ALU.logical_shift_right)
                    nc.vector.tensor_copy(wheref[:], where[:])
                    do(nc.vector.tensor_scalar(rc[:, 1], pos[:], 15, None, ALU.bitwise_and))
                    do(nc.vector.tensor_copy(rcf[:], rc[:]))
                    do(nc.vector.tensor_tensor(hot[:], rcf[:].unsqueeze(3).broadcast_to(wide),
                                               iota.unsqueeze(1).broadcast_to(wide), ALU.is_equal))
                    do(nc.vector.tensor_tensor(hot[:], hot[:], wheref[:].unsqueeze(2).broadcast_to(wide), ALU.mult))
                    do(nc.vector.tensor_reduce(key[:], hot[:], AXX, ALU.add))
                    if not is_first(n, 2):
                        for q in range(2):
                            dve.wait_ge(u_arrived[q], 16 * HALF * n - 16 * HALF)
                            dve.wait_ge(v_arrived[q], 16 * HALF * n - 16 * HALF)
                        dve.wait_ge(weight_ready, n - 1)
                    nc.vector.scalar_tensor_tensor(index[:, b], key[:, 0], float(NKEYS), key[:, 1], ALU.mult,
                                                   ALU.add).then_inc(index_ready, 1)
                    nc.vector.tensor_scalar(e[:, b], top[:], top[:, 0:1], None, ALU.subtract).then_inc(shifted, 1)
                    dve.wait_ge(exped, n + 1)
                    nc.vector.reciprocal(r[:, b:b + 1], s[:, b:b + 1]).then_inc(recip_ready, 1)

                def add(n, t, b):
                    dve.wait_ge(summed, 2 * n + 2)
                    if not is_first(n):
                        dve.wait_ge(added, 2 * n)
                    for c in range(2):
                        part = x[:, t, c * 512:(c + 1) * 512]
                        nc.vector.tensor_tensor(part, bank[2 * b + c][:], part, ALU.add).then_inc(added, 1)

                def head(n, b):
                    t = n // PH
                    for q in range(4):
                        dve.wait_ge(u_arrived[q % 2], 16 * HALF * n + 16 * GROUP * (q // 2 + 1))
                        if q == 0 and not is_first(n):
                            dve.wait_ge(gelu_done, n)
                        for k in range(GROUP):
                            if not (is_first(n) and q + k == 0):
                                dve.wait_ge(dot_done, TOPK * n + (GROUP * q + k))
                            nc.vector.scalar_tensor_tensor(junk[:], ubuf[:, q % 2 * GROUP + k], 1.0, h2[:, t], ALU.mult,
                                                           ALU.mult, accum_out=dots[:, GROUP * q + k:GROUP * q + k + 1]
                                                           ).then_inc(dot_done, 1)
                    dve.wait_ge(gelu_done, n + 1)
                    dve.wait_ge(recip_ready, n + 1)
                    if not is_first(n):
                        dve.wait_ge(diag_ready, TOPK * n)
                    nc.vector.scalar_tensor_tensor(weight[:], gelu[:], r[:, b:b + 1], e[:, b], ALU.mult, ALU.mult
                                                   ).then_inc(weight_ready, 1)
                    if not is_first(n):
                        add(n - 1, (n - 1) // PH, 1 - b)
                    if not (isinstance(n, int) and n + 2 >= HEADS):
                        choose(n + 2, b)

                choose(0, 0)
                choose(1, 1)
                head_rounds(dve, head)
                add(HEADS - 1, TT - 1, 1)

            @block.scalar
            def _(act):
                def copy_scores(n, b):
                    if not is_first(n, 2):
                        act.wait_ge(index_ready, n - 1)
                    nc.scalar.activation(sc[:, b], score_heads[:, n], ACT.Copy).then_inc(scores_ready, 1)

                def exps(n, b):
                    act.wait_ge(shifted, n + 1)
                    if not is_first(n, 2):
                        act.wait_ge(recip_ready, n - 1)
                    nc.scalar.activation(e[:, b], e[:, b], ACT.Exp, accum_out=s[:, b:b + 1]).then_inc(exped, 1)

                def head(n, b):
                    if not (isinstance(n, int) and n + 2 >= HEADS):
                        copy_scores(n + 2, b)
                    act.wait_ge(dot_done, TOPK * n + TOPK)
                    if not is_first(n):
                        act.wait_ge(weight_ready, n)
                    nc.scalar.activation(gelu[:], dots[:], ACT.Gelu).then_inc(gelu_done, 1)
                    act.wait_ge(weight_ready, n + 1)
                    for k in range(TOPK):
                        if not is_first(n) and k % HALF == 0:
                            act.wait_ge(summed, 2 * n + (k // HALF - 1))
                        nc.scalar.activation(diag[:, k], ident, ACT.Copy, scale=weight[:, k:k + 1]).then_inc(diag_ready, 1)
                    if not (isinstance(n, int) and n + 2 >= HEADS):
                        exps(n + 2, b)

                copy_scores(0, 0)
                copy_scores(1, 1)
                exps(0, 0)
                exps(1, 1)
                head_rounds(act, head)

            @block.tensor
            def _(pe):
                def head(n, b):
                    if not is_first(n, 2):
                        pe.wait_ge(added, 2 * n - 2)
                    for half in range(2):
                        pe.wait_ge(v_arrived[half], 16 * HALF * n + 16 * HALF)
                        for k in range(half * HALF, (half + 1) * HALF):
                            pe.wait_ge(diag_ready, TOPK * n + (k + 1))
                            for c in range(2):
                                mm = nc.tensor.matmul(bank[2 * b + c][:], diag[:, k], vbuf[:, k, c * 512:(c + 1) * 512],
                                                      start=(k == 0), stop=(k == TOPK - 1))
                        mm.then_inc(summed, 1)
                head_rounds(pe, head)


def final_norm(nc, w, x, gain):
    with Stage(nc, "final") as st:
        junk = st.sb("junk", [P, D])
        ss, ms, rms, rstd = (st.sb(n, [P, TT]) for n in ("ss", "ms", "rms", "rstd"))
        squared, mean_ready, root_ready = st.sem("squared"), st.sem("mean_ready"), st.sem("root_ready")
        rstd_ready, normed = st.sem("rstd_ready"), st.sem("normed")
        with st.block() as block:
            @block.scalar
            def _(act):
                for t in range(TT):
                    if t:
                        act.wait_ge(squared, t)
                    nc.scalar.activation(junk[:], x[:, t], ACT.Square, accum_out=ss[:, t:t + 1]).then_inc(squared, 1)
                act.wait_ge(mean_ready, 1)
                nc.scalar.activation(rms[:], ms[:], ACT.Sqrt).then_inc(root_ready, 1)

            @block.vector
            def _(dve):
                dve.wait_ge(squared, TT)
                nc.vector.tensor_scalar(ms[:], ss[:], 1.0 / D, EPS, ALU.mult, ALU.add).then_inc(mean_ready, 1)
                dve.wait_ge(root_ready, 1)
                nc.vector.reciprocal(rstd[:], rms[:]).then_inc(rstd_ready, 1)
                dve.wait_ge(rstd_ready, 1)
                for t in range(TT):
                    nc.vector.scalar_tensor_tensor(x[:, t], x[:, t], rstd[:, t:t + 1], gain, ALU.mult,
                                                   ALU.mult).then_inc(normed, 1)


def project_tiles(nc, w, bank, name, unit, count, src, takers, prefetch):
    width = src.shape[-1]
    with Stage(nc, name) as st:
        kept = st.sem("kept")
        u0 = first_unit(unit)
        with st.block() as block:
            @block.sync
            def _(sp):
                w.load(sp, prefetch)

            @block.tensor
            def _(pe):
                def four_tiles(i, first, count=RING):
                    for j in range(count):
                        ring = w.wait(pe, u0 + j, i)
                        if not first:
                            pe.wait_ge(kept, i * RING + (j - RING + 1))
                        for k in range(DT):
                            mm = nc.tensor.matmul(bank[j][:, 0:width], ring[:, k], src[:, k], start=(k == 0),
                                                  stop=(k == DT - 1))
                        mm.then_inc(w.done, 1)
                rounds(pe, count // RING, four_tiles)
                if count % RING:
                    four_tiles(count // RING, False, count % RING)

            @block.scalar
            def _(act):
                for n in range(count):
                    func, to = takers[n]
                    act.wait_ge(w.done, u0 + n + 1)
                    nc.scalar.activation(to, bank[n % RING][:, 0:width], func).then_inc(kept, 1)


def rms_over_partitions(nc, w, bank, name, tiles, gain, group_ones, per, scale_tile=None):
    width = tiles[0].shape[-1]
    with Stage(nc, name) as st:
        sq = st.sb("sq", [P, 2, width])
        ms = st.sb("ms", [P, 2, width])
        root = st.sb("root", [P, 2, width])
        rstd = st.sb("rstd", [P, 2, width])
        squared, summed, mean_ready, root_ready, step_done = (st.sem(n) for n in (
            "squared", "summed", "mean_ready", "root_ready", "step_done"))
        with st.block() as block:
            @block.scalar
            def _(act):
                for n in range(len(tiles) + 1):
                    if n < len(tiles):
                        if n >= 2:
                            act.wait_ge(summed, n - 1)
                        nc.scalar.activation(sq[:, n % 2], tiles[n], ACT.Square).then_inc(squared, 1)
                    if n:
                        m = n - 1
                        act.wait_ge(mean_ready, m + 1)
                        if m >= 2:
                            act.wait_ge(step_done, 2 * m - 3)
                        nc.scalar.activation(root[:, m % 2], ms[:, m % 2], ACT.Sqrt).then_inc(root_ready, 1)

            @block.tensor
            def _(pe):
                for n in range(len(tiles)):
                    pe.wait_ge(squared, n + 1)
                    if n >= 2:
                        pe.wait_ge(mean_ready, n - 1)
                    nc.tensor.matmul(bank[n % 2][:, 0:width], group_ones, sq[:, n % 2], start=True, stop=True
                                     ).then_inc(summed, 1)

            @block.vector
            def _(dve):
                for n in range(len(tiles)):
                    dve.wait_ge(summed, n + 1)
                    if n >= 2:
                        dve.wait_ge(root_ready, n - 1)
                    nc.vector.tensor_scalar(ms[:, n % 2], bank[n % 2][:, 0:width], 1.0 / per, EPS, ALU.mult,
                                            ALU.add).then_inc(mean_ready, 1)
                    dve.wait_ge(root_ready, n + 1)
                    if n >= 2:
                        dve.wait_ge(step_done, 2 * n - 2)
                    nc.vector.reciprocal(rstd[:, n % 2], root[:, n % 2]).then_inc(step_done, 1)
                    dve.wait_ge(step_done, 2 * n + 1)
                    nc.vector.scalar_tensor_tensor(tiles[n], tiles[n], gain, rstd[:, n % 2], ALU.mult,
                                                   ALU.mult).then_inc(step_done, 1)


def second_block(nc, ctx, w, bank, a, x, out, dump, load):
    cols_sb = ctx.enter_context(nc.sbuf_tensor("cols2", [P, sum(COLS2.values())], F32))
    const_sb = ctx.enter_context(nc.sbuf_tensor("const2", [P, sum(CONST2.values())], F32))
    cols, const = Columns(cols_sb, COLS2), Columns(const_sb, CONST2)
    ident = const.whole("ident")
    load("second", [(cols_sb[:], a["cols2"]), (const_sb[:], a["const2"])])

    hT = ctx.enter_context(nc.sbuf_tensor("h3T", [P, DT, T], F32))
    yT = [ctx.enter_context(nc.sbuf_tensor("yaT", [P, 4, T], F32))]
    norm_to_T(nc, w, bank, "norm3", x, TT, cols.whole("norm"), ident, hT, first_unit("rwkv") + RING)
    rwkv_branch(nc, w, bank, a, cols, const, hT, yT[0], dump, load)
    yT += [ctx.enter_context(nc.sbuf_tensor(f"y{n}T", [P, 4, T], F32)) for n in "bc"]
    sliding_branch(nc, w, bank, a, cols, const, hT, yT[1], dump, load)
    memory_branch(nc, w, bank, a, cols, const, hT, yT[2], dump, load)
    with nc.sbuf_tensor("merged2T", [P, DT, T], F32) as mergedT:
        merge_second(nc, w, bank, hT, yT, mergedT)
        out_residual(nc, w, bank, "wout2", mergedT, x, sum(n for _, n in UNITS), store=out)


def memory_branch(nc, w, bank, a, cols, const, hT, y, dump, load):
    ident, ones = const.whole("ident"), const.whole("ones")
    with ExitStack() as s:
        kT = s.enter_context(nc.sbuf_tensor("kT", [P, 4, MEM], F32))
        v_tok = s.enter_context(nc.sbuf_tensor("vm_tok", [P, 2, 512], F32))
        with ExitStack() as m:
            mem = m.enter_context(nc.sbuf_tensor("mem", [P, 2, D], F32))
            memT = m.enter_context(nc.sbuf_tensor("memT", [P, DT, MEM], F32))
            vT = m.enter_context(nc.sbuf_tensor("vT", [P, 4, MEM], F32))
            load("mem", [(mem[:], a["mem"].rearrange("(t p) d -> p t d", p=P))])
            norm_to_T(nc, w, bank, "memnorm", mem, 2, cols.whole("memnorm"), ident, memT, first_unit("mem") + RING)
            project_tiles(nc, w, bank, "memkv", "mem", 8, memT,
                          [(ACT.Copy, kT[:, n]) for n in range(4)] + [(ACT.Copy, vT[:, n]) for n in range(4)],
                          first_unit("xq") + RING)
            turn_tiles(nc, w, bank, "turn_vm", [([vT[:, n, c * P:(c + 1) * P] for n in range(4)], v_tok[:, c])
                                                for c in range(2)], ident, first_unit("xq") + RING)
        rms_over_partitions(nc, w, bank, "knorm", [kT[:, n] for n in range(4)], cols.whole("xk_g"), ones, P)
        qz = s.enter_context(nc.sbuf_tensor("xqz", [P, 8, T], F32))
        project_tiles(nc, w, bank, "xqz", "xq", 8, hT,
                      [(ACT.Copy if n < 4 else ACT.Silu, qz[:, n]) for n in range(8)], first_unit("merge") + RING)
        rms_over_partitions(nc, w, bank, "xqnorm", [qz[:, n] for n in range(4)], cols.whole("xq_g"), ones, P)
        units = [dict(q=qz[:, h, b * P:(b + 1) * P], k=kT[:, h], bias=None,
                      v=[v_tok[:, c, h * P:(h + 1) * P] for c in range(2)], half=0) for b in range(TT) for h in range(4)]
        attention(nc, w, bank, "attn3", units, first_unit("merge") + RING, scale=P ** -0.5, sink=None, ident=ident,
                  out=lambda g: y[:, :, g * P:(g + 1) * P], group=4, dim=P)
        multiply(nc, "xgate", y, qz[:, 4:8])
    dump("yc", y)


def multiply(nc, name, to, by):
    with Stage(nc, name) as st, st.block() as block:
        @block.vector
        def _(dve):
            nc.vector.tensor_tensor(to[:], to[:], by, ALU.mult)


def sliding_branch(nc, w, bank, a, cols, const, hT, y, dump, load):
    ident = const.whole("ident")
    with ExitStack() as s:
        z = s.enter_context(nc.sbuf_tensor("swz", [P, 10, T], F32))
        v_tok = s.enter_context(nc.sbuf_tensor("vs_tok", [P, TT, P], F32))
        sink8 = s.enter_context(nc.sbuf_tensor("sink8_2", [P, 8], F32))
        project_tiles(nc, w, bank, "swz", "sw", 10, hT,
                      [(ACT.Copy if n < 6 else ACT.Silu, z[:, n]) for n in range(10)], first_unit("mem") + RING)
        rms_over_partitions(nc, w, bank, "sqnorm", [z[:, n] for n in range(4)], cols.whole("q_g"), const.whole("halves"), HD)
        rms_over_partitions(nc, w, bank, "sknorm", [z[:, 4]], cols.whole("k_g"), const.whole("halves"), HD)
        turn_tiles(nc, w, bank, "turn_vs", [([z[:, 5, t * P:(t + 1) * P]], v_tok[:, t]) for t in range(TT)], ident,
                   first_unit("mem") + RING)
        rotate(nc, bank, a, cols, const, z, load)
        with Stage(nc, "sink2") as st, st.block() as block:
            @block.vector
            def _(dve):
                nc.vector.tensor_scalar(sink8[:], cols.whole("sinks"), float(HD ** 0.5), None, ALU.mult)
        units = []
        for b in range(TT):
            lo = max(b - 1, 0)
            for i in range(4):
                for e in range(2):
                    h, part = HEADS2[i][e], slice(e * HD, (e + 1) * HD)
                    units.append(dict(q=z[part, i, b * P:(b + 1) * P], k=z[part, 4, lo * P:(b + 1) * P],
                                      bias=(const.whole("band")[:, (lo - b + 1) * P:2 * P], 1.0),
                                      v=[v_tok[:, c, part] for c in range(lo, b + 1)],
                                      sink=cols("sinks", h), sink_scaled=sink8[:, h:h + 1], half=e))
        attention(nc, w, bank, "attn2", units, first_unit("mem") + RING, scale=HD ** -0.5, sink=True, ident=ident,
                  out=lambda g: y[:, :, g * P:(g + 1) * P], group=8, dim=HD)
        multiply(nc, "sgate", y, z[:, 6:10])
    dump("yb", y)


def rotate(nc, bank, a, cols, const, z, load):
    two_pi = 2 * np.pi
    c1 = 6.28125
    c2 = float(np.float32(np.floor((two_pi - c1) * 2 ** 22) / 2 ** 22))
    c3 = float(two_pi - c1 - c2)
    magic = 1.5 * 2 ** 23
    with Stage(nc, "rope") as st:
        pos = st.sb("pos", [P, T], I32)
        angle, turns, count, part, trig = (st.sb(n, [P, T]) for n in ("angle", "turns", "count", "part", "trig"))
        sin, cos = st.sb("sin", [P, T]), st.sb("cos", [P, T])
        straight = st.sb("straight", [P, 2, T])
        crossed = st.sb("crossed", [P, 2, T])
        step_done, reduced, trig_ready, swapped, taken = (st.sem(n) for n in (
            "step_done", "reduced", "trig_ready", "swapped", "taken"))
        load("positions", [(pos[:], a["positions"])])
        with st.block() as block:
            @block.vector
            def _(dve):
                do = Chain(dve, step_done)
                do(nc.vector.tensor_copy(angle[:], pos[:]))
                do(nc.vector.tensor_scalar(angle[:], angle[:], cols("inv"), None, ALU.mult))
                for n, (shift, quarter) in enumerate(((0.0, 0.0), (0.25, np.pi / 2))):
                    do(nc.vector.tensor_scalar(turns[:], angle[:], 1.0 / two_pi, shift, ALU.mult, ALU.add))
                    do(nc.vector.tensor_scalar(count[:], turns[:], magic, None, ALU.add))
                    do(nc.vector.tensor_scalar(count[:], count[:], -magic, None, ALU.add))
                    do(nc.vector.scalar_tensor_tensor(part[:], count[:], -c1, angle[:], ALU.mult, ALU.add))
                    do(nc.vector.scalar_tensor_tensor(part[:], count[:], -c2, part[:], ALU.mult, ALU.add))
                    do(nc.vector.scalar_tensor_tensor(part[:], count[:], -c3, part[:], ALU.mult, ALU.add))
                    if n:
                        dve.wait_ge(trig_ready, n)
                    do(nc.vector.tensor_scalar(trig[:], part[:], float(quarter), 3.1415925, ALU.add, ALU.min))
                    nc.vector.tensor_scalar(trig[:], trig[:], -3.1415925, None, ALU.max).then_inc(reduced, 1)
                for i in range(5):
                    dve.wait_ge(trig_ready, 2)
                    dve.wait_ge(swapped, i + 1)
                    if i >= 2:
                        dve.wait_ge(taken, i - 1)
                    do(nc.vector.tensor_tensor(crossed[:, i % 2], bank[i][:], sin[:], ALU.mult))
                    do(nc.vector.tensor_tensor(straight[:, i % 2], z[:, i], cos[:], ALU.mult))
                    nc.vector.tensor_tensor(z[:, i], straight[:, i % 2], crossed[:, i % 2], ALU.add).then_inc(taken, 1)

            @block.scalar
            def _(act):
                for n, to in enumerate((sin, cos)):
                    act.wait_ge(reduced, n + 1)
                    nc.scalar.activation(to[:], trig[:], ACT.Sin).then_inc(trig_ready, 1)

            @block.tensor
            def _(pe):
                for i in range(5):
                    nc.tensor.matmul(bank[i][:], const.whole("swap"), z[:, i], start=True, stop=True).then_inc(swapped, 1)


def rwkv_branch(nc, w, bank, a, cols, const, hT, y, dump, load):
    ident, halves = const.whole("ident"), const.whole("halves")
    with ExitStack() as s:
        sb = lambda n, shape: s.enter_context(nc.sbuf_tensor(f"rw_{n}", shape, F32))
        gate = sb("gate", [P, 4, T])
        bonus = sb("bonus", [P, 4, T])
        r_end = sb("r_end", [P, 4, T // CH])
        R = sb("R", [P, 4, T])
        A = sb("A", [P, 4, T])
        B = sb("B", [P, 4, T])
        Kt = sb("K", [P, 4, T])
        toks = {n: sb(f"{n}_tok", [P, TT, 512]) for n in "ABKV"}
        with ExitStack() as s2:
            z = s2.enter_context(nc.sbuf_tensor("rwz", [P, 13, T + 1], F32))
            project_tiles(nc, w, bank, "rwz", "rwkv", 17, hT,
                          [(ACT.Copy, z[:, n, 1:T + 1]) for n in range(13)] + [(ACT.Silu, gate[:, n]) for n in range(4)],
                          first_unit("sw") + RING)
            rwkv_prepare(nc, bank, a, cols, const, z, R, A, B, Kt, bonus, r_end, toks, load)
            turn_tiles(nc, w, bank, "turn_rw",
                       [([m[:, n, o + t * P:o + (t + 1) * P] for n in range(4)], toks[name][:, t])
                        for name, m, o in (("A", A, 0), ("B", B, 0), ("K", Kt, 0), ("V", z[:, 8:12], 1))
                        for t in range(TT)], ident, first_unit("sw") + RING)
        ZW = sb("ZW", [P, TT, 8, 2 * CH])
        WT = sb("WT", [P, TT, 4, P])
        for t in range(TT):
            rwkv_solve(nc, bank, const, t, A, B, Kt, toks, ZW, WT)
        S = sb("S", [P, T // CH + 1, 4, CH])
        rwkv_chain(nc, bank, const, toks, ZW, r_end, S)
        for t in range(TT):
            rwkv_output(nc, bank, const, t, R, B, Kt, toks, ZW, WT, S, y)
        rwkv_finish(nc, bank, cols, halves, y, bonus, gate, dump)


def rwkv_prepare(nc, bank, a, cols, const, z, R, A, B, Kt, bonus, r_end, toks, load):
    halves = const.whole("halves")
    with Stage(nc, "rwprep") as st:
        lora, w0, tl, tmp = toks["V"][:, 0], toks["V"][:, 1], toks["V"][:, 2], toks["K"][:, 0:2]
        rate, aa = toks["A"], toks["B"]
        inv = Kt
        load("lora", [(lora, a["lora"]), (w0, a["rows2"])])
        zero, step_done, mixed, tanh_ready = st.sem("zero"), st.sem("step_done"), st.sem("mixed"), st.sem("tanh_ready")
        lora_ready, biased, rate_ready, a_ready = st.sem("lora_ready"), st.sem("biased"), st.sem("rate_ready"), st.sem("a_ready")
        with st.block() as block:
            @block.vector
            def _(dve):
                do = Chain(dve, step_done)
                do(nc.vector.memset(z[:, :, 0:1], 0.0))
                for n in [12] + list(range(12)):
                    do(nc.vector.tensor_tensor(tmp[:, n % 2], z[:, n, 0:T], z[:, n, 1:T + 1], ALU.subtract))
                    ins = nc.vector.scalar_tensor_tensor(z[:, n, 1:T + 1], tmp[:, n % 2], cols("mu", n), z[:, n, 1:T + 1],
                                                         ALU.mult, ALU.add)
                    if n == 12:
                        ins.then_inc(mixed, 1)
                        dve.wait_ge(mixed, 1)
                    else:
                        do(ins)
                for t in range(TT):
                    dve.wait_ge(lora_ready, t + 1)
                    nc.vector.tensor_tensor(rate[:, t], bank[t][:], w0, ALU.add).then_inc(biased, 1)

            @block.scalar
            def _(act):
                act.wait_ge(mixed, 1)
                nc.scalar.activation(tl[0:CH], z[0:CH, 12, 1:T + 1], ACT.Tanh).then_inc(tanh_ready, 1)
                for t in range(TT):
                    act.wait_ge(biased, t + 1)
                    nc.scalar.activation(rate[:, t], rate[:, t], ACT.Sigmoid).then_inc(rate_ready, 1)
                for c in range(4):
                    act.wait_ge(lora_ready, TT + c + 1)
                    nc.scalar.activation(aa[:, c], bank[4 + c][:], ACT.Sigmoid, bias=cols("a0", c)).then_inc(a_ready, 1)

            @block.tensor
            def _(pe):
                pe.wait_ge(tanh_ready, 1)
                for t in range(TT):
                    nc.tensor.matmul(bank[t][:], tl[0:CH, t * P:(t + 1) * P], lora[0:CH, :], start=True,
                                     stop=True).then_inc(lora_ready, 1)
                for c in range(4):
                    nc.tensor.matmul(bank[4 + c][:], lora[CH:P, c * P:(c + 1) * P], z[CH:P, 12, 1:T + 1], start=True,
                                     stop=True).then_inc(lora_ready, 1)
        cum_ready, exp_ready = st.sem("cum_ready"), st.sem("exp_ready")
        with st.block() as block:
            @block.tensor
            def _(pe):
                for e, mask in enumerate(("incl", "strict")):
                    for c in range(4):
                        for t in range(TT):
                            mm = nc.tensor.matmul(bank[4 * e + c][:, t * P:(t + 1) * P], rate[:, t, c * P:(c + 1) * P],
                                                  const.whole(mask), start=True, stop=True)
                        mm.then_inc(cum_ready, 1)

            @block.scalar
            def _(act):
                for c in range(4):
                    act.wait_ge(cum_ready, c + 1)
                    nc.scalar.activation(R[:, c], bank[c][:], ACT.Exp, scale=-DECAY).then_inc(exp_ready, 1)
                    nc.scalar.activation(inv[:, c], bank[c][:], ACT.Exp, scale=DECAY).then_inc(exp_ready, 1)
                for c in range(4):
                    act.wait_ge(cum_ready, 4 + c + 1)
                    nc.scalar.activation(A[:, c], bank[4 + c][:], ACT.Exp, scale=-DECAY).then_inc(exp_ready, 1)
        kk_ready, squared, norm_ready, root_ready, k_done, rk_ready, bonus_ready = (st.sem(n) for n in (
            "kk_ready", "squared", "norm_ready", "root_ready", "k_done", "rk_ready", "bonus_ready"))
        with st.block() as block:
            @block.vector
            def _(dve):
                do = Chain(dve, k_done)
                zr, zk, zv = ([z[:, n + c, 1:T + 1] for c in range(4)] for n in (0, 4, 8))
                do(nc.vector.tensor_copy(r_end[:], R[:, :, CH - 1:T:CH]))
                for c in range(4):
                    nc.vector.tensor_scalar(B[:, c], zk[c], cols("k_k", c), None, ALU.mult).then_inc(kk_ready, 1)
                for c in range(4):
                    dve.wait_ge(root_ready, c + 1)
                    do(nc.vector.tensor_scalar(tmp[:, 0], rate[:, c], 1e-12, None, ALU.max))
                    do(nc.vector.reciprocal(tmp[:, 1], tmp[:, 0]))
                    do(nc.vector.tensor_tensor(B[:, c], B[:, c], tmp[:, 1], ALU.mult))
                    do(nc.vector.scalar_tensor_tensor(A[:, c], B[:, c], -1.0, A[:, c], ALU.mult, ALU.mult))
                    do(nc.vector.tensor_tensor(B[:, c], B[:, c], aa[:, c], ALU.mult))
                    do(nc.vector.tensor_tensor(B[:, c], B[:, c], inv[:, c], ALU.mult))
                    do(nc.vector.tensor_scalar(aa[:, c], aa[:, c], -1.0, cols("k_a", c), ALU.add, ALU.mult))
                    do(nc.vector.scalar_tensor_tensor(zk[c], aa[:, c], 1.0, zk[c], ALU.add, ALU.mult))
                    do(nc.vector.tensor_tensor(Kt[:, c], zk[c], inv[:, c], ALU.mult))
                    do(nc.vector.tensor_tensor(bonus[:, c], zr[c], zk[c], ALU.mult))
                    nc.vector.tensor_scalar(bonus[:, c], bonus[:, c], cols("r_k", c), None, ALU.mult).then_inc(rk_ready, 1)
                    do(nc.vector.tensor_tensor(R[:, c], zr[c], R[:, c], ALU.mult))
                for c in range(4):
                    dve.wait_ge(bonus_ready, c + 1)
                    do(nc.vector.tensor_tensor(bonus[:, c], bank[4 + c][:], zv[c], ALU.mult))

            @block.scalar
            def _(act):
                for c in range(4):
                    act.wait_ge(kk_ready, c + 1)
                    nc.scalar.activation(rate[:, c], B[:, c], ACT.Square).then_inc(squared, 1)
                for c in range(4):
                    act.wait_ge(norm_ready, c + 1)
                    nc.scalar.activation(rate[:, c], bank[c][:], ACT.Sqrt).then_inc(root_ready, 1)

            @block.tensor
            def _(pe):
                for c in range(4):
                    pe.wait_ge(squared, c + 1)
                    nc.tensor.matmul(bank[c][:], halves, rate[:, c], start=True, stop=True).then_inc(norm_ready, 1)
                for c in range(4):
                    pe.wait_ge(rk_ready, c + 1)
                    nc.tensor.matmul(bank[4 + c][:], halves, bonus[:, c], start=True, stop=True).then_inc(bonus_ready, 1)


def head(o):
    half, c = o // 4, o % 4
    return slice(half * HD, (half + 1) * HD), c, slice((2 * c + half) * HD, (2 * c + half + 1) * HD)


def by_head(tok):
    return tok.rearrange("p (c e v) -> p e c v", c=4, e=2)


def over_heads(mask, n=4):
    return mask.unsqueeze(1).broadcast_to([P, n, P])


def rwkv_solve(nc, bank, const, t, A, B, Kt, toks, ZW, WT):
    ident = const.whole("ident")
    here = slice(t * P, (t + 1) * P)
    with Stage(nc, f"solve{t}") as st:
        AB, AK = st.sb("AB", [P, 8, P]), st.sb("AK", [P, 8, P])
        Tm, TmT, G, E = (st.sb(n, [P, 8, P]) for n in ("T", "TT", "G", "E"))
        QA = st.sb("QA", [P, 8, 2 * CH])
        step_done, products, turned, g_kept, filled = (st.sem(n) for n in (
            "step_done", "products", "turned", "g_kept", "filled"))
        with st.block() as block:
            @block.tensor
            def _(pe):
                for e, left in enumerate((B, Kt)):
                    for h in range(8):
                        part, c, cols = head(h)
                        mm = nc.tensor.matmul(bank[2 * e + h // 4][:, h % 4 * P:(h % 4 + 1) * P], left[part, c, here],
                                              A[part, c, here], start=True, stop=True)
                        if h % 4 == 3:
                            mm.then_inc(products, 1)
                pe.wait_ge(step_done, 6)
                for h in range(8):
                    mm = nc.tensor.transpose(bank[4 + h // 4][:, h % 4 * P:(h % 4 + 1) * P], TmT[:, h], ident)
                mm.then_inc(turned, 1)
                for h in range(8):
                    _, _, cols = head(h)
                    mm = nc.tensor.matmul(bank[6][:, h * CH:(h + 1) * CH], AK[:, h], toks["V"][:, t, cols],
                                          start=True, stop=True)
                mm.then_inc(turned, 1)

            @block.vector
            def _(dve):
                do = Chain(dve, step_done)
                for n, to in enumerate((AB, AB, AK, AK)):
                    dve.wait_ge(products, n + 1)
                    g = n % 2
                    do(nc.vector.tensor_tensor(to[:, 4 * g:4 * g + 4], bank[n][:].rearrange("p (h t) -> p h t", h=4),
                                               over_heads(const.whole("strict")), ALU.mult))
                do(nc.vector.tensor_tensor(TmT[:], AB[:], over_heads(const("level", 0, P), 8), ALU.mult))
                do(nc.vector.tensor_tensor(TmT[:], TmT[:], over_heads(ident, 8), ALU.add))

            @block.scalar
            def _(act):
                act.wait_ge(turned, 1)
                for g in range(2):
                    nc.scalar.activation(Tm[:, 4 * g:4 * g + 4], bank[4 + g][:].rearrange("p (h t) -> p h t", h=4),
                                         ACT.Copy).then_inc(filled, 1)
                act.wait_ge(turned, 2)
                nc.scalar.activation(QA[:, :, 0:CH], bank[6][:].rearrange("p (h t) -> p h t", h=8), ACT.Copy
                                     ).then_inc(filled, 1)
                for e in range(2):
                    nc.scalar.activation(QA[:, 4 * e:4 * e + 4, CH:2 * CH], by_head(toks["A"][:, t])[:, e], ACT.Copy
                                         ).then_inc(filled, 1)
        g_ready, d_ready, added, masked = (st.sem(n) for n in ("g_ready", "d_ready", "added", "masked"))
        with st.block() as block:
            @block.tensor
            def _(pe):
                for m in range(1, LEVELS):
                    for g in range(2):
                        pe.wait_ge(masked, m)
                        if m > 1:
                            pe.wait_ge(added, 2 * (m - 2) * 2 + 2 * g + 2)
                        for h in range(4 * g, 4 * g + 4):
                            mm = nc.tensor.matmul(bank[g][:, h % 4 * P:(h % 4 + 1) * P], E[:, h], Tm[:, h], start=True,
                                                  stop=True)
                        mm.then_inc(g_ready, 1)
                    for g in range(2):
                        pe.wait_ge(g_kept, 2 * (m - 1) + g + 1)
                        for e in range(2):
                            for h in range(4 * g, 4 * g + 4):
                                mm = nc.tensor.matmul(bank[2 + 2 * g + e][:, h % 4 * P:(h % 4 + 1) * P],
                                                      G[:, h] if e else TmT[:, h], TmT[:, h] if e else G[:, h],
                                                      start=True, stop=True)
                            mm.then_inc(d_ready, 1)

            @block.vector
            def _(dve):
                for m in range(1, LEVELS):
                    if m > 1:
                        dve.wait_ge(g_ready, 2 * (m - 1))
                    nc.vector.tensor_tensor(E[:], AB[:], over_heads(const("level", m * P, P), 8), ALU.mult
                                            ).then_inc(masked, 1)
                    for g in range(2):
                        for e, to in enumerate((Tm, TmT)):
                            dve.wait_ge(d_ready, 4 * (m - 1) + 2 * g + 2)
                            if m > 1:
                                dve.wait_ge(added, 4 * (m - 2) + 2 * g + e + 1)
                            nc.vector.tensor_tensor(to[:, 4 * g:4 * g + 4], to[:, 4 * g:4 * g + 4],
                                                    bank[2 + 2 * g + e][:].rearrange("p (h t) -> p h t", h=4), ALU.add
                                                    ).then_inc(added, 1)

            @block.scalar
            def _(act):
                for m in range(1, LEVELS):
                    for g in range(2):
                        act.wait_ge(g_ready, 2 * (m - 1) + g + 1)
                        if m > 1:
                            act.wait_ge(d_ready, 4 * (m - 2) + 2 * g + 2)
                        nc.scalar.activation(G[:, 4 * g:4 * g + 4], bank[g][:].rearrange("p (h t) -> p h t", h=4),
                                             ACT.Copy).then_inc(g_kept, 1)
        zw_ready, zw_kept = st.sem("zw_ready"), st.sem("zw_kept")
        with st.block() as block:
            @block.tensor
            def _(pe):
                for g in range(2):
                    for h in range(4 * g, 4 * g + 4):
                        mm = nc.tensor.matmul(bank[g][:, h % 4 * P:(h % 4 + 1) * P], TmT[:, h], QA[:, h], start=True,
                                              stop=True)
                    mm.then_inc(zw_ready, 1)
                for h in range(8):
                    part, c, cols = head(h)
                    mm = nc.tensor.matmul(bank[2][part, c * P:(c + 1) * P], toks["A"][:, t, cols],
                                          TmT[:, h], start=True, stop=True)
                mm.then_inc(zw_ready, 1)

            @block.scalar
            def _(act):
                for g in range(2):
                    act.wait_ge(zw_ready, g + 1)
                    nc.scalar.activation(ZW[:, t, 4 * g:4 * g + 4], bank[g][:].rearrange("p (h t) -> p h t", h=4), ACT.Copy
                                         ).then_inc(zw_kept, 1)
                act.wait_ge(zw_ready, 3)
                nc.scalar.activation(WT[:, t], bank[2][:].rearrange("p (c t) -> p c t", c=4), ACT.Copy).then_inc(zw_kept, 1)


def rwkv_chain(nc, bank, const, toks, ZW, r_end, S):
    n = T // CH
    with Stage(nc, "chain") as st:
        H = st.sb("H", [P, 2, 4, CH])
        new = st.sb("new", [P, 2, 4, CH])
        old = st.sb("old", [P, 4, CH])
        parts_ready, h_kept, new_kept, s_sum, scaled, s_ready = (st.sem(n) for n in (
            "parts_ready", "h_kept", "new_kept", "s_sum", "scaled", "s_ready"))
        tiles = lambda b, at: b[:, at:at + 4 * CH].rearrange("p (c k) -> p c k", c=4)
        with st.block() as block:
            @block.tensor
            def _(pe):
                def parts(ch):
                    rows, t = slice(ch % 2 * CH, (ch % 2 + 1) * CH), ch // 2
                    if ch >= 2:
                        pe.wait_ge(new_kept, ch - 1)
                    for o in range(8):
                        part, c, cols = head(o)
                        nc.tensor.matmul(bank[ch % 2][part, c * CH:(c + 1) * CH], ZW[rows, t, o, CH:2 * CH],
                                         toks["B"][rows, t, cols], start=True, stop=True)
                        to = bank[ch % 2][part, (4 + c) * CH:(5 + c) * CH]
                        nc.tensor.matmul(to, toks["B"][rows, t, cols], ZW[rows, t, o, 0:CH], start=True, stop=False)
                        mm = nc.tensor.matmul(to, toks["K"][rows, t, cols], toks["V"][rows, t, cols], start=False, stop=True)
                    mm.then_inc(parts_ready, 1)

                parts(0)
                for ch in range(n):
                    if ch + 1 < n:
                        parts(ch + 1)
                    pe.wait_ge(h_kept, ch + 1)
                    pe.wait_ge(s_ready, ch + 1)
                    for o in range(8):
                        part, c, _ = head(o)
                        mm = nc.tensor.matmul(bank[2 + ch % 2][part, c * CH:(c + 1) * CH], H[part, ch % 2, c],
                                              S[part, ch, c], start=True, stop=True)
                    mm.then_inc(s_sum, 1)

            @block.vector
            def _(dve):
                def keep(ch):
                    dve.wait_ge(parts_ready, ch + 1)
                    if ch >= 2:
                        dve.wait_ge(s_sum, ch - 1)
                        dve.wait_ge(s_ready, ch)
                    nc.vector.tensor_tensor(H[:, ch % 2], tiles(bank[ch % 2], 0),
                                            const.whole("eye2").unsqueeze(1).broadcast_to([P, 4, CH]), ALU.add
                                            ).then_inc(h_kept, 1)
                    nc.vector.tensor_tensor(new[:, ch % 2], tiles(bank[ch % 2], 4 * CH),
                                            r_end[:, :, ch:ch + 1].broadcast_to([P, 4, CH]), ALU.mult).then_inc(new_kept, 1)

                nc.vector.memset(S[:, 0], 0.0).then_inc(s_ready, 1)
                keep(0)
                for ch in range(n):
                    if ch + 1 < n:
                        keep(ch + 1)
                    dve.wait_ge(s_sum, ch + 1)
                    if ch:
                        dve.wait_ge(s_ready, ch + 1)
                    nc.vector.tensor_tensor(old[:], tiles(bank[2 + ch % 2], 0),
                                            r_end[:, :, ch:ch + 1].broadcast_to([P, 4, CH]), ALU.mult).then_inc(scaled, 1)
                    dve.wait_ge(scaled, ch + 1)
                    dve.wait_ge(new_kept, ch + 1)
                    nc.vector.tensor_tensor(S[:, ch + 1], old[:], new[:, ch % 2], ALU.add).then_inc(s_ready, 1)


def rwkv_output(nc, bank, const, t, R, B, Kt, toks, ZW, WT, S, y):
    here = slice(t * P, (t + 1) * P)
    with Stage(nc, f"rwout{t}") as st:
        RB, RK = st.sb("RB", [P, 8, P]), st.sb("RK", [P, 8, P])
        U = st.sb("U", [P, 8, CH])
        products, masked, u_sum, u_ready, y_ready, y_kept = (st.sem(n) for n in (
            "products", "masked", "u_sum", "u_ready", "y_ready", "y_kept"))
        with st.block() as block:
            @block.tensor
            def _(pe):
                for h in range(8):
                    part, c, cols = head(h)
                    for e in range(2):
                        mm = nc.tensor.matmul(bank[4 + h // 4][e * CH:(e + 1) * CH, c * CH:(c + 1) * CH],
                                              WT[part, t, c, e * CH:(e + 1) * CH], S[part, 2 * t + e, c], start=True,
                                              stop=True)
                mm.then_inc(u_sum, 1)
                for e, left in enumerate((B, Kt)):
                    for h in range(8):
                        part, c, cols = head(h)
                        mm = nc.tensor.matmul(bank[2 * e + h // 4][:, h % 4 * P:(h % 4 + 1) * P], left[part, c, here],
                                              R[part, c, here], start=True, stop=True)
                        if h % 4 == 3:
                            mm.then_inc(products, 1)
                pe.wait_ge(u_ready, 2)
                pe.wait_ge(masked, 4)
                for h in range(8):
                    part, c, cols = head(h)
                    nc.tensor.matmul(bank[6][part, c * P:(c + 1) * P], U[:, h], RB[:, h], start=True, stop=False)
                    nc.tensor.matmul(bank[6][part, c * P:(c + 1) * P], toks["V"][:, t, cols], RK[:, h],
                                     start=False, stop=False)
                    for e in range(2):
                        mm = nc.tensor.matmul(bank[6][part, c * P + e * CH:c * P + (e + 1) * CH], S[part, 2 * t + e, c],
                                              R[part, c, t * P + e * CH:t * P + (e + 1) * CH], start=False, stop=(e == 1))
                mm.then_inc(y_ready, 1)

            @block.vector
            def _(dve):
                dve.wait_ge(u_sum, 1)
                for e in range(2):
                    nc.vector.tensor_tensor(U[:, 4 * e:4 * e + 4],
                                            bank[4 + e][:, 0:4 * CH].rearrange("p (h v) -> p h v", h=4),
                                            ZW[:, t, 4 * e:4 * e + 4, 0:CH], ALU.add).then_inc(u_ready, 1)
                for n, to in enumerate((RB, RB, RK, RK)):
                    dve.wait_ge(products, n + 1)
                    g = n % 2
                    nc.vector.tensor_tensor(to[:, 4 * g:4 * g + 4], bank[n][:].rearrange("p (h t) -> p h t", h=4),
                                            over_heads(const.whole("incl")), ALU.mult).then_inc(masked, 1)

            @block.scalar
            def _(act):
                act.wait_ge(y_ready, 1)
                nc.scalar.activation(y[:, :, here], bank[6][:].rearrange("p (c t) -> p c t", c=4), ACT.Copy
                                     ).then_inc(y_kept, 1)


def rwkv_finish(nc, bank, cols, halves, y, bonus, gate, dump):
    with Stage(nc, "rwfin") as st:
        sq = st.sb("sq", [P, 4, T])
        mean, var, root, rstd = (st.sb(n, [P, T]) for n in ("mean", "var", "root", "rstd"))
        step_done, summed, centred, squared, var_ready, root_ready = (st.sem(n) for n in (
            "step_done", "summed", "centred", "squared", "var_ready", "root_ready"))
        with st.block() as block:
            @block.tensor
            def _(pe):
                for c in range(4):
                    nc.tensor.matmul(bank[c][:], halves, y[:, c], start=True, stop=True).then_inc(summed, 1)
                for c in range(4):
                    pe.wait_ge(squared, c + 1)
                    nc.tensor.matmul(bank[4 + c][:], halves, sq[:, c], start=True, stop=True).then_inc(summed, 1)

            @block.scalar
            def _(act):
                for c in range(4):
                    act.wait_ge(centred, c + 1)
                    nc.scalar.activation(sq[:, c], y[:, c], ACT.Square).then_inc(squared, 1)
                for c in range(4):
                    act.wait_ge(var_ready, c + 1)
                    nc.scalar.activation(root[:], var[:], ACT.Sqrt).then_inc(root_ready, 1)

            @block.vector
            def _(dve):
                do = Chain(dve, step_done)
                for c in range(4):
                    dve.wait_ge(summed, c + 1)
                    do(nc.vector.tensor_scalar(mean[:], bank[c][:], 1.0 / HD, None, ALU.mult))
                    nc.vector.tensor_tensor(y[:, c], y[:, c], mean[:], ALU.subtract).then_inc(centred, 1)
                    dve.wait_ge(centred, c + 1)
                for c in range(4):
                    dve.wait_ge(summed, 4 + c + 1)
                    if c:
                        dve.wait_ge(root_ready, c)
                    nc.vector.tensor_scalar(var[:], bank[4 + c][:], 1.0 / HD, LNX_EPS, ALU.mult, ALU.add
                                            ).then_inc(var_ready, 1)
                    dve.wait_ge(root_ready, c + 1)
                    do(nc.vector.reciprocal(rstd[:], root[:]))
                    do(nc.vector.scalar_tensor_tensor(y[:, c], y[:, c], cols("lnx_g", c), rstd[:], ALU.mult, ALU.mult))
                    do(nc.vector.scalar_tensor_tensor(y[:, c], y[:, c], cols("lnx_b", c), bonus[:, c], ALU.add, ALU.add))
                    do(nc.vector.tensor_tensor(y[:, c], y[:, c], gate[:, c], ALU.mult))
    dump("ya", y)


def merge_second(nc, w, bank, hT, yT, mergedT):
    u0 = first_unit("merge")

    def adds(n):
        return 2 * (n - (n + 2) // 3)

    with Stage(nc, "merge2") as st:
        gate = st.sb("gate", [P, 2, 2, T])
        part = st.sb("part", [P, 2, 2, T])
        sig_ready, parts, merged, proj_ready = st.sem("sig_ready"), st.sem("parts"), st.sem("merged"), st.sem("proj_ready")
        with st.block() as block:
            @block.sync
            def _(sp):
                w.load(sp, first_unit("wout2") + RING)

            @block.tensor
            def _(pe):
                for n in range(12):
                    b = 4 * (n % 2)
                    if n >= 2:
                        pe.wait_ge(parts, 2 * (n - 1))
                    ring = w.wait(pe, u0 + 3 * n)
                    for e in range(2):
                        for k in range(4):
                            mm = nc.tensor.matmul(bank[b + e][:], ring[:, 4 * e + k], yT[n % 3][:, k], start=(k == 0),
                                                  stop=(k == 3))
                    mm.then_inc(w.done, 1)
                    for e in range(2):
                        ring = w.wait(pe, u0 + 3 * n + 1 + e)
                        for k in range(DT):
                            mm = nc.tensor.matmul(bank[b + 2 + e][:], ring[:, k], hT[:, k], start=(k == 0),
                                                  stop=(k == DT - 1))
                        mm.then_inc(w.done, 1)

            @block.scalar
            def _(act):
                for n in range(12):
                    for e in range(2):
                        act.wait_ge(w.done, u0 + 3 * n + 2 + e)
                        if n >= 2:
                            act.wait_ge(parts, 2 * (n - 1))
                        nc.scalar.activation(gate[:, n % 2, e], bank[4 * (n % 2) + 2 + e][:], ACT.Sigmoid
                                             ).then_inc(sig_ready, 1)

            @block.vector
            def _(dve):
                for n in range(12):
                    f = n // 3 * 2
                    for e in range(2):
                        dve.wait_ge(sig_ready, 2 * n + e + 1)
                        to = mergedT[:, f + e] if n % 3 == 0 else part[:, n % 2, e]
                        if adds(n - 1) > 0:
                            dve.wait_ge(merged, adds(n - 1))
                        nc.vector.tensor_tensor(to, bank[4 * (n % 2) + e][:], gate[:, n % 2, e], ALU.mult
                                                ).then_inc(parts, 1)
                        if n % 3:
                            dve.wait_ge(parts, 2 * n + e + 1)
                            if n % 3 == 2:
                                dve.wait_ge(merged, adds(n))
                            nc.vector.tensor_tensor(mergedT[:, f + e], mergedT[:, f + e], part[:, n % 2, e], ALU.add
                                                    ).then_inc(merged, 1)


def program(nc, a, out, dump_to=None):
    dumped = []
    with ExitStack() as ctx:
        bank = [ctx.enter_context(nc.psum_tensor(f"bank{i}", [P, 512], F32)) for i in range(8)]
        w = Weights(nc, ctx, a["weights"])
        x = ctx.enter_context(nc.sbuf_tensor("x", [P, TT, D], F32))

        def dump(name, tensor):
            if dump_to is None or name not in dump_to:
                return
            with Stage(nc, f"dump_{name}") as st, st.block() as block:
                s = st.sem("s")

                @block.sync
                def _(sp):
                    sp.dma_start(dump_to[name], tensor[:]).then_inc(s, 16)
                    sp.wait_ge(s, 16)

        def load(name, pairs):
            with Stage(nc, name) as st, st.block() as block:
                s = st.sem("arrived")

                @block.sync
                def _(sp):
                    for to, of in pairs:
                        sp.dma_start(to, of).then_inc(s, 16)
                    sp.wait_ge(s, 16 * len(pairs))

        with ExitStack() as one:
            cols_sb = one.enter_context(nc.sbuf_tensor("cols1", [P, sum(COLS1.values())], F32))
            const_sb = one.enter_context(nc.sbuf_tensor("const1", [P, sum(CONST1.values())], F32))
            rows = one.enter_context(nc.sbuf_tensor("rows1", [P, 2 * D], F32))
            subkeys = one.enter_context(nc.sbuf_tensor("subkeys", [P, 2, NKEYS], F32))
            load("first", [(x[:], a["x"].rearrange("(t p) d -> p t d", p=P)), (cols_sb[:], a["cols1"]),
                           (const_sb[:], a["const1"]), (rows[:], a["rows1"]), (subkeys[:], a["subkeys"])])
            first_block(nc, w, bank, Columns(cols_sb, COLS1), Columns(const_sb, CONST1), rows, subkeys,
                        a["peer_u"], a["peer_v"], x, dump)
        if dump_to is None or "final" in dump_to or True:
            second_block(nc, ctx, w, bank, a, x, out, dump, load)


def constants():
    p, c = np.arange(P)[:, None], np.arange(P)[None, :]
    ident = np.eye(P)
    r, s3 = np.arange(P)[:, None], np.arange(3 * P)[None, :]
    dist = np.abs(r + P - s3).astype(np.float64)
    dist[dist > P] = FAR
    iota = np.broadcast_to(np.tile(np.arange(TOPK), TOPK), (P, TOPK * TOPK))
    const1 = np.concatenate([ident, np.ones((P, P)), dist, iota], 1).astype(np.float32)
    halves = (p // 64 == c // 64)
    swap = np.zeros((P, P))
    for o in range(P):
        if o % 64 < 32:
            swap[o + 32, o] = -1
        else:
            swap[o - 32, o] = 1
    s2 = np.arange(2 * P)[None, :]
    rel = r - s2 + P
    band = np.where((rel >= 0) & (rel < P), 0.0, -1e31)
    same = p // CH == c // CH
    strict, incl = same & (p < c), same & (p <= c)
    levels = [(p // (2 * m) == c // (2 * m)) & (p % (2 * m) < m) & (c % (2 * m) >= m) for m in (1, 2, 4, 8, 16, 32)]
    eye2 = np.concatenate([np.eye(CH), np.eye(CH)], 0)
    const2 = np.concatenate([ident, np.ones((P, P)), halves, swap, band, strict, incl, *levels, eye2], 1).astype(np.float32)
    inv = (10000.0 ** (-np.arange(32) / 32)).astype(np.float32)
    return const1, const2, np.tile(inv, 4)[:, None]


def unit_columns(mat, cols):
    m = mat[:, cols] if cols is not None else mat
    k, n = m.shape[0] // P, m.shape[1] // P
    return m.reshape(k, P, n, P).transpose(2, 1, 0, 3)


def lay_out(i):
    i = {k: np.asarray(v) for k, v in i.items()}
    col = lambda v: v.reshape(-1, P).T
    rep = lambda v: np.broadcast_to(v.reshape(1, -1), (P, v.size))
    full = lambda u: u.reshape(u.shape[0], P, DT * P)
    order1 = np.concatenate([np.arange(HD) + HD * h for pair in HEADS1 for h in pair])
    order2 = np.concatenate([np.arange(HD) + HD * h for pair in HEADS2 for h in pair])

    w_in = i["w_in"][0]
    z1 = []
    for t in range(DT):
        z1 += [np.arange(P) + D + t * P, np.arange(P) + t * P]
    z1 = np.concatenate(z1 + [2 * D + order1, np.arange(3 * D, 3 * D + 512), np.arange(3 * D + 512, 5 * D + 512)])
    co = np.stack([unit_columns(i["conv_w_pw"][0], None), unit_columns(i["attn_w_o"][0][order1], None)], 1)
    w2 = i["w_in_2"][0]
    at = np.cumsum([0, 512, 512, 512, 64, 64, 512, 512, 128, 128, 512, 512, 512, 3072])
    rng = lambda a, b: np.arange(at[a], at[b])
    rwkv = rng(0, 6)
    sw = np.concatenate([at[6] + order2, rng(7, 9), at[9] + order2])
    xq = rng(10, 12)
    proj = [i["w_proj_a_2"][0], i["w_proj_b_2"][0][order2], i["w_proj_c_2"][0]]
    merge = []
    gates = [unit_columns(w2, at[12] + D * b + np.arange(D)) for b in range(3)]
    proj = [unit_columns(m, None) for m in proj]
    for f in range(0, DT, 2):
        for b in range(3):
            merge.append(np.concatenate([proj[b][f], proj[b][f + 1]], 1)[None])
            merge += [gates[b][f:f + 1], gates[b][f + 1:f + 2]]
    rows_of = lambda m: m.reshape(DT, P, D)
    weights = np.concatenate([
        full(unit_columns(w_in, z1)), full(co.reshape(16, P, DT, P)), rows_of(i["w_out"][0]),
        full(unit_columns(i["peer_w_query"][0], None)), full(unit_columns(w2, rwkv)), full(unit_columns(w2, sw)),
        full(unit_columns(i["w_mem_kv_2"][0], None)), full(unit_columns(w2, xq)),
        *[full(m) for m in merge], rows_of(i["w_out_2"][0])], 0)
    const1, const2, inv = constants()
    two = lambda v: np.concatenate([v, v])[:, None]
    cols1 = np.concatenate([col(i["norm1_g"][0]), col(i["conv_dw_w"][0]), col(i["conv_dw_b"][0]),
                            col(i["conv_ln_g"][0]), col(i["conv_ln_b"][0]), rep(i["attn_sink"][0])], 1)
    cols2 = np.concatenate([
        col(i["norm_g_2"][0]), col(i["mem_norm_g_2"][0]), col(i["mu_rkv_2"][0]), i["mu_wa_2"][0].reshape(P, 1),
        col(i["a0_2"][0]), col(i["k_k_2"][0]), col(i["k_a_2"][0]), col(i["r_k_2"][0]), col(i["lnx_g_2"][0]),
        col(i["lnx_b_2"][0]), two(i["q_norm_g_2"][0]), two(i["k_norm_g_2"][0]), i["xq_norm_g_2"][0][:, None],
        i["xk_norm_g_2"][0][:, None], inv, rep(i["sinks_2"][0])], 1)
    a = dict(x=i["x"][0], weights=weights.reshape(-1, P, DT * P), cols1=cols1, cols2=cols2, const1=const1, const2=const2,
             rows1=np.concatenate([rep(i["norm2_g"][0]), rep(i["final_g"])], 1), rows2=rep(i["w0_2"][0]),
             subkeys=i["peer_sub_keys"][0].transpose(2, 0, 1), peer_u=i["peer_u"][0], peer_v=i["peer_v"][0],
             mem=i["mem_2"][0], lora=np.concatenate([i["w2_2"][0], i["a2_2"][0]], 0),
             positions=np.broadcast_to(i["positions_2"].reshape(1, T), (P, T)))
    return {k: np.ascontiguousarray(v) for k, v in a.items()}


def kernel(**inputs):
    import concourse.bacc as bacc
    from concourse.bass_utils import run_bass_kernel_spmd

    arrays = lay_out(inputs)
    nc = bacc.Bacc("TRN2", target_bir_lowering=False, num_devices=1)
    a = {k: nc.dram_tensor(f"in_{k}", v.shape, mybir.dt.from_np(v.dtype), kind="ExternalInput").ap()
         for k, v in arrays.items()}
    out = nc.dram_tensor("out", (T, D), F32, kind="ExternalOutput").ap()
    program(nc, a, out)
    r = run_bass_kernel_spmd(nc, [{f"in_{k}": v for k, v in arrays.items()}], core_ids=[0])
    return r.results[0]["out"].reshape(1, T, D)
```

```python
from contextlib import ExitStack, contextmanager

import numpy as np

import concourse.bass as bass
from concourse import mybir

F32 = mybir.dt.float32
U32 = mybir.dt.uint32
I32 = mybir.dt.int32
ALU = mybir.AluOpType
ACT = mybir.ActivationFunctionType
AXX = mybir.AxisListType.X

P = 128
T = 512
TT = T // P
D = 1024
DT = D // P
TAPS = 31
PAD = TAPS // 2
EPS = 1e-6
RING = 4

H1, KV1, HD = 16, 4, 64
SLOPES = [2.0 ** (-8.0 * (h + 1) / H1) for h in range(H1)]
FAR = 1e33
PH, TOPK, NKEYS = 8, 16, 128
PICKS = PH * TOPK

MEM = 256
LNX_EPS = 64e-5
DECAY = float(np.exp(-0.5))
CH = 64
LEVELS = 6

HEADS1 = [[4 * (2 * (i // 4) + e) + i % 4 for e in range(2)] for i in range(8)]
HEADS2 = [[i, 4 + i] for i in range(4)]

COLS1 = dict(norm1=8, conv_w=TAPS * 8, conv_b=8, ln_g=8, ln_b=8, sink=16)
COLS2 = dict(norm=8, memnorm=8, mu=13, a0=4, k_k=4, k_a=4, r_k=4, lnx_g=4, lnx_b=4, q_g=1, k_g=1,
             xq_g=1, xk_g=1, inv=1, sinks=8)
CONST1 = dict(ident=P, ones=P, dist=3 * P, iota=TOPK * TOPK)
CONST2 = dict(ident=P, ones=P, halves=P, swap=P, band=2 * P, strict=P, incl=P, level=LEVELS * P, eye2=CH)

FILL1, FILL2 = 24, 42
FILL2_BEFORE_MEM = 36
UNITS = [("z1", 28), ("fill1", FILL1), ("wo", 8), ("wout1", 8), ("query", 16), ("rwkv", 17), ("fill2", FILL2_BEFORE_MEM),
         ("mem", 8), ("fill2_rest", FILL2 - FILL2_BEFORE_MEM), ("merge", 12), ("wout2", 8)]


def first_unit(name):
    at = 0
    for n, count in UNITS:
        if n == name:
            return at
        at += count
    return at


def offsets(widths):
    at, out = 0, {}
    for name, w in widths.items():
        out[name] = (at, at + w)
        at += w
    return out, at


class Columns:

    def __init__(self, tensor, widths):
        self.tensor, (self.at, self.width) = tensor, offsets(widths)

    def __call__(self, name, i=0, n=1):
        a = self.at[name][0] + i
        return self.tensor[:, a:a + n]

    def whole(self, name):
        a, b = self.at[name]
        return self.tensor[:, a:b]


class Chain:

    def __init__(self, eng, sem):
        self.eng, self.sem, self.count = eng, sem, 0

    def __call__(self, ins):
        self.count += 1
        ins.then_inc(self.sem, 1)
        self.eng.wait_ge(self.sem, self.count)


class Weights:

    def __init__(self, nc, ctx, dram):
        self.dram = dram
        self.ring = ctx.enter_context(nc.sbuf_tensor("weight_ring", [P, RING, DT, P], F32))
        self.arrived = [ctx.enter_context(nc.semaphore(f"weights_arrived{s}")) for s in range(RING)]
        self.done = ctx.enter_context(nc.semaphore("unit_done"))
        self.issued = 0

    def load(self, sp, upto):
        def one(u, i, j):
            slot = (u + j) % RING
            if u + j >= RING:
                sp.wait_ge(self.done, RING * i + (u + j - RING + 1))
            sp.dma_start(self.ring[:, slot], self.dram[u + j + RING * i]).then_inc(self.arrived[slot], 16)

        upto = max(upto, self.issued)
        u, n = self.issued, upto - self.issued
        while u < RING and n > 0:
            one(u, 0, 0)
            u, n = u + 1, n - 1
        if n >= 2 * RING:
            with sp.Fori(0, n // RING) as i:
                for j in range(RING):
                    one(u, i, j)
            u, n = u + n // RING * RING, n % RING
        for j in range(n):
            one(u, 0, j)
        self.issued = upto

    def wait(self, pe, u, i=0):
        pe.wait_ge(self.arrived[u % RING], 16 * i + 16 * (u // RING + 1))
        return self.ring[:, u % RING]


class Filler:

    def __init__(self, nc, st, w, banks, unit, items, store=None):
        self.nc, self.w, self.banks, self.unit, self.items, self.store = nc, w, banks, unit, items, store
        self.kept = st.sem("kept")
        if store is not None:
            self.stored = [st.sem(f"stored{i}") for i in range(2)]
            self.stage = st.sb("stage", [P, 2, T])
        self.step = self.taken = self.sent = 0
        self.limit = len(items)
        self.marks = []

    @property
    def done(self):
        return self.step // DT

    def pe(self, pe, steps):
        for _ in range(min(steps, DT * self.limit - self.step)):
            n, k = divmod(self.step, DT)
            src = self.items[n][0]
            if k == 0:
                self.ring = self.w.wait(pe, self.unit(n))
                if n >= len(self.banks):
                    pe.wait_ge(self.kept, n - len(self.banks) + 1)
            mm = self.nc.tensor.matmul(self.banks[n % len(self.banks)][:], self.ring[:, k], src[:, k], start=(k == 0), stop=(k == DT - 1))
            if k == DT - 1:
                mm.then_inc(self.w.done, 1)
            self.step += 1

    def mark(self):
        self.marks.append(self.done)

    def act(self, act, upto=None):
        upto = self.done if upto is None else upto
        while self.taken < upto:
            n = self.taken
            _, func, scale, to = self.items[n]
            act.wait_ge(self.w.done, self.unit(n) + 1)
            if to is None:
                if n >= 2:
                    act.wait_ge(self.stored[n % 2], 16 * (n // 2))
                to = self.stage[:, n % 2]
            self.nc.scalar.activation(to, self.banks[n % len(self.banks)][:], func, scale=scale).then_inc(self.kept, 1)
            self.taken += 1

    def sp(self, sp):
        while self.sent < self.done:
            n = self.sent
            self.w.load(sp, min(self.unit(n) + RING, sum(c for _, c in UNITS)))
            if self.store is not None:
                sp.wait_ge(self.kept, n + 1)
                sp.dma_start(self.store[n], self.stage[:, n % 2]).then_inc(self.stored[n % 2], 16)
            self.sent += 1
        self.marks = []

    def wait_stored(self, sp):
        for i in range(2):
            sp.wait_ge(self.stored[i], 16 * ((self.sent + 1 - i) // 2))


def catch_up(nc, fill):
    with nc.Block() as block:
        @block.tensor
        def _(pe):
            fill.pe(pe, DT * FILL2)

        @block.scalar
        def _(act):
            fill.act(act)

        @block.sync
        def _(sp):
            fill.sp(sp)
            fill.wait_stored(sp)


def rounds(eng, n, body):
    body(0, True)
    if n > 1:
        with eng.Fori(1, n) as i:
            body(i, False)


class Stage:

    owner, free = None, []

    def __init__(self, nc, name):
        self.nc, self.name, self.ctx, self.sems = nc, name, ExitStack(), []
        if Stage.owner is not nc:
            Stage.owner, Stage.free = nc, list(nc.free_semaphores)

    def __enter__(self):
        self.ctx.__enter__()
        return self

    def __exit__(self, *e):
        if self.sems:
            numbers = [s.num for s in self.sems]
            self.nc.clear_and_free_semaphores(self.sems)
            Stage.free += numbers
        return self.ctx.__exit__(*e)

    def sb(self, name, shape, dt=F32):
        return self.ctx.enter_context(self.nc.sbuf_tensor(f"{self.name}_{name}", shape, dt))

    def sem(self, name):
        self.sems.append(self.nc.alloc_semaphore(name=f"{self.name}_{name}", num=Stage.free.pop(0)))
        return self.sems[-1]

    def block(self):
        return self.nc.Block()


def norm_to_T(nc, w, bank, name, x, tiles, gain, ident, xT, prefetch, scaled=None, row_gain=None):
    with Stage(nc, name) as st:
        junk = st.sb("junk", [P, D])
        ss = st.sb("ss", [P, tiles])
        ms = st.sb("ms", [P, tiles])
        rms = st.sb("rms", [P, tiles])
        rstd = st.sb("rstd", [P, tiles])
        xn = scaled if scaled is not None else st.sb("xn", [P, tiles, D])
        squared, mean_ready, root_ready = st.sem("squared"), st.sem("mean_ready"), st.sem("root_ready")
        rstd_ready, normed, turned, kept = st.sem("rstd_ready"), st.sem("normed"), st.sem("turned"), st.sem("kept")
        with st.block() as block:
            @block.sync
            def _(sp):
                w.load(sp, prefetch)

            @block.scalar
            def _(act):
                for t in range(tiles):
                    if t:
                        act.wait_ge(squared, t)
                    nc.scalar.activation(junk[:], x[:, t], ACT.Square, accum_out=ss[:, t:t + 1]).then_inc(squared, 1)
                act.wait_ge(mean_ready, 1)
                nc.scalar.activation(rms[:], ms[:], ACT.Sqrt).then_inc(root_ready, 1)
                for f in range(DT):
                    act.wait_ge(turned, f + 1)
                    scale = 1.0 if gain is None else gain[:, f:f + 1]
                    nc.scalar.activation(xT[:, f], bank[f][:, 0:tiles * P], ACT.Copy, scale=scale).then_inc(kept, 1)

            @block.vector
            def _(dve):
                dve.wait_ge(squared, tiles)
                nc.vector.tensor_scalar(ms[:], ss[:], 1.0 / D, EPS, ALU.mult, ALU.add).then_inc(mean_ready, 1)
                dve.wait_ge(root_ready, 1)
                nc.vector.reciprocal(rstd[:], rms[:]).then_inc(rstd_ready, 1)
                dve.wait_ge(rstd_ready, 1)
                for t in range(tiles):
                    if row_gain is None:
                        nc.vector.tensor_scalar(xn[:, t], x[:, t], rstd[:, t:t + 1], None, ALU.mult).then_inc(normed, 1)
                    else:
                        nc.vector.scalar_tensor_tensor(xn[:, t], x[:, t], rstd[:, t:t + 1], row_gain, ALU.mult,
                                                       ALU.mult).then_inc(normed, 1)

            @block.tensor
            def _(pe):
                if xT is None:
                    return
                pe.wait_ge(normed, tiles)
                for f in range(DT):
                    for t in range(tiles):
                        mm = nc.tensor.transpose(bank[f][:, t * P:(t + 1) * P], xn[:, t, f * P:(f + 1) * P], ident)
                    mm.then_inc(turned, 1)


def attention(nc, w, bank, name, units, prefetch, *, scale, sink, ident, out, group, dim,
              fill=None, fill_steps=0):
    B = 3
    n = len(units)
    width = max(u["k"].shape[-1] for u in units)
    per = P // dim
    with Stage(nc, name) as st:
        logit = st.sb("logit", [P, B, width])
        prob = st.sb("prob", [P, B, width])
        probT = st.sb("probT", [P, 2, width])
        diag = st.sb("diag", [P, B, P])
        top = st.sb("top", [P, B])
        negtop = st.sb("negtop", [P, B])
        total = st.sb("total", [P, B])
        sinkexp = st.sb("sinkexp", [P, B])
        full = st.sb("full", [P, B])
        recip = st.sb("recip", [P, B])
        scores_ready, biased, top_ready = st.sem("scores_ready"), st.sem("biased"), st.sem("top_ready")
        negtop_ready, exp_ready, full_ready = st.sem("negtop_ready"), st.sem("exp_ready"), st.sem("full_ready")
        recip_ready, diag_ready, turned = st.sem("recip_ready"), st.sem("diag_ready"), st.sem("turned")
        turned_kept, out_ready, out_kept = st.sem("turned_kept"), st.sem("out_ready"), st.sem("out_kept")
        has_bias, has_sink = units[0]["bias"] is not None, sink is not None
        with st.block() as block:
            @block.tensor
            def _(pe):
                def scores(i):
                    if i >= 2:
                        pe.wait_ge(biased if has_bias else exp_ready, i - 1)
                        if not has_bias:
                            pe.wait_ge(top_ready, i - 1)
                    u = units[i]
                    nc.tensor.matmul(bank[i % 2][:, 0:u["k"].shape[-1]], u["q"], u["k"], start=True,
                                     stop=True).then_inc(scores_ready, 1)

                def turn(i):
                    pe.wait_ge(exp_ready, i + 1)
                    pe.wait_ge(diag_ready, i + 1)
                    if i >= 2:
                        pe.wait_ge(turned_kept, i - 1)
                    for c in range(len(units[i]["v"])):
                        mm = nc.tensor.matmul(bank[2 + i % 2][:, c * P:(c + 1) * P], prob[:, i % B, c * P:(c + 1) * P],
                                              diag[:, i % B], start=True, stop=True)
                    mm.then_inc(turned, 1)

                def values(i):
                    u, g = units[i], i // group
                    pe.wait_ge(turned_kept, i + 1)
                    if g >= 2:
                        pe.wait_ge(out_kept, g - 1)
                    at = u["half"] * dim
                    col = (i % group) // per * P
                    for c, v in enumerate(u["v"]):
                        mm = nc.tensor.matmul(bank[4 + g % 2][at:at + dim, col:col + P], v,
                                              probT[:, i % 2, c * P:(c + 1) * P], start=(c == 0),
                                              stop=(c == len(u["v"]) - 1))
                    mm.then_inc(out_ready, 1)

                for i in range(n + 3):
                    if i < n:
                        scores(i)
                    if 2 <= i < n + 2:
                        turn(i - 2)
                    if i >= 3:
                        values(i - 3)
                    if fill is not None:
                        fill.pe(pe, fill_steps)
                        fill.mark()

            @block.vector
            def _(dve):
                def maximum(i):
                    u, b = units[i], i % B
                    k = u["k"].shape[-1]
                    dve.wait_ge(scores_ready, i + 1)
                    if i >= B:
                        dve.wait_ge(exp_ready, i - B + 1)
                    src = bank[i % 2][:, 0:k]
                    if has_bias:
                        tile, coef = u["bias"]
                        nc.vector.scalar_tensor_tensor(logit[:, b, 0:k], tile, coef, src, ALU.mult,
                                                       ALU.add).then_inc(biased, 1)
                        dve.wait_ge(biased, i + 1)
                        src = logit[:, b, 0:k]
                    nc.vector.tensor_reduce(top[:, b:b + 1], src, AXX, ALU.max).then_inc(top_ready, 1)
                    dve.wait_ge(top_ready, i + 1)
                    if has_sink:
                        nc.vector.tensor_scalar(negtop[:, b:b + 1], top[:, b:b + 1], u["sink_scaled"], -scale, ALU.max,
                                                ALU.mult).then_inc(negtop_ready, 1)
                    else:
                        nc.vector.tensor_scalar(negtop[:, b:b + 1], top[:, b:b + 1], -scale, None,
                                                ALU.mult).then_inc(negtop_ready, 1)

                def divisor(i):
                    b = i % B
                    dve.wait_ge(exp_ready, i + 1)
                    src = total[:, b:b + 1]
                    if has_sink:
                        nc.vector.tensor_tensor(full[:, b:b + 1], src, sinkexp[:, b:b + 1], ALU.add).then_inc(full_ready, 1)
                        dve.wait_ge(full_ready, i + 1)
                        src = full[:, b:b + 1]
                    nc.vector.reciprocal(recip[:, b:b + 1], src).then_inc(recip_ready, 1)
                    dve.wait_ge(recip_ready, i + 1)
                    if i >= B:
                        dve.wait_ge(turned, i - B + 1)
                    nc.vector.tensor_scalar(diag[:, b], ident, recip[:, b:b + 1], None, ALU.mult).then_inc(diag_ready, 1)

                def keep(g):
                    dve.wait_ge(out_ready, group * (g + 1))
                    nc.vector.tensor_copy(out(g), bank[4 + g % 2][:].rearrange("p (a t) -> p a t", t=P)[:, 0:group // per]
                                          ).then_inc(out_kept, 1)

                for i in range(n + 4):
                    if i < n:
                        maximum(i)
                    if 1 <= i <= n:
                        divisor(i - 1)
                    if i >= 4 and (i - 4) % group == group - 1:
                        keep((i - 4) // group)

            @block.scalar
            def _(act):
                def exps(i):
                    u, b = units[i], i % B
                    k = u["k"].shape[-1]
                    act.wait_ge(negtop_ready, i + 1)
                    if i >= B:
                        act.wait_ge(turned, i - B + 1)
                        act.wait_ge(recip_ready, i - B + 1)
                    if has_sink:
                        nc.scalar.activation(sinkexp[:, b:b + 1], u["sink"], ACT.Exp, bias=negtop[:, b:b + 1])
                    nc.scalar.activation(prob[:, b, 0:k], logit[:, b, 0:k] if has_bias else bank[i % 2][:, 0:k], ACT.Exp,
                                         bias=negtop[:, b:b + 1], scale=scale,
                                         accum_out=total[:, b:b + 1]).then_inc(exp_ready, 1)

                def keep(i):
                    k = units[i]["k"].shape[-1]
                    act.wait_ge(turned, i + 1)
                    if i >= 2:
                        act.wait_ge(out_ready, i - 1)
                    nc.scalar.activation(probT[:, i % 2, 0:k], bank[2 + i % 2][:, 0:k], ACT.Copy).then_inc(turned_kept, 1)

                for i in range(n + 2):
                    if i < n:
                        exps(i)
                    if i >= 2:
                        keep(i - 2)
                    if fill is not None and i:
                        fill.act(act, fill.marks[i - 1])
                if fill is not None:
                    fill.act(act, fill.done)

            @block.sync
            def _(sp):
                if fill is None:
                    w.load(sp, prefetch)
                else:
                    fill.sp(sp)


def turn_tiles(nc, w, bank, name, pairs, ident, prefetch):
    with Stage(nc, name) as st:
        turned, kept = st.sem("turned"), st.sem("kept")
        with st.block() as block:
            @block.sync
            def _(sp):
                w.load(sp, prefetch)

            @block.tensor
            def _(pe):
                for n, (sources, _) in enumerate(pairs):
                    if n >= 6:
                        pe.wait_ge(kept, n - 5)
                    for j, s in enumerate(sources):
                        mm = nc.tensor.transpose(bank[n % 6][:, j * P:(j + 1) * P], s, ident)
                    mm.then_inc(turned, 1)

            @block.scalar
            def _(act):
                for n, (sources, to) in enumerate(pairs):
                    act.wait_ge(turned, n + 1)
                    if n:
                        act.wait_ge(kept, n)
                    src = bank[n % 6][:, 0:len(sources) * P]
                    if len(to.shape) == 3:
                        src = src.rearrange("p (a t) -> p a t", a=to.shape[1])
                    nc.scalar.activation(to, src, ACT.Copy).then_inc(kept, 1)


def first_block(nc, w, bank, cols, const, rows, subkeys, peer_u, peer_v, x, dump):
    ident, ones = const.whole("ident"), const.whole("ones")
    with ExitStack() as outer:
        attnT = outer.enter_context(nc.sbuf_tensor("attnT", [P, DT, T], F32))
        gateT = outer.enter_context(nc.sbuf_tensor("gateT", [P, 16, T], F32))
        convoutT = outer.enter_context(nc.sbuf_tensor("convoutT", [P, DT, T], F32))
        with ExitStack() as inner:
            convT = inner.enter_context(nc.sbuf_tensor("convT", [P, DT, T], F32))
            qkvT = inner.enter_context(nc.sbuf_tensor("qkvT", [P, 12, T], F32))
            hT = inner.enter_context(nc.sbuf_tensor("hT", [P, DT, T], F32))
            norm_to_T(nc, w, bank, "norm1", x, TT, cols.whole("norm1"), ident, hT, first_unit("z1") + RING)
            project_first(nc, w, bank, cols, hT, qkvT, convT)
            dump("conv", convT)
            dump("qkv", qkvT)
            conv_norm(nc, w, bank, cols, ones, convT)
            dump("convn", convT)
            v_tok = inner.enter_context(nc.sbuf_tensor("v_tok", [P, TT, KV1 * HD], F32))
            sink8 = inner.enter_context(nc.sbuf_tensor("sink8", [P, H1], F32))
            scale_sinks(nc, "sink1", sink8, cols.whole("sink"))
            turn_tiles(nc, w, bank, "turn_v",
                       [([qkvT[:, 10 + a, t * P:(t + 1) * P] for a in range(2)], v_tok[:, t]) for t in range(TT)],
                       ident, first_unit("fill1") + RING)
            units = []
            for b in range(TT):
                lo, hi = max(b - 1, 0), min(b + 2, TT)
                for i in range(8):
                    for e in range(2):
                        h = HEADS1[i][e]
                        a, part = i // 4, slice(e * HD, (e + 1) * HD)
                        kv = 2 * a + e
                        units.append(dict(
                            q=qkvT[part, i, b * P:(b + 1) * P], k=qkvT[part, 8 + a, lo * P:hi * P],
                            bias=(const.whole("dist")[:, (lo - b + 1) * P:(hi - b + 1) * P], -SLOPES[h] * HD ** 0.5),
                            v=[v_tok[:, c, kv * HD:(kv + 1) * HD] for c in range(lo, hi)],
                            sink=cols("sink", h), sink_scaled=sink8[:, h:h + 1], half=e))
            fill = Filler(nc, inner.enter_context(Stage(nc, "fill1")), w, bank[6:8], lambda n: first_unit("fill1") + n,
                          [(hT, ACT.Tanh, 0.5, gateT[:, n]) for n in range(16)]
                          + [(convT, ACT.Copy, 1.0, convoutT[:, n]) for n in range(DT)])
            attention(nc, w, bank, "attn1", units, 0, scale=HD ** -0.5, sink=True, ident=ident,
                      out=lambda g: attnT[:, 4 * (g % 2):4 * (g % 2) + 4, (g // 2) * P:(g // 2 + 1) * P],
                      group=8, dim=HD, fill=fill, fill_steps=3)
            assert fill.done == FILL1
        dump("attn", attnT)
        with nc.sbuf_tensor("mergedT", [P, DT, T], F32) as mergedT:
            merge_first(nc, w, bank, convoutT, attnT, gateT, mergedT)
            out_residual(nc, w, bank, "wout1", mergedT, x, first_unit("query") + RING, 0.5)
    dump("x1", x)
    with ExitStack() as inner:
        h2 = inner.enter_context(nc.sbuf_tensor("h2", [P, TT, D], F32))
        scores = inner.enter_context(nc.sbuf_tensor("scores", [P, TT, 2 * PH, NKEYS], F32))
        with nc.sbuf_tensor("h2T", [P, DT, T], F32) as h2T:
            norm_to_T(nc, w, bank, "norm2", x, TT, None, ident, h2T, first_unit("query") + RING, scaled=h2,
                      row_gain=rows[:, 0:D])
            query_scores(nc, w, bank, h2T, subkeys, scores)
        dump("scores", scores)
        experts(nc, w, bank, const, ident, scores, h2, peer_u, peer_v, x)
    dump("x2", x)
    final_norm(nc, w, x, rows[:, D:2 * D])
    dump("y", x)


def scale_sinks(nc, name, to, sink):
    with Stage(nc, name) as st, st.block() as block:
        @block.vector
        def _(dve):
            nc.vector.tensor_scalar(to[:], sink, float(HD ** 0.5), None, ALU.mult)


def project_first(nc, w, bank, cols, hT, qkvT, convT):
    with Stage(nc, "z1") as st:
        sig = st.sb("sig", [P, 2, T])
        u = st.sb("u", [P, DT, T + 2 * PAD])
        sig_ready, z_kept = st.sem("sig_ready"), st.sem("z_kept")
        u0 = first_unit("z1")
        u_zero, gated, tap_done = st.sem("u_zero"), st.sem("gated"), st.sem("tap_done")
        with st.block() as block:
            @block.sync
            def _(sp):
                w.load(sp, first_unit("fill1") + RING)

            @block.gpsimd
            def _(pool):
                nc.gpsimd.memset(u[:, :, 0:PAD], 0.0).then_inc(u_zero, 1)
                nc.gpsimd.memset(u[:, :, T + PAD:T + 2 * PAD], 0.0).then_inc(u_zero, 1)

            @block.tensor
            def _(pe):
                def four_tiles(i, taken):
                    for j in range(RING):
                        ring = w.wait(pe, u0 + j, i)
                        if taken is gated:
                            pe.wait_ge(gated, 2 * i + (j // 2 - 1))
                        elif taken is z_kept:
                            pe.wait_ge(z_kept, i * RING + (j - RING + 1 - 2 * DT))
                        for k in range(DT):
                            mm = nc.tensor.matmul(bank[j][:], ring[:, k], hT[:, k], start=(k == 0), stop=(k == DT - 1))
                        mm.then_inc(w.done, 1)
                four_tiles(0, None)
                with pe.Fori(1, 5) as i:
                    four_tiles(i, gated)
                for i in range(5, 28 // RING):
                    four_tiles(i, z_kept)

            @block.scalar
            def _(act):
                def conv_gates(i, first):
                    for j in range(2):
                        act.wait_ge(w.done, i * RING + (u0 + 2 * j + 1))
                        if not first:
                            act.wait_ge(gated, 2 * i + (j - 1))
                        nc.scalar.activation(sig[:, j], bank[2 * j][:], ACT.Sigmoid).then_inc(sig_ready, 1)
                rounds(act, 4, conv_gates)
                for n in range(16, 28):
                    act.wait_ge(w.done, u0 + n + 1)
                    nc.scalar.activation(qkvT[:, n - 16], bank[n % RING][:], ACT.Copy).then_inc(z_kept, 1)

            @block.vector
            def _(dve):
                dve.wait_ge(u_zero, 2)
                for c in range(DT):
                    j = c % 2
                    dve.wait_ge(w.done, u0 + 2 * c + 2)
                    dve.wait_ge(sig_ready, c + 1)
                    nc.vector.tensor_tensor(u[:, c, PAD:PAD + T], bank[2 * j + 1][:], sig[:, j], ALU.mult).then_inc(gated, 1)
                    dve.wait_ge(gated, c + 1)
                    nc.vector.tensor_scalar(convT[:, c], u[:, c, 0:T], cols("conv_w", c), cols("conv_b", c), ALU.mult,
                                            ALU.add).then_inc(tap_done, 1)
                    for k in range(1, TAPS):
                        dve.wait_ge(tap_done, TAPS * c + k)
                        nc.vector.scalar_tensor_tensor(convT[:, c], u[:, c, k:k + T], cols("conv_w", k * DT + c),
                                                       convT[:, c], ALU.mult, ALU.add).then_inc(tap_done, 1)


def conv_norm(nc, w, bank, cols, ones, convT):
    with Stage(nc, "convnorm") as st:
        mean = st.sb("mean", [P, T])
        sq = st.sb("sq", [P, DT, T])
        var = st.sb("var", [P, T])
        std = st.sb("std", [P, T])
        rstd = st.sb("rstd", [P, T])
        sum_ready, mean_ready, centred, squared = st.sem("sum_ready"), st.sem("mean_ready"), st.sem("centred"), st.sem("squared")
        var_ready, std_ready, rstd_ready, scaled, done = st.sem("var_ready"), st.sem("std_ready"), st.sem("rstd_ready"), st.sem("scaled"), st.sem("done")
        with st.block() as block:
            @block.tensor
            def _(pe):
                for c in range(DT):
                    mm = nc.tensor.matmul(bank[0][:], ones, convT[:, c], start=(c == 0), stop=(c == DT - 1))
                mm.then_inc(sum_ready, 1)
                for c in range(DT):
                    pe.wait_ge(squared, c + 1)
                    mm = nc.tensor.matmul(bank[1][:], ones, sq[:, c], start=(c == 0), stop=(c == DT - 1))
                mm.then_inc(sum_ready, 1)

            @block.vector
            def _(dve):
                dve.wait_ge(sum_ready, 1)
                nc.vector.tensor_scalar(mean[:], bank[0][:], 1.0 / D, None, ALU.mult).then_inc(mean_ready, 1)
                dve.wait_ge(mean_ready, 1)
                for c in range(DT):
                    nc.vector.tensor_tensor(convT[:, c], convT[:, c], mean[:], ALU.subtract).then_inc(centred, 1)
                dve.wait_ge(sum_ready, 2)
                nc.vector.tensor_scalar(var[:], bank[1][:], 1.0 / D, EPS, ALU.mult, ALU.add).then_inc(var_ready, 1)
                dve.wait_ge(std_ready, 1)
                nc.vector.reciprocal(rstd[:], std[:]).then_inc(rstd_ready, 1)
                dve.wait_ge(rstd_ready, 1)
                for c in range(DT):
                    nc.vector.tensor_tensor(convT[:, c], convT[:, c], rstd[:], ALU.mult).then_inc(scaled, 1)

            @block.scalar
            def _(act):
                for c in range(DT):
                    act.wait_ge(centred, c + 1)
                    nc.scalar.activation(sq[:, c], convT[:, c], ACT.Square).then_inc(squared, 1)
                act.wait_ge(var_ready, 1)
                nc.scalar.activation(std[:], var[:], ACT.Sqrt).then_inc(std_ready, 1)
                for c in range(DT):
                    act.wait_ge(scaled, c + 1)
                    nc.scalar.activation(convT[:, c], convT[:, c], ACT.Silu, bias=cols("ln_b", c),
                                         scale=cols("ln_g", c)).then_inc(done, 1)


def merge_first(nc, w, bank, convoutT, attnT, gateT, mergedT):
    with Stage(nc, "merge1") as st:
        part = st.sb("part", [P, 2, 2, T])
        conv_gated, gated, merged = st.sem("conv_gated"), st.sem("gated"), st.sem("merged")
        u0 = first_unit("wo")
        with st.block() as block:
            @block.sync
            def _(sp):
                w.load(sp, first_unit("wout1") + RING)

            @block.tensor
            def _(pe):
                for n in range(DT):
                    ring = w.wait(pe, u0 + n)
                    if n >= RING:
                        pe.wait_ge(gated, n - RING + 1)
                    for k in range(DT):
                        mm = nc.tensor.matmul(bank[n % RING][:], ring[:, k], attnT[:, k], start=(k == 0), stop=(k == DT - 1))
                    mm.then_inc(w.done, 1)

            @block.vector
            def _(dve):
                for f in range(DT):
                    if f >= 2:
                        dve.wait_ge(merged, f - 1)
                    nc.vector.scalar_tensor_tensor(part[:, f % 2, 0], gateT[:, f], 1.0, convoutT[:, f], ALU.add,
                                                   ALU.mult).then_inc(conv_gated, 1)
                    dve.wait_ge(w.done, u0 + f + 1)
                    nc.vector.scalar_tensor_tensor(part[:, f % 2, 1], gateT[:, DT + f], 1.0, bank[f % RING][:], ALU.add,
                                                   ALU.mult).then_inc(gated, 1)
                    dve.wait_ge(conv_gated, f + 1)
                    dve.wait_ge(gated, f + 1)
                    nc.vector.tensor_tensor(mergedT[:, f], part[:, f % 2, 0], part[:, f % 2, 1], ALU.add).then_inc(merged, 1)


def out_residual(nc, w, bank, name, mergedT, x, prefetch, scale, store=None):
    with Stage(nc, name) as st:
        ready, added, stored = st.sem("ready"), st.sem("added"), st.sem("stored")
        u0 = first_unit(name)
        with st.block() as block:
            @block.sync
            def _(sp):
                w.load(sp, prefetch)
                if store is not None:
                    for t in range(TT):
                        sp.wait_ge(added, 2 * t + 2)
                        sp.dma_start(store[t * P:(t + 1) * P, :], x[:, t]).then_inc(stored, 16)
                    sp.wait_ge(stored, 16 * TT)

            @block.tensor
            def _(pe):
                for k in range(DT):
                    ring = w.wait(pe, u0 + k).rearrange("p a b -> p (a b)")
                    for t in range(TT):
                        for e in range(2):
                            mm = nc.tensor.matmul(bank[2 * t + e][:], mergedT[:, k, t * P:(t + 1) * P],
                                                  ring[:, e * 512:(e + 1) * 512], start=(k == 0), stop=(k == DT - 1))
                            if k == DT - 1 and (t, e) != (TT - 1, 1):
                                mm.then_inc(ready, 1)
                    mm.then_inc(w.done, 1)

            @block.vector
            def _(dve):
                for n in range(2 * TT):
                    t, e = n // 2, n % 2
                    if n < 2 * TT - 1:
                        dve.wait_ge(ready, n + 1)
                    else:
                        dve.wait_ge(w.done, u0 + DT)
                    part = x[:, t, e * 512:(e + 1) * 512]
                    nc.vector.scalar_tensor_tensor(part, bank[n][:], scale, part, ALU.mult, ALU.add).then_inc(added, 1)


def query_scores(nc, w, bank, h2T, subkeys, scores):
    with Stage(nc, "query") as st:
        queryT = st.sb("queryT", [P, RING, T])
        query_kept = st.sem("query_kept")
        u0 = first_unit("query")
        scored, score_kept = st.sem("scored"), st.sem("score_kept")
        with st.block() as block:
            @block.sync
            def _(sp):
                w.load(sp, first_unit("rwkv") + RING)

            @block.tensor
            def _(pe):
                def four_tiles(i, first):
                    for j in range(RING):
                        ring = w.wait(pe, u0 + j, i)
                        if not first:
                            pe.wait_ge(query_kept, i * RING + (j - RING + 1))
                        for k in range(DT):
                            mm = nc.tensor.matmul(bank[j][:], ring[:, k], h2T[:, k], start=(k == 0), stop=(k == DT - 1))
                        mm.then_inc(w.done, 1)
                    for j in range(RING):
                        pe.wait_ge(query_kept, i * RING + (j + 1))
                        if not first:
                            pe.wait_ge(score_kept, i * RING + (j - RING + 1))
                        for t in range(TT):
                            mm = nc.tensor.matmul(bank[4 + j][:, t * P:(t + 1) * P], queryT[:, j, t * P:(t + 1) * P],
                                                  subkeys[:, j % 2], start=True, stop=True)
                        mm.then_inc(scored, 1)
                rounds(pe, 4, four_tiles)

            @block.scalar
            def _(act):
                def four_tiles(i, first):
                    for j in range(RING):
                        act.wait_ge(w.done, i * RING + (u0 + j + 1))
                        if not first:
                            act.wait_ge(scored, i * RING + (j - RING + 1))
                        nc.scalar.activation(queryT[:, j], bank[j][:], ACT.Copy).then_inc(query_kept, 1)
                rounds(act, 4, four_tiles)

            @block.vector
            def _(dve):
                for n in range(16):
                    dve.wait_ge(scored, n + 1)
                    nc.vector.tensor_copy(scores[:, :, n], bank[4 + n % RING][:].rearrange("p (t n) -> p t n", t=TT)
                                          ).then_inc(score_kept, 1)


HEADS = TT * PH
GROUP = 4


def is_first(n, bound=1):
    return isinstance(n, int) and n < bound


def head_rounds(eng, body):
    def pair(i):
        for b in range(2):
            body(2 * i + b, b)
    pair(0)
    with eng.Fori(1, HEADS // 2 - 1) as i:
        pair(i)
    pair(HEADS // 2 - 1)


def experts(nc, w, bank, const, ident, scores, h2, peer_u, peer_v, x):
    HALF = TOPK // 2
    with Stage(nc, "peer") as st:
        ubuf = st.sb("ubuf", [P, 2 * GROUP, D])
        vbuf = st.sb("vbuf", [P, TOPK, D])
        junk = st.sb("junk", [P, D])
        sc = st.sb("sc", [P, 2, 2, NKEYS])
        index = st.sb("index", [P, 2, TOPK], I32)
        dots, gelu, weight = (st.sb(n, [P, TOPK]) for n in ("dots", "gelu", "weight"))
        diag = st.sb("diag", [P, TOPK, P])
        best, wheref, rcf, key = (st.sb(n, [P, 2, TOPK]) for n in ("best", "wheref", "rcf", "key"))
        where, rc = (st.sb(n, [P, 2, TOPK], U32) for n in ("where", "rc"))
        left = st.sb("left", [P, NKEYS])
        hot = st.sb("hot", [P, 2, TOPK, TOPK])
        pair, pairleft = hot[:, 0], hot[:, 1].rearrange("p a b -> p (a b)")
        top = st.sb("top", [P, TOPK])
        pos = st.sb("pos", [P, TOPK], U32)
        e, s, r = st.sb("e", [P, 2, TOPK]), st.sb("s", [P, 2]), st.sb("r", [P, 2])
        choice_open = st.sem("choice_open")
        scores_ready, step_done, index_ready = st.sem("scores_ready"), st.sem("step_done"), st.sem("index_ready")
        shifted, exped, recip_ready, gathers_open = (st.sem(n) for n in ("shifted", "exped", "recip_ready", "gathers_open"))
        u_arrived = [st.sem(f"u_arrived{q}") for q in range(2)]
        v_arrived = [st.sem(f"v_arrived{q}") for q in range(2)]
        dot_done, gelu_done, weight_ready = st.sem("dot_done"), st.sem("gelu_done"), st.sem("weight_ready")
        diag_ready, summed, added = st.sem("diag_ready"), st.sem("summed"), st.sem("added")
        iota = const.whole("iota").rearrange("p (a b) -> p a b", a=TOPK)
        score_heads = scores[:].rearrange("p t (h e) k -> p (t h) e k", e=2)

        with st.block() as block:
            @block.gpsimd
            def _(pool):
                def head(n, b):
                    pool.wait_ge(index_ready, n + 1)
                    for half in range(2):
                        for q in (2 * half, 2 * half + 1):
                            if not (is_first(n) and q < 2):
                                pool.wait_ge(dot_done, TOPK * n + GROUP * (q - 1))
                            pool.sem_inc(gathers_open, 1)
                            for k in range(GROUP):
                                col = index[:, b, q * GROUP + k:q * GROUP + k + 1]
                                pool.indirect_dma_start(ubuf[:, q % 2 * GROUP + k], None, peer_u,
                                                        bass.IndirectOffsetOnAxis(col, 0)).then_inc(u_arrived[q % 2], 16)
                        if not is_first(n):
                            pool.wait_ge(summed, 2 * n + (half - 1))
                        pool.sem_inc(gathers_open, 1)
                        for k in range(half * HALF, (half + 1) * HALF):
                            pool.indirect_dma_start(vbuf[:, k], None, peer_v,
                                                    bass.IndirectOffsetOnAxis(index[:, b, k:k + 1], 0)
                                                    ).then_inc(v_arrived[half], 16)
                head_rounds(pool, head)

            @block.vector
            def _(dve):
                def choose(n, b):
                    count = 0

                    def do(ins):
                        nonlocal count
                        count += 1
                        ins.then_inc(step_done, 1)
                        dve.wait_ge(step_done, count)

                    def top16(src, rest, vals, idx):
                        do(nc.vector.max(vals[:, 0:8], src))
                        do(nc.vector.max_index(idx[:, 0:8], vals[:, 0:8], src))
                        do(nc.vector.match_replace(rest, vals[:, 0:8], src, -3.0e38))
                        do(nc.vector.max(vals[:, 8:16], rest))
                        do(nc.vector.max_index(idx[:, 8:16], vals[:, 8:16], rest))

                    wide = [P, 2, TOPK, TOPK]
                    dve.wait_ge(scores_ready, n + 1)
                    dve.sem_inc(choice_open, 1)
                    dve.sem_clear(step_done)
                    for half in range(2):
                        top16(sc[:, b, half], left[:], best[:, half], where[:, half])
                    do(nc.vector.tensor_tensor(pair, best[:, 0].unsqueeze(2).broadcast_to([P, TOPK, TOPK]),
                                               best[:, 1].unsqueeze(1).broadcast_to([P, TOPK, TOPK]), ALU.add))
                    top16(pair.rearrange("p a b -> p (a b)"), pairleft, top[:], pos[:])
                    nc.vector.tensor_scalar(rc[:, 0], pos[:], 4, None, ALU.logical_shift_right)
                    nc.vector.tensor_copy(wheref[:], where[:])
                    do(nc.vector.tensor_scalar(rc[:, 1], pos[:], 15, None, ALU.bitwise_and))
                    do(nc.vector.tensor_copy(rcf[:], rc[:]))
                    do(nc.vector.tensor_tensor(hot[:], rcf[:].unsqueeze(3).broadcast_to(wide),
                                               iota.unsqueeze(1).broadcast_to(wide), ALU.is_equal))
                    do(nc.vector.tensor_tensor(hot[:], hot[:], wheref[:].unsqueeze(2).broadcast_to(wide), ALU.mult))
                    do(nc.vector.tensor_reduce(key[:], hot[:], AXX, ALU.add))
                    if not is_first(n, 2):
                        for q in range(2):
                            dve.wait_ge(u_arrived[q], 16 * HALF * n - 16 * HALF)
                            dve.wait_ge(v_arrived[q], 16 * HALF * n - 16 * HALF)
                        dve.wait_ge(weight_ready, n - 1)
                    nc.vector.scalar_tensor_tensor(index[:, b], key[:, 0], float(NKEYS), key[:, 1], ALU.mult,
                                                   ALU.add).then_inc(index_ready, 1)
                    nc.vector.tensor_scalar(e[:, b], top[:], top[:, 0:1], None, ALU.subtract).then_inc(shifted, 1)
                    dve.wait_ge(exped, n + 1)
                    nc.vector.reciprocal(r[:, b:b + 1], s[:, b:b + 1]).then_inc(recip_ready, 1)

                def add(n, t, b):
                    dve.wait_ge(summed, 2 * n + 2)
                    if not is_first(n):
                        dve.wait_ge(added, 2 * n)
                    for c in range(2):
                        part = x[:, t, c * 512:(c + 1) * 512]
                        nc.vector.tensor_tensor(part, bank[2 * b + c][:], part, ALU.add).then_inc(added, 1)

                def head(n, b):
                    t = n // PH
                    for q in range(4):
                        dve.wait_ge(u_arrived[q % 2], 16 * HALF * n + 16 * GROUP * (q // 2 + 1))
                        if q == 0 and not is_first(n):
                            dve.wait_ge(gelu_done, n)
                        for k in range(GROUP):
                            if not (is_first(n) and q + k == 0):
                                dve.wait_ge(dot_done, TOPK * n + (GROUP * q + k))
                            nc.vector.scalar_tensor_tensor(junk[:], ubuf[:, q % 2 * GROUP + k], 1.0, h2[:, t], ALU.mult,
                                                           ALU.mult, accum_out=dots[:, GROUP * q + k:GROUP * q + k + 1]
                                                           ).then_inc(dot_done, 1)
                    dve.wait_ge(gelu_done, n + 1)
                    dve.wait_ge(recip_ready, n + 1)
                    if not is_first(n):
                        dve.wait_ge(diag_ready, TOPK * n)
                    nc.vector.scalar_tensor_tensor(weight[:], gelu[:], r[:, b:b + 1], e[:, b], ALU.mult, ALU.mult
                                                   ).then_inc(weight_ready, 1)
                    if not is_first(n):
                        add(n - 1, (n - 1) // PH, 1 - b)
                    if not (isinstance(n, int) and n + 2 >= HEADS):
                        choose(n + 2, b)

                choose(0, 0)
                choose(1, 1)
                head_rounds(dve, head)
                add(HEADS - 1, TT - 1, 1)

            @block.scalar
            def _(act):
                def copy_scores(n, b):
                    if not is_first(n, 2):
                        act.wait_ge(index_ready, n - 1)
                    nc.scalar.activation(sc[:, b], score_heads[:, n], ACT.Copy).then_inc(scores_ready, 1)

                def exps(n, b):
                    act.wait_ge(shifted, n + 1)
                    if not is_first(n, 2):
                        act.wait_ge(recip_ready, n - 1)
                    nc.scalar.activation(e[:, b], e[:, b], ACT.Exp, accum_out=s[:, b:b + 1]).then_inc(exped, 1)

                def head(n, b):
                    if not (isinstance(n, int) and n + 2 >= HEADS):
                        copy_scores(n + 2, b)
                    act.wait_ge(dot_done, TOPK * n + TOPK)
                    if not is_first(n):
                        act.wait_ge(weight_ready, n)
                    nc.scalar.activation(gelu[:], dots[:], ACT.Gelu).then_inc(gelu_done, 1)
                    act.wait_ge(weight_ready, n + 1)
                    for k in range(TOPK):
                        if not is_first(n) and k % HALF == 0:
                            act.wait_ge(summed, 2 * n + (k // HALF - 1))
                        nc.scalar.activation(diag[:, k], ident, ACT.Copy, scale=weight[:, k:k + 1]).then_inc(diag_ready, 1)
                    if not (isinstance(n, int) and n + 2 >= HEADS):
                        exps(n + 2, b)

                copy_scores(0, 0)
                copy_scores(1, 1)
                exps(0, 0)
                exps(1, 1)
                head_rounds(act, head)

            @block.tensor
            def _(pe):
                def head(n, b):
                    if not is_first(n, 2):
                        pe.wait_ge(added, 2 * n - 2)
                    for half in range(2):
                        pe.wait_ge(v_arrived[half], 16 * HALF * n + 16 * HALF)
                        for k in range(half * HALF, (half + 1) * HALF):
                            pe.wait_ge(diag_ready, TOPK * n + (k + 1))
                            for c in range(2):
                                mm = nc.tensor.matmul(bank[2 * b + c][:], diag[:, k], vbuf[:, k, c * 512:(c + 1) * 512],
                                                      start=(k == 0), stop=(k == TOPK - 1))
                        mm.then_inc(summed, 1)
                head_rounds(pe, head)


def final_norm(nc, w, x, gain):
    with Stage(nc, "final") as st:
        junk = st.sb("junk", [P, D])
        ss, ms, rms, rstd = (st.sb(n, [P, TT]) for n in ("ss", "ms", "rms", "rstd"))
        squared, mean_ready, root_ready = st.sem("squared"), st.sem("mean_ready"), st.sem("root_ready")
        rstd_ready, normed = st.sem("rstd_ready"), st.sem("normed")
        with st.block() as block:
            @block.scalar
            def _(act):
                for t in range(TT):
                    if t:
                        act.wait_ge(squared, t)
                    nc.scalar.activation(junk[:], x[:, t], ACT.Square, accum_out=ss[:, t:t + 1]).then_inc(squared, 1)
                act.wait_ge(mean_ready, 1)
                nc.scalar.activation(rms[:], ms[:], ACT.Sqrt).then_inc(root_ready, 1)

            @block.vector
            def _(dve):
                dve.wait_ge(squared, TT)
                nc.vector.tensor_scalar(ms[:], ss[:], 1.0 / D, EPS, ALU.mult, ALU.add).then_inc(mean_ready, 1)
                dve.wait_ge(root_ready, 1)
                nc.vector.reciprocal(rstd[:], rms[:]).then_inc(rstd_ready, 1)
                dve.wait_ge(rstd_ready, 1)
                for t in range(TT):
                    nc.vector.scalar_tensor_tensor(x[:, t], x[:, t], rstd[:, t:t + 1], gain, ALU.mult,
                                                   ALU.mult).then_inc(normed, 1)


def project_tiles(nc, w, bank, name, unit, count, src, takers, prefetch):
    width = src.shape[-1]
    with Stage(nc, name) as st:
        kept = st.sem("kept")
        u0 = first_unit(unit)
        with st.block() as block:
            @block.sync
            def _(sp):
                w.load(sp, prefetch)

            @block.tensor
            def _(pe):
                def four_tiles(i, first, count=RING):
                    for j in range(count):
                        ring = w.wait(pe, u0 + j, i)
                        if not first:
                            pe.wait_ge(kept, i * RING + (j - RING + 1))
                        for k in range(DT):
                            mm = nc.tensor.matmul(bank[j][:, 0:width], ring[:, k], src[:, k], start=(k == 0),
                                                  stop=(k == DT - 1))
                        mm.then_inc(w.done, 1)
                rounds(pe, count // RING, four_tiles)
                if count % RING:
                    four_tiles(count // RING, False, count % RING)

            @block.scalar
            def _(act):
                for n in range(count):
                    func, to = takers[n]
                    act.wait_ge(w.done, u0 + n + 1)
                    nc.scalar.activation(to, bank[n % RING][:, 0:width], func).then_inc(kept, 1)


def rms_over_partitions(nc, bank, name, tiles, gain, group_ones, per, fill, steps):
    width = tiles[0].shape[-1]
    with Stage(nc, name) as st:
        sq = st.sb("sq", [P, 2, width])
        ms = st.sb("ms", [P, 2, width])
        root = st.sb("root", [P, 2, width])
        rstd = st.sb("rstd", [P, 2, width])
        squared, summed, mean_ready, root_ready, step_done = (st.sem(n) for n in (
            "squared", "summed", "mean_ready", "root_ready", "step_done"))
        with st.block() as block:
            @block.tensor
            def _(pe):
                for n in range(len(tiles)):
                    pe.wait_ge(squared, n + 1)
                    if n >= 2:
                        pe.wait_ge(mean_ready, n - 1)
                    nc.tensor.matmul(bank[n % 2][:, 0:width], group_ones, sq[:, n % 2], start=True, stop=True
                                     ).then_inc(summed, 1)
                    fill.pe(pe, steps)

            @block.scalar
            def _(act):
                for n in range(len(tiles) + 1):
                    if n < len(tiles):
                        if n >= 2:
                            act.wait_ge(summed, n - 1)
                        nc.scalar.activation(sq[:, n % 2], tiles[n], ACT.Square).then_inc(squared, 1)
                    if n:
                        m = n - 1
                        act.wait_ge(mean_ready, m + 1)
                        if m >= 2:
                            act.wait_ge(step_done, 2 * m - 3)
                        nc.scalar.activation(root[:, m % 2], ms[:, m % 2], ACT.Sqrt).then_inc(root_ready, 1)
                fill.act(act)

            @block.vector
            def _(dve):
                for n in range(len(tiles)):
                    dve.wait_ge(summed, n + 1)
                    if n >= 2:
                        dve.wait_ge(root_ready, n - 1)
                    nc.vector.tensor_scalar(ms[:, n % 2], bank[n % 2][:, 0:width], 1.0 / per, EPS, ALU.mult,
                                            ALU.add).then_inc(mean_ready, 1)
                    dve.wait_ge(root_ready, n + 1)
                    if n >= 2:
                        dve.wait_ge(step_done, 2 * n - 2)
                    nc.vector.reciprocal(rstd[:, n % 2], root[:, n % 2]).then_inc(step_done, 1)
                    dve.wait_ge(step_done, 2 * n + 1)
                    nc.vector.scalar_tensor_tensor(tiles[n], tiles[n], gain, rstd[:, n % 2], ALU.mult,
                                                   ALU.mult).then_inc(step_done, 1)

            @block.sync
            def _(sp):
                fill.sp(sp)


def second_block(nc, ctx, w, bank, a, x, out, dump, load):
    cols_sb = ctx.enter_context(nc.sbuf_tensor("cols2", [P, sum(COLS2.values())], F32))
    const_sb = ctx.enter_context(nc.sbuf_tensor("const2", [P, sum(CONST2.values())], F32))
    cols, const = Columns(cols_sb, COLS2), Columns(const_sb, CONST2)
    ident = const.whole("ident")
    load("second", [(cols_sb[:], a["cols2"]), (const_sb[:], a["const2"])])

    hT = ctx.enter_context(nc.sbuf_tensor("h3T", [P, DT, T], F32))
    yT = [ctx.enter_context(nc.sbuf_tensor("yaT", [P, 4, T], F32))]
    norm_to_T(nc, w, bank, "norm3", x, TT, cols.whole("norm"), ident, hT, first_unit("rwkv") + RING)
    z_store = nc.dram_tensor("z_store", (FILL2, P, T), F32, kind="Internal").ap()
    st = ctx.enter_context(Stage(nc, "fill2"))
    fill = Filler(nc, st, w, bank[6:8],
                  lambda n: first_unit("fill2") + n if n < FILL2_BEFORE_MEM
                  else first_unit("fill2_rest") + n - FILL2_BEFORE_MEM,
                  [(hT, ACT.Copy, 1.0, None)] * FILL2, z_store)
    fill.limit = FILL2_BEFORE_MEM
    rwkv_branch(nc, w, bank, a, cols, const, hT, yT[0], dump, load, fill)
    yT += [ctx.enter_context(nc.sbuf_tensor(f"y{n}T", [P, 4, T], F32)) for n in "bc"]
    sliding_branch(nc, w, bank, a, cols, const, yT[1], dump, load, fill)
    catch_up(nc, fill)
    memory_branch(nc, w, bank, a, cols, const, yT[2], dump, load, fill)
    catch_up(nc, fill)
    with nc.sbuf_tensor("merged2T", [P, DT, T], F32) as mergedT:
        merge_second(nc, w, bank, yT, z_store, mergedT)
        out_residual(nc, w, bank, "wout2", mergedT, x, sum(n for _, n in UNITS), 1.0, store=out)


def fetch(nc, name, fill, first, z, silu, steps):
    n = z.shape[1]
    with Stage(nc, name) as st, st.block() as block:
        arrived, done = st.sem("arrived"), st.sem("done")

        @block.tensor
        def _(pe):
            fill.pe(pe, steps)

        @block.scalar
        def _(act):
            act.wait_ge(arrived, 16)
            for k in range(silu, n):
                nc.scalar.activation(z[:, k], z[:, k], ACT.Silu).then_inc(done, 1)
            fill.act(act)

        @block.sync
        def _(sp):
            assert fill.sent >= first + n
            fill.wait_stored(sp)
            sp.dma_start(z, fill.store[first:first + n].rearrange("n p t -> p n t")).then_inc(arrived, 16)
            fill.sp(sp)


def memory_branch(nc, w, bank, a, cols, const, y, dump, load, fill):
    ident, ones = const.whole("ident"), const.whole("ones")
    with ExitStack() as s:
        kT = s.enter_context(nc.sbuf_tensor("kT", [P, 4, MEM], F32))
        v_tok = s.enter_context(nc.sbuf_tensor("vm_tok", [P, 2, 512], F32))
        with ExitStack() as m:
            mem = m.enter_context(nc.sbuf_tensor("mem", [P, 2, D], F32))
            memT = m.enter_context(nc.sbuf_tensor("memT", [P, DT, MEM], F32))
            vT = m.enter_context(nc.sbuf_tensor("vT", [P, 4, MEM], F32))
            load("mem", [(mem[:], a["mem"].rearrange("(t p) d -> p t d", p=P))])
            norm_to_T(nc, w, bank, "memnorm", mem, 2, cols.whole("memnorm"), ident, memT, first_unit("mem") + RING)
            project_tiles(nc, w, bank, "memkv", "mem", 8, memT,
                          [(ACT.Copy, kT[:, n]) for n in range(4)] + [(ACT.Copy, vT[:, n]) for n in range(4)],
                          first_unit("fill2_rest") + RING)
            turn_tiles(nc, w, bank, "turn_vm", [([vT[:, n, c * P:(c + 1) * P] for n in range(4)], v_tok[:, c])
                                                for c in range(2)], ident, first_unit("fill2_rest") + RING)
        fill.limit = FILL2
        rms_over_partitions(nc, bank, "knorm", [kT[:, n] for n in range(4)], cols.whole("xk_g"), ones, P, fill, 2)
        qz = s.enter_context(nc.sbuf_tensor("xqz", [P, 8, T], F32))
        fetch(nc, "xqz", fill, 10, qz[:], 4, 6)
        rms_over_partitions(nc, bank, "xqnorm", [qz[:, n] for n in range(4)], cols.whole("xq_g"), ones, P, fill, 2)
        units = [dict(q=qz[:, h, b * P:(b + 1) * P], k=kT[:, h], bias=None,
                      v=[v_tok[:, c, h * P:(h + 1) * P] for c in range(2)], half=0) for b in range(TT) for h in range(4)]
        attention(nc, w, bank, "attn3", units, 0, scale=P ** -0.5, sink=None, ident=ident,
                  out=lambda g: y[:, :, g * P:(g + 1) * P], group=4, dim=P, fill=fill, fill_steps=1)
        multiply(nc, "xgate", y, qz[:, 4:8])
    dump("yc", y)


def multiply(nc, name, to, by):
    with Stage(nc, name) as st, st.block() as block:
        @block.vector
        def _(dve):
            nc.vector.tensor_tensor(to[:], to[:], by, ALU.mult)


def sliding_branch(nc, w, bank, a, cols, const, y, dump, load, fill):
    ident = const.whole("ident")
    with ExitStack() as s:
        z = s.enter_context(nc.sbuf_tensor("swz", [P, 10, T], F32))
        v_tok = s.enter_context(nc.sbuf_tensor("vs_tok", [P, TT, P], F32))
        sink8 = s.enter_context(nc.sbuf_tensor("sink8_2", [P, 8], F32))
        fetch(nc, "swz", fill, 0, z[:], 6, 6)
        rms_over_partitions(nc, bank, "sqnorm", [z[:, n] for n in range(4)], cols.whole("q_g"), const.whole("halves"), HD,
                            fill, 2)
        rms_over_partitions(nc, bank, "sknorm", [z[:, 4]], cols.whole("k_g"), const.whole("halves"), HD, fill, 3)
        turn_tiles(nc, w, bank, "turn_vs", [([z[:, 5, t * P:(t + 1) * P]], v_tok[:, t]) for t in range(TT)], ident, 0)
        rotate(nc, bank, a, cols, const, z, load, fill)
        with Stage(nc, "sink2") as st, st.block() as block:
            @block.vector
            def _(dve):
                nc.vector.tensor_scalar(sink8[:], cols.whole("sinks"), float(HD ** 0.5), None, ALU.mult)
        units = []
        for b in range(TT):
            lo = max(b - 1, 0)
            for i in range(4):
                for e in range(2):
                    h, part = HEADS2[i][e], slice(e * HD, (e + 1) * HD)
                    units.append(dict(q=z[part, i, b * P:(b + 1) * P], k=z[part, 4, lo * P:(b + 1) * P],
                                      bias=(const.whole("band")[:, (lo - b + 1) * P:2 * P], 1.0),
                                      v=[v_tok[:, c, part] for c in range(lo, b + 1)],
                                      sink=cols("sinks", h), sink_scaled=sink8[:, h:h + 1], half=e))
        attention(nc, w, bank, "attn2", units, 0, scale=HD ** -0.5, sink=True, ident=ident,
                  out=lambda g: y[:, :, g * P:(g + 1) * P], group=8, dim=HD, fill=fill, fill_steps=1)
        multiply(nc, "sgate", y, z[:, 6:10])
    dump("yb", y)


def rotate(nc, bank, a, cols, const, z, load, fill):
    two_pi = 2 * np.pi
    c1 = 6.28125
    c2 = float(np.float32(np.floor((two_pi - c1) * 2 ** 22) / 2 ** 22))
    c3 = float(two_pi - c1 - c2)
    magic = 1.5 * 2 ** 23
    with Stage(nc, "rope") as st:
        pos = st.sb("pos", [P, T], I32)
        angle, turns, count, part, trig = (st.sb(n, [P, T]) for n in ("angle", "turns", "count", "part", "trig"))
        sin, cos = st.sb("sin", [P, T]), st.sb("cos", [P, T])
        straight = st.sb("straight", [P, 2, T])
        crossed = st.sb("crossed", [P, 2, T])
        step_done, reduced, trig_ready, swapped, taken = (st.sem(n) for n in (
            "step_done", "reduced", "trig_ready", "swapped", "taken"))
        load("positions", [(pos[:], a["positions"])])
        with st.block() as block:
            @block.vector
            def _(dve):
                do = Chain(dve, step_done)
                do(nc.vector.tensor_copy(angle[:], pos[:]))
                do(nc.vector.tensor_scalar(angle[:], angle[:], cols("inv"), None, ALU.mult))
                for n, (shift, quarter) in enumerate(((0.0, 0.0), (0.25, np.pi / 2))):
                    do(nc.vector.tensor_scalar(turns[:], angle[:], 1.0 / two_pi, shift, ALU.mult, ALU.add))
                    do(nc.vector.tensor_scalar(count[:], turns[:], magic, None, ALU.add))
                    do(nc.vector.tensor_scalar(count[:], count[:], -magic, None, ALU.add))
                    do(nc.vector.scalar_tensor_tensor(part[:], count[:], -c1, angle[:], ALU.mult, ALU.add))
                    do(nc.vector.scalar_tensor_tensor(part[:], count[:], -c2, part[:], ALU.mult, ALU.add))
                    do(nc.vector.scalar_tensor_tensor(part[:], count[:], -c3, part[:], ALU.mult, ALU.add))
                    if n:
                        dve.wait_ge(trig_ready, n)
                    do(nc.vector.tensor_scalar(trig[:], part[:], float(quarter), 3.1415925, ALU.add, ALU.min))
                    nc.vector.tensor_scalar(trig[:], trig[:], -3.1415925, None, ALU.max).then_inc(reduced, 1)
                for i in range(5):
                    dve.wait_ge(trig_ready, 2)
                    dve.wait_ge(swapped, i + 1)
                    if i >= 2:
                        dve.wait_ge(taken, i - 1)
                    do(nc.vector.tensor_tensor(crossed[:, i % 2], bank[i][:], sin[:], ALU.mult))
                    do(nc.vector.tensor_tensor(straight[:, i % 2], z[:, i], cos[:], ALU.mult))
                    nc.vector.tensor_tensor(z[:, i], straight[:, i % 2], crossed[:, i % 2], ALU.add).then_inc(taken, 1)

            @block.tensor
            def _(pe):
                for i in range(5):
                    nc.tensor.matmul(bank[i][:], const.whole("swap"), z[:, i], start=True, stop=True).then_inc(swapped, 1)
                fill.pe(pe, 20)

            @block.scalar
            def _(act):
                for n, to in enumerate((sin, cos)):
                    act.wait_ge(reduced, n + 1)
                    nc.scalar.activation(to[:], trig[:], ACT.Sin).then_inc(trig_ready, 1)
                fill.act(act)

            @block.sync
            def _(sp):
                fill.sp(sp)


def rwkv_branch(nc, w, bank, a, cols, const, hT, y, dump, load, fill):
    ident, halves = const.whole("ident"), const.whole("halves")
    with ExitStack() as s:
        sb = lambda n, shape: s.enter_context(nc.sbuf_tensor(f"rw_{n}", shape, F32))
        gate = sb("gate", [P, 4, T])
        bonus = sb("bonus", [P, 4, T])
        r_end = sb("r_end", [P, 4, T // CH])
        R = sb("R", [P, 4, T])
        A = sb("A", [P, 4, T])
        B = sb("B", [P, 4, T])
        Kt = sb("K", [P, 4, T])
        toks = {n: sb(f"{n}_tok", [P, TT, 512]) for n in "ABKV"}
        with ExitStack() as s2:
            z = s2.enter_context(nc.sbuf_tensor("rwz", [P, 13, T + 1], F32))
            project_tiles(nc, w, bank, "rwz", "rwkv", 17, hT,
                          [(ACT.Copy, z[:, n, 1:T + 1]) for n in range(13)] + [(ACT.Silu, gate[:, n]) for n in range(4)],
                          first_unit("fill2") + RING)
            rwkv_prepare(nc, bank, a, cols, const, z, R, A, B, Kt, bonus, r_end, toks, load, fill)
            turn_tiles(nc, w, bank, "turn_rw",
                       [([m[:, n, o + t * P:o + (t + 1) * P] for n in range(4)], toks[name][:, t])
                        for name, m, o in (("A", A, 0), ("B", B, 0), ("K", Kt, 0), ("V", z[:, 8:12], 1))
                        for t in range(TT)], ident, 0)
        ZW = sb("ZW", [P, TT, 8, 2 * CH])
        WT = sb("WT", [P, TT, 4, P])
        for t in range(TT):
            rwkv_solve(nc, bank, const, t, A, B, Kt, toks, ZW, WT, fill)
        S = sb("S", [P, T // CH + 1, 4, CH])
        rwkv_chain(nc, bank, const, toks, ZW, r_end, S, fill)
        for t in range(TT):
            rwkv_output(nc, bank, const, t, R, B, Kt, toks, ZW, WT, S, y, fill)
        rwkv_finish(nc, bank, cols, halves, y, bonus, gate, dump, fill)


def rwkv_prepare(nc, bank, a, cols, const, z, R, A, B, Kt, bonus, r_end, toks, load, fill):
    halves = const.whole("halves")
    with Stage(nc, "rwprep") as st:
        lora, w0, tl, tmp = toks["V"][:, 0], toks["V"][:, 1], toks["V"][:, 2], toks["K"][:, 0:2]
        rate, aa = toks["A"], toks["B"]
        inv = Kt
        load("lora", [(lora, a["lora"]), (w0, a["rows2"])])
        zero, step_done, mixed, tanh_ready = st.sem("zero"), st.sem("step_done"), st.sem("mixed"), st.sem("tanh_ready")
        lora_ready, biased, rate_ready, a_ready = st.sem("lora_ready"), st.sem("biased"), st.sem("rate_ready"), st.sem("a_ready")
        with st.block() as block:
            @block.vector
            def _(dve):
                do = Chain(dve, step_done)
                do(nc.vector.memset(z[:, :, 0:1], 0.0))
                for n in [12] + list(range(12)):
                    do(nc.vector.tensor_tensor(tmp[:, n % 2], z[:, n, 0:T], z[:, n, 1:T + 1], ALU.subtract))
                    ins = nc.vector.scalar_tensor_tensor(z[:, n, 1:T + 1], tmp[:, n % 2], cols("mu", n), z[:, n, 1:T + 1],
                                                         ALU.mult, ALU.add)
                    if n == 12:
                        ins.then_inc(mixed, 1)
                        dve.wait_ge(mixed, 1)
                    else:
                        do(ins)
                    if n == 2:
                        for t in range(TT):
                            dve.wait_ge(lora_ready, t + 1)
                            nc.vector.tensor_tensor(rate[:, t], bank[t][:], w0, ALU.add).then_inc(biased, 1)

            @block.tensor
            def _(pe):
                pe.wait_ge(tanh_ready, 1)
                for t in range(TT):
                    nc.tensor.matmul(bank[t][:], tl[0:CH, t * P:(t + 1) * P], lora[0:CH, :], start=True,
                                     stop=True).then_inc(lora_ready, 1)
                fill.pe(pe, 3)
                for c in range(4):
                    if c >= 2:
                        pe.wait_ge(a_ready, c - 1)
                    nc.tensor.matmul(bank[4 + c % 2][:], lora[CH:P, c * P:(c + 1) * P], z[CH:P, 12, 1:T + 1], start=True,
                                     stop=True).then_inc(lora_ready, 1)
                fill.pe(pe, 12)

            @block.scalar
            def _(act):
                act.wait_ge(mixed, 1)
                nc.scalar.activation(tl[0:CH], z[0:CH, 12, 1:T + 1], ACT.Tanh).then_inc(tanh_ready, 1)
                for t in range(TT):
                    act.wait_ge(biased, t + 1)
                    nc.scalar.activation(rate[:, t], rate[:, t], ACT.Sigmoid).then_inc(rate_ready, 1)
                for c in range(4):
                    act.wait_ge(lora_ready, TT + c + 1)
                    nc.scalar.activation(aa[:, c], bank[4 + c % 2][:], ACT.Sigmoid, bias=cols("a0", c)).then_inc(a_ready, 1)
                fill.act(act)

            @block.sync
            def _(sp):
                fill.sp(sp)
        cum_ready, exp_ready = st.sem("cum_ready"), st.sem("exp_ready")
        with st.block() as block:
            @block.tensor
            def _(pe):
                for e, mask in enumerate(("incl", "strict")):
                    for c in range(4):
                        if e and c >= 2:
                            pe.wait_ge(exp_ready, 8 + c - 1)
                        for t in range(TT):
                            mm = nc.tensor.matmul(bank[4 * e + (c % 2 if e else c)][:, t * P:(t + 1) * P], rate[:, t, c * P:(c + 1) * P],
                                                  const.whole(mask), start=True, stop=True)
                        mm.then_inc(cum_ready, 1)
                fill.pe(pe, 8)

            @block.scalar
            def _(act):
                for c in range(4):
                    act.wait_ge(cum_ready, c + 1)
                    nc.scalar.activation(R[:, c], bank[c][:], ACT.Exp, scale=-DECAY).then_inc(exp_ready, 1)
                    nc.scalar.activation(inv[:, c], bank[c][:], ACT.Exp, scale=DECAY).then_inc(exp_ready, 1)
                for c in range(4):
                    act.wait_ge(cum_ready, 4 + c + 1)
                    nc.scalar.activation(A[:, c], bank[4 + c % 2][:], ACT.Exp, scale=-DECAY).then_inc(exp_ready, 1)
                fill.act(act)

            @block.sync
            def _(sp):
                fill.sp(sp)
        kk_ready, squared, norm_ready, root_ready, k_done, rk_ready, bonus_ready = (st.sem(n) for n in (
            "kk_ready", "squared", "norm_ready", "root_ready", "k_done", "rk_ready", "bonus_ready"))
        with st.block() as block:
            @block.vector
            def _(dve):
                do = Chain(dve, k_done)
                zr, zk, zv = ([z[:, n + c, 1:T + 1] for c in range(4)] for n in (0, 4, 8))
                do(nc.vector.tensor_copy(r_end[:], R[:, :, CH - 1:T:CH]))
                for c in range(4):
                    nc.vector.tensor_scalar(B[:, c], zk[c], cols("k_k", c), None, ALU.mult).then_inc(kk_ready, 1)
                for c in range(4):
                    dve.wait_ge(root_ready, c + 1)
                    do(nc.vector.tensor_scalar(tmp[:, 0], rate[:, c], 1e-12, None, ALU.max))
                    do(nc.vector.reciprocal(tmp[:, 1], tmp[:, 0]))
                    do(nc.vector.tensor_tensor(B[:, c], B[:, c], tmp[:, 1], ALU.mult))
                    do(nc.vector.scalar_tensor_tensor(A[:, c], B[:, c], -1.0, A[:, c], ALU.mult, ALU.mult))
                    do(nc.vector.tensor_tensor(B[:, c], B[:, c], aa[:, c], ALU.mult))
                    do(nc.vector.tensor_tensor(B[:, c], B[:, c], inv[:, c], ALU.mult))
                    do(nc.vector.tensor_scalar(aa[:, c], aa[:, c], -1.0, cols("k_a", c), ALU.add, ALU.mult))
                    do(nc.vector.scalar_tensor_tensor(zk[c], aa[:, c], 1.0, zk[c], ALU.add, ALU.mult))
                    do(nc.vector.tensor_tensor(Kt[:, c], zk[c], inv[:, c], ALU.mult))
                    do(nc.vector.tensor_tensor(bonus[:, c], zr[c], zk[c], ALU.mult))
                    nc.vector.tensor_scalar(bonus[:, c], bonus[:, c], cols("r_k", c), None, ALU.mult).then_inc(rk_ready, 1)
                    do(nc.vector.tensor_tensor(R[:, c], zr[c], R[:, c], ALU.mult))
                for c in range(4):
                    dve.wait_ge(bonus_ready, c + 1)
                    do(nc.vector.tensor_tensor(bonus[:, c], bank[c][:], zv[c], ALU.mult))

            @block.tensor
            def _(pe):
                for c in range(4):
                    pe.wait_ge(squared, c + 1)
                    nc.tensor.matmul(bank[c][:], halves, rate[:, c], start=True, stop=True).then_inc(norm_ready, 1)
                fill.pe(pe, 10)
                for c in range(4):
                    pe.wait_ge(rk_ready, c + 1)
                    nc.tensor.matmul(bank[c][:], halves, bonus[:, c], start=True, stop=True).then_inc(bonus_ready, 1)
                    fill.pe(pe, 8 if c < 3 else 2)

            @block.scalar
            def _(act):
                for c in range(4):
                    act.wait_ge(kk_ready, c + 1)
                    nc.scalar.activation(rate[:, c], B[:, c], ACT.Square).then_inc(squared, 1)
                for c in range(4):
                    act.wait_ge(norm_ready, c + 1)
                    nc.scalar.activation(rate[:, c], bank[c][:], ACT.Sqrt).then_inc(root_ready, 1)
                fill.act(act)

            @block.sync
            def _(sp):
                fill.sp(sp)


def head(o):
    half, c = o // 4, o % 4
    return slice(half * HD, (half + 1) * HD), c, slice((2 * c + half) * HD, (2 * c + half + 1) * HD)


def by_head(tok):
    return tok.rearrange("p (c e v) -> p e c v", c=4, e=2)


def over_heads(mask, n=4):
    return mask.unsqueeze(1).broadcast_to([P, n, P])


def rwkv_solve(nc, bank, const, t, A, B, Kt, toks, ZW, WT, fill):
    ident = const.whole("ident")
    here = slice(t * P, (t + 1) * P)
    with Stage(nc, f"solve{t}") as st:
        AB, AK = st.sb("AB", [P, 8, P]), st.sb("AK", [P, 8, P])
        Tm, TmT, G, E = (st.sb(n, [P, 8, P]) for n in ("T", "TT", "G", "E"))
        QA = st.sb("QA", [P, 8, 2 * CH])
        step_done, products, turned, g_kept, filled = (st.sem(n) for n in (
            "step_done", "products", "turned", "g_kept", "filled"))
        with st.block() as block:
            @block.tensor
            def _(pe):
                for e, left in enumerate((B, Kt)):
                    for h in range(8):
                        part, c, cols = head(h)
                        mm = nc.tensor.matmul(bank[2 * e + h // 4][:, h % 4 * P:(h % 4 + 1) * P], left[part, c, here],
                                              A[part, c, here], start=True, stop=True)
                        if h % 4 == 3:
                            mm.then_inc(products, 1)
                fill.pe(pe, 4)
                fill.mark()
                pe.wait_ge(step_done, 6)
                for h in range(8):
                    mm = nc.tensor.transpose(bank[4 + h // 4][:, h % 4 * P:(h % 4 + 1) * P], TmT[:, h], ident)
                mm.then_inc(turned, 1)
                for h in range(8):
                    _, _, cols = head(h)
                    mm = nc.tensor.matmul(bank[0][:, h * CH:(h + 1) * CH], AK[:, h], toks["V"][:, t, cols],
                                          start=True, stop=True)
                mm.then_inc(turned, 1)
                fill.pe(pe, 3)

            @block.vector
            def _(dve):
                do = Chain(dve, step_done)
                for n, to in enumerate((AB, AB, AK, AK)):
                    dve.wait_ge(products, n + 1)
                    g = n % 2
                    do(nc.vector.tensor_tensor(to[:, 4 * g:4 * g + 4], bank[n][:].rearrange("p (h t) -> p h t", h=4),
                                               over_heads(const.whole("strict")), ALU.mult))
                do(nc.vector.tensor_tensor(TmT[:], AB[:], over_heads(const("level", 0, P), 8), ALU.mult))
                do(nc.vector.tensor_tensor(TmT[:], TmT[:], over_heads(ident, 8), ALU.add))

            @block.scalar
            def _(act):
                fill.act(act, fill.marks[0])
                act.wait_ge(turned, 1)
                for g in range(2):
                    nc.scalar.activation(Tm[:, 4 * g:4 * g + 4], bank[4 + g][:].rearrange("p (h t) -> p h t", h=4),
                                         ACT.Copy).then_inc(filled, 1)
                act.wait_ge(turned, 2)
                nc.scalar.activation(QA[:, :, 0:CH], bank[0][:].rearrange("p (h t) -> p h t", h=8), ACT.Copy
                                     ).then_inc(filled, 1)
                for e in range(2):
                    nc.scalar.activation(QA[:, 4 * e:4 * e + 4, CH:2 * CH], by_head(toks["A"][:, t])[:, e], ACT.Copy
                                         ).then_inc(filled, 1)
                fill.act(act)

            @block.sync
            def _(sp):
                fill.sp(sp)
        g_ready, d_ready, added, masked = (st.sem(n) for n in ("g_ready", "d_ready", "added", "masked"))
        with st.block() as block:
            @block.tensor
            def _(pe):
                for m in range(1, LEVELS):
                    for g in range(2):
                        pe.wait_ge(masked, m)
                        if m > 1:
                            pe.wait_ge(added, 2 * (m - 2) * 2 + 2 * g + 2)
                        for h in range(4 * g, 4 * g + 4):
                            mm = nc.tensor.matmul(bank[g][:, h % 4 * P:(h % 4 + 1) * P], E[:, h], Tm[:, h], start=True,
                                                  stop=True)
                        mm.then_inc(g_ready, 1)
                    fill.pe(pe, 1)
                    for g in range(2):
                        pe.wait_ge(g_kept, 2 * (m - 1) + g + 1)
                        for e in range(2):
                            for h in range(4 * g, 4 * g + 4):
                                mm = nc.tensor.matmul(bank[2 + 2 * g + e][:, h % 4 * P:(h % 4 + 1) * P],
                                                      G[:, h] if e else TmT[:, h], TmT[:, h] if e else G[:, h],
                                                      start=True, stop=True)
                            mm.then_inc(d_ready, 1)
                    fill.pe(pe, 1)
                    fill.mark()

            @block.vector
            def _(dve):
                for m in range(1, LEVELS):
                    if m > 1:
                        dve.wait_ge(g_ready, 2 * (m - 1))
                    nc.vector.tensor_tensor(E[:], AB[:], over_heads(const("level", m * P, P), 8), ALU.mult
                                            ).then_inc(masked, 1)
                    for g in range(2):
                        for e, to in enumerate((Tm, TmT)):
                            dve.wait_ge(d_ready, 4 * (m - 1) + 2 * g + 2)
                            if m > 1:
                                dve.wait_ge(added, 4 * (m - 2) + 2 * g + e + 1)
                            nc.vector.tensor_tensor(to[:, 4 * g:4 * g + 4], to[:, 4 * g:4 * g + 4],
                                                    bank[2 + 2 * g + e][:].rearrange("p (h t) -> p h t", h=4), ALU.add
                                                    ).then_inc(added, 1)

            @block.scalar
            def _(act):
                for m in range(1, LEVELS):
                    for g in range(2):
                        act.wait_ge(g_ready, 2 * (m - 1) + g + 1)
                        if m > 1:
                            act.wait_ge(d_ready, 4 * (m - 2) + 2 * g + 2)
                        nc.scalar.activation(G[:, 4 * g:4 * g + 4], bank[g][:].rearrange("p (h t) -> p h t", h=4),
                                             ACT.Copy).then_inc(g_kept, 1)
                    if m > 1:
                        fill.act(act, fill.marks[m - 2])
                fill.act(act)

            @block.sync
            def _(sp):
                fill.sp(sp)
        zw_ready, zw_kept = st.sem("zw_ready"), st.sem("zw_kept")
        with st.block() as block:
            @block.tensor
            def _(pe):
                for g in range(2):
                    for h in range(4 * g, 4 * g + 4):
                        mm = nc.tensor.matmul(bank[g][:, h % 4 * P:(h % 4 + 1) * P], TmT[:, h], QA[:, h], start=True,
                                              stop=True)
                    mm.then_inc(zw_ready, 1)
                for h in range(8):
                    part, c, cols = head(h)
                    mm = nc.tensor.matmul(bank[2][part, c * P:(c + 1) * P], toks["A"][:, t, cols],
                                          TmT[:, h], start=True, stop=True)
                mm.then_inc(zw_ready, 1)
                fill.pe(pe, 2)

            @block.scalar
            def _(act):
                for g in range(2):
                    act.wait_ge(zw_ready, g + 1)
                    nc.scalar.activation(ZW[:, t, 4 * g:4 * g + 4], bank[g][:].rearrange("p (h t) -> p h t", h=4), ACT.Copy
                                         ).then_inc(zw_kept, 1)
                act.wait_ge(zw_ready, 3)
                nc.scalar.activation(WT[:, t], bank[2][:].rearrange("p (c t) -> p c t", c=4), ACT.Copy).then_inc(zw_kept, 1)
                fill.act(act)

            @block.sync
            def _(sp):
                fill.sp(sp)


def rwkv_chain(nc, bank, const, toks, ZW, r_end, S, fill):
    n = T // CH
    with Stage(nc, "chain") as st:
        H = st.sb("H", [P, 2, 4, CH])
        new = st.sb("new", [P, 2, 4, CH])
        old = st.sb("old", [P, 4, CH])
        parts_ready, h_kept, new_kept, s_sum, scaled, s_ready = (st.sem(n) for n in (
            "parts_ready", "h_kept", "new_kept", "s_sum", "scaled", "s_ready"))
        tiles = lambda b, at: b[:, at:at + 4 * CH].rearrange("p (c k) -> p c k", c=4)
        with st.block() as block:
            @block.tensor
            def _(pe):
                def parts(ch):
                    rows, t = slice(ch % 2 * CH, (ch % 2 + 1) * CH), ch // 2
                    if ch >= 2:
                        pe.wait_ge(new_kept, ch - 1)
                    for o in range(8):
                        part, c, cols = head(o)
                        nc.tensor.matmul(bank[ch % 2][part, c * CH:(c + 1) * CH], ZW[rows, t, o, CH:2 * CH],
                                         toks["B"][rows, t, cols], start=True, stop=True)
                        to = bank[ch % 2][part, (4 + c) * CH:(5 + c) * CH]
                        nc.tensor.matmul(to, toks["B"][rows, t, cols], ZW[rows, t, o, 0:CH], start=True, stop=False)
                        mm = nc.tensor.matmul(to, toks["K"][rows, t, cols], toks["V"][rows, t, cols], start=False, stop=True)
                    mm.then_inc(parts_ready, 1)

                parts(0)
                for ch in range(n):
                    if ch + 1 < n:
                        parts(ch + 1)
                    fill.pe(pe, 1)
                    pe.wait_ge(h_kept, ch + 1)
                    pe.wait_ge(s_ready, ch + 1)
                    for o in range(8):
                        part, c, _ = head(o)
                        mm = nc.tensor.matmul(bank[2 + ch % 2][part, c * CH:(c + 1) * CH], H[part, ch % 2, c],
                                              S[part, ch, c], start=True, stop=True)
                    mm.then_inc(s_sum, 1)

            @block.vector
            def _(dve):
                def keep(ch):
                    dve.wait_ge(parts_ready, ch + 1)
                    if ch >= 2:
                        dve.wait_ge(s_sum, ch - 1)
                        dve.wait_ge(s_ready, ch)
                    nc.vector.tensor_tensor(H[:, ch % 2], tiles(bank[ch % 2], 0),
                                            const.whole("eye2").unsqueeze(1).broadcast_to([P, 4, CH]), ALU.add
                                            ).then_inc(h_kept, 1)
                    nc.vector.tensor_tensor(new[:, ch % 2], tiles(bank[ch % 2], 4 * CH),
                                            r_end[:, :, ch:ch + 1].broadcast_to([P, 4, CH]), ALU.mult).then_inc(new_kept, 1)

                nc.vector.memset(S[:, 0], 0.0).then_inc(s_ready, 1)
                keep(0)
                for ch in range(n):
                    if ch + 1 < n:
                        keep(ch + 1)
                    dve.wait_ge(s_sum, ch + 1)
                    if ch:
                        dve.wait_ge(s_ready, ch + 1)
                    nc.vector.tensor_tensor(old[:], tiles(bank[2 + ch % 2], 0),
                                            r_end[:, :, ch:ch + 1].broadcast_to([P, 4, CH]), ALU.mult).then_inc(scaled, 1)
                    dve.wait_ge(scaled, ch + 1)
                    dve.wait_ge(new_kept, ch + 1)
                    nc.vector.tensor_tensor(S[:, ch + 1], old[:], new[:, ch % 2], ALU.add).then_inc(s_ready, 1)

            @block.scalar
            def _(act):
                fill.act(act)

            @block.sync
            def _(sp):
                fill.sp(sp)


def rwkv_output(nc, bank, const, t, R, B, Kt, toks, ZW, WT, S, y, fill):
    here = slice(t * P, (t + 1) * P)
    with Stage(nc, f"rwout{t}") as st:
        RB, RK = st.sb("RB", [P, 8, P]), st.sb("RK", [P, 8, P])
        U = st.sb("U", [P, 8, CH])
        products, masked, u_sum, u_ready, y_ready, y_kept = (st.sem(n) for n in (
            "products", "masked", "u_sum", "u_ready", "y_ready", "y_kept"))
        with st.block() as block:
            @block.tensor
            def _(pe):
                for h in range(8):
                    part, c, cols = head(h)
                    for e in range(2):
                        mm = nc.tensor.matmul(bank[4 + h // 4][e * CH:(e + 1) * CH, c * CH:(c + 1) * CH],
                                              WT[part, t, c, e * CH:(e + 1) * CH], S[part, 2 * t + e, c], start=True,
                                              stop=True)
                mm.then_inc(u_sum, 1)
                for e, left in enumerate((B, Kt)):
                    for h in range(8):
                        part, c, cols = head(h)
                        mm = nc.tensor.matmul(bank[2 * e + h // 4][:, h % 4 * P:(h % 4 + 1) * P], left[part, c, here],
                                              R[part, c, here], start=True, stop=True)
                        if h % 4 == 3:
                            mm.then_inc(products, 1)
                fill.pe(pe, 2)
                pe.wait_ge(u_ready, 2)
                pe.wait_ge(masked, 4)
                for h in range(8):
                    part, c, cols = head(h)
                    nc.tensor.matmul(bank[4][part, c * P:(c + 1) * P], U[:, h], RB[:, h], start=True, stop=False)
                    nc.tensor.matmul(bank[4][part, c * P:(c + 1) * P], toks["V"][:, t, cols], RK[:, h],
                                     start=False, stop=False)
                    for e in range(2):
                        mm = nc.tensor.matmul(bank[4][part, c * P + e * CH:c * P + (e + 1) * CH], S[part, 2 * t + e, c],
                                              R[part, c, t * P + e * CH:t * P + (e + 1) * CH], start=False, stop=(e == 1))
                mm.then_inc(y_ready, 1)
                fill.pe(pe, 1)

            @block.vector
            def _(dve):
                dve.wait_ge(u_sum, 1)
                for e in range(2):
                    nc.vector.tensor_tensor(U[:, 4 * e:4 * e + 4],
                                            bank[4 + e][:, 0:4 * CH].rearrange("p (h v) -> p h v", h=4),
                                            ZW[:, t, 4 * e:4 * e + 4, 0:CH], ALU.add).then_inc(u_ready, 1)
                for n, to in enumerate((RB, RB, RK, RK)):
                    dve.wait_ge(products, n + 1)
                    g = n % 2
                    nc.vector.tensor_tensor(to[:, 4 * g:4 * g + 4], bank[n][:].rearrange("p (h t) -> p h t", h=4),
                                            over_heads(const.whole("incl")), ALU.mult).then_inc(masked, 1)

            @block.scalar
            def _(act):
                act.wait_ge(y_ready, 1)
                nc.scalar.activation(y[:, :, here], bank[4][:].rearrange("p (c t) -> p c t", c=4), ACT.Copy
                                     ).then_inc(y_kept, 1)
                fill.act(act)

            @block.sync
            def _(sp):
                fill.sp(sp)


def rwkv_finish(nc, bank, cols, halves, y, bonus, gate, dump, fill):
    with Stage(nc, "rwfin") as st:
        sq = st.sb("sq", [P, 4, T])
        mean, var, root, rstd = (st.sb(n, [P, T]) for n in ("mean", "var", "root", "rstd"))
        step_done, summed, centred, squared, var_ready, root_ready = (st.sem(n) for n in (
            "step_done", "summed", "centred", "squared", "var_ready", "root_ready"))
        with st.block() as block:
            @block.tensor
            def _(pe):
                for c in range(4):
                    nc.tensor.matmul(bank[c][:], halves, y[:, c], start=True, stop=True).then_inc(summed, 1)
                fill.pe(pe, 2)
                for c in range(4):
                    pe.wait_ge(squared, c + 1)
                    nc.tensor.matmul(bank[c][:], halves, sq[:, c], start=True, stop=True).then_inc(summed, 1)
                fill.pe(pe, 20)

            @block.scalar
            def _(act):
                for c in range(4):
                    act.wait_ge(centred, c + 1)
                    nc.scalar.activation(sq[:, c], y[:, c], ACT.Square).then_inc(squared, 1)
                for c in range(4):
                    act.wait_ge(var_ready, c + 1)
                    nc.scalar.activation(root[:], var[:], ACT.Sqrt).then_inc(root_ready, 1)
                fill.act(act)

            @block.vector
            def _(dve):
                do = Chain(dve, step_done)
                for c in range(4):
                    dve.wait_ge(summed, c + 1)
                    do(nc.vector.tensor_scalar(mean[:], bank[c][:], 1.0 / HD, None, ALU.mult))
                    nc.vector.tensor_tensor(y[:, c], y[:, c], mean[:], ALU.subtract).then_inc(centred, 1)
                    dve.wait_ge(centred, c + 1)
                for c in range(4):
                    dve.wait_ge(summed, 4 + c + 1)
                    if c:
                        dve.wait_ge(root_ready, c)
                    nc.vector.tensor_scalar(var[:], bank[c][:], 1.0 / HD, LNX_EPS, ALU.mult, ALU.add
                                            ).then_inc(var_ready, 1)
                    dve.wait_ge(root_ready, c + 1)
                    do(nc.vector.reciprocal(rstd[:], root[:]))
                    do(nc.vector.scalar_tensor_tensor(y[:, c], y[:, c], cols("lnx_g", c), rstd[:], ALU.mult, ALU.mult))
                    do(nc.vector.scalar_tensor_tensor(y[:, c], y[:, c], cols("lnx_b", c), bonus[:, c], ALU.add, ALU.add))
                    do(nc.vector.tensor_tensor(y[:, c], y[:, c], gate[:, c], ALU.mult))
            @block.sync
            def _(sp):
                fill.sp(sp)
    dump("ya", y)


def merge_second(nc, w, bank, yT, z_store, mergedT):
    u0, g0 = first_unit("merge"), FILL2 - 24

    def adds(n):
        return 2 * (n - (n + 2) // 3)

    with Stage(nc, "merge2") as st:
        z = st.sb("z", [P, 3, 2, T])
        gate = st.sb("gate", [P, 2, 2, T])
        part = st.sb("part", [P, 2, 2, T])
        z_arrived = [st.sem(f"z_arrived{i}") for i in range(3)]
        gate_ready, parts, merged = st.sem("gate_ready"), st.sem("parts"), st.sem("merged")
        with st.block() as block:
            @block.sync
            def _(sp):
                for n in range(12):
                    if n >= 3:
                        sp.wait_ge(gate_ready, n - 2)
                    at = g0 + 2 * n
                    sp.dma_start(z[:, n % 3], z_store[at:at + 2].rearrange("e p t -> p e t")
                                 ).then_inc(z_arrived[n % 3], 16)
                    w.load(sp, u0 + RING + max(n - 1, 0))
                w.load(sp, first_unit("wout2") + RING)

            @block.tensor
            def _(pe):
                for n in range(12):
                    ring = w.wait(pe, u0 + n)
                    if n >= 2:
                        pe.wait_ge(parts, 2 * (n - 1))
                    for e in range(2):
                        for k in range(4):
                            mm = nc.tensor.matmul(bank[2 * (n % 2) + e][:], ring[:, 4 * e + k], yT[n % 3][:, k],
                                                  start=(k == 0), stop=(k == 3))
                    mm.then_inc(w.done, 1)

            @block.scalar
            def _(act):
                for n in range(12):
                    act.wait_ge(z_arrived[n % 3], 16 * (n // 3 + 1))
                    if n >= 2:
                        act.wait_ge(parts, 2 * (n - 1))
                    nc.scalar.activation(gate[:, n % 2], z[:, n % 3], ACT.Sigmoid).then_inc(gate_ready, 1)

            @block.vector
            def _(dve):
                for n in range(12):
                    f = n // 3 * 2
                    dve.wait_ge(gate_ready, n + 1)
                    dve.wait_ge(w.done, u0 + n + 1)
                    for e in range(2):
                        to = mergedT[:, f + e] if n % 3 == 0 else part[:, n % 2, e]
                        if adds(n - 1) > 0:
                            dve.wait_ge(merged, adds(n - 1))
                        nc.vector.tensor_tensor(to, bank[2 * (n % 2) + e][:], gate[:, n % 2, e], ALU.mult
                                                ).then_inc(parts, 1)
                        if n % 3:
                            dve.wait_ge(parts, 2 * n + e + 1)
                            if n % 3 == 2:
                                dve.wait_ge(merged, adds(n))
                            nc.vector.tensor_tensor(mergedT[:, f + e], mergedT[:, f + e], part[:, n % 2, e], ALU.add
                                                    ).then_inc(merged, 1)


def program(nc, a, out, dump_to=None):
    dumped = []
    with ExitStack() as ctx:
        bank = [ctx.enter_context(nc.psum_tensor(f"bank{i}", [P, 512], F32)) for i in range(8)]
        w = Weights(nc, ctx, a["weights"])
        x = ctx.enter_context(nc.sbuf_tensor("x", [P, TT, D], F32))

        def dump(name, tensor):
            if dump_to is None or name not in dump_to:
                return
            with Stage(nc, f"dump_{name}") as st, st.block() as block:
                s = st.sem("s")

                @block.sync
                def _(sp):
                    sp.dma_start(dump_to[name], tensor[:]).then_inc(s, 16)
                    sp.wait_ge(s, 16)

        def load(name, pairs):
            with Stage(nc, name) as st, st.block() as block:
                s = st.sem("arrived")

                @block.sync
                def _(sp):
                    for to, of in pairs:
                        sp.dma_start(to, of).then_inc(s, 16)
                    sp.wait_ge(s, 16 * len(pairs))

        with ExitStack() as one:
            cols_sb = one.enter_context(nc.sbuf_tensor("cols1", [P, sum(COLS1.values())], F32))
            const_sb = one.enter_context(nc.sbuf_tensor("const1", [P, sum(CONST1.values())], F32))
            rows = one.enter_context(nc.sbuf_tensor("rows1", [P, 2 * D], F32))
            subkeys = one.enter_context(nc.sbuf_tensor("subkeys", [P, 2, NKEYS], F32))
            load("first", [(x[:], a["x"].rearrange("(t p) d -> p t d", p=P)), (cols_sb[:], a["cols1"]),
                           (const_sb[:], a["const1"]), (rows[:], a["rows1"]), (subkeys[:], a["subkeys"])])
            first_block(nc, w, bank, Columns(cols_sb, COLS1), Columns(const_sb, CONST1), rows, subkeys,
                        a["peer_u"], a["peer_v"], x, dump)
        if dump_to is None or "final" in dump_to or True:
            second_block(nc, ctx, w, bank, a, x, out, dump, load)


def constants():
    p, c = np.arange(P)[:, None], np.arange(P)[None, :]
    ident = np.eye(P)
    r, s3 = np.arange(P)[:, None], np.arange(3 * P)[None, :]
    dist = np.abs(r + P - s3).astype(np.float64)
    dist[dist > P] = FAR
    iota = np.broadcast_to(np.tile(np.arange(TOPK), TOPK), (P, TOPK * TOPK))
    const1 = np.concatenate([ident, np.ones((P, P)), dist, iota], 1).astype(np.float32)
    halves = (p // 64 == c // 64)
    swap = np.zeros((P, P))
    for o in range(P):
        if o % 64 < 32:
            swap[o + 32, o] = -1
        else:
            swap[o - 32, o] = 1
    s2 = np.arange(2 * P)[None, :]
    rel = r - s2 + P
    band = np.where((rel >= 0) & (rel < P), 0.0, -1e31)
    same = p // CH == c // CH
    strict, incl = same & (p < c), same & (p <= c)
    levels = [(p // (2 * m) == c // (2 * m)) & (p % (2 * m) < m) & (c % (2 * m) >= m) for m in (1, 2, 4, 8, 16, 32)]
    eye2 = np.concatenate([np.eye(CH), np.eye(CH)], 0)
    const2 = np.concatenate([ident, np.ones((P, P)), halves, swap, band, strict, incl, *levels, eye2], 1).astype(np.float32)
    inv = (10000.0 ** (-np.arange(32) / 32)).astype(np.float32)
    return const1, const2, np.tile(inv, 4)[:, None]


def unit_columns(mat, cols):
    m = mat[:, cols] if cols is not None else mat
    k, n = m.shape[0] // P, m.shape[1] // P
    return m.reshape(k, P, n, P).transpose(2, 1, 0, 3)


def lay_out(i):
    i = {k: np.asarray(v) for k, v in i.items()}
    col = lambda v: v.reshape(-1, P).T
    rep = lambda v: np.broadcast_to(v.reshape(1, -1), (P, v.size))
    full = lambda u: u.reshape(u.shape[0], P, DT * P)
    order1 = np.concatenate([np.arange(HD) + HD * h for pair in HEADS1 for h in pair])
    order2 = np.concatenate([np.arange(HD) + HD * h for pair in HEADS2 for h in pair])

    w_in = i["w_in"][0]
    z1 = []
    for t in range(DT):
        z1 += [np.arange(P) + D + t * P, np.arange(P) + t * P]
    z1 = np.concatenate(z1 + [2 * D + order1, np.arange(3 * D, 3 * D + 512)])
    gate1 = np.arange(3 * D + 512, 5 * D + 512)
    w2 = i["w_in_2"][0]
    at = np.cumsum([0, 512, 512, 512, 64, 64, 512, 512, 128, 128, 512, 512, 512, 3072])
    rng = lambda a, b: np.arange(at[a], at[b])
    rwkv = rng(0, 6)
    sw = np.concatenate([at[6] + order2, rng(7, 9), at[9] + order2])
    xq = rng(10, 12)
    proj = [i["w_proj_a_2"][0], i["w_proj_b_2"][0][order2], i["w_proj_c_2"][0]]
    merge, beside = [], [unit_columns(w2, sw), unit_columns(w2, xq)]
    gates = [unit_columns(w2, at[12] + D * b + np.arange(D)) for b in range(3)]
    proj = [unit_columns(m, None) for m in proj]
    for f in range(0, DT, 2):
        for b in range(3):
            merge.append(np.concatenate([proj[b][f], proj[b][f + 1]], 1)[None])
            beside.append(gates[b][f:f + 2])
    beside = np.concatenate(beside)
    rows_of = lambda m: m.reshape(DT, P, D)
    weights = np.concatenate([
        full(unit_columns(w_in, z1)), full(unit_columns(w_in, gate1)), full(unit_columns(i["conv_w_pw"][0], None)),
        full(unit_columns(i["attn_w_o"][0][order1], None)), rows_of(i["w_out"][0]),
        full(unit_columns(i["peer_w_query"][0], None)), full(unit_columns(w2, rwkv)),
        full(beside[:FILL2_BEFORE_MEM]), full(unit_columns(i["w_mem_kv_2"][0], None)), full(beside[FILL2_BEFORE_MEM:]),
        *[full(m) for m in merge], rows_of(i["w_out_2"][0])], 0)
    const1, const2, inv = constants()
    two = lambda v: np.concatenate([v, v])[:, None]
    cols1 = np.concatenate([col(i["norm1_g"][0]), col(i["conv_dw_w"][0]), col(i["conv_dw_b"][0]),
                            col(i["conv_ln_g"][0]), col(i["conv_ln_b"][0]), rep(i["attn_sink"][0])], 1)
    cols2 = np.concatenate([
        col(i["norm_g_2"][0]), col(i["mem_norm_g_2"][0]), col(i["mu_rkv_2"][0]), i["mu_wa_2"][0].reshape(P, 1),
        col(i["a0_2"][0]), col(i["k_k_2"][0]), col(i["k_a_2"][0]), col(i["r_k_2"][0]), col(i["lnx_g_2"][0]),
        col(i["lnx_b_2"][0]), two(i["q_norm_g_2"][0]), two(i["k_norm_g_2"][0]), i["xq_norm_g_2"][0][:, None],
        i["xk_norm_g_2"][0][:, None], inv, rep(i["sinks_2"][0])], 1)
    a = dict(x=i["x"][0], weights=weights.reshape(-1, P, DT * P), cols1=cols1, cols2=cols2, const1=const1, const2=const2,
             rows1=np.concatenate([rep(i["norm2_g"][0]), rep(i["final_g"])], 1), rows2=rep(i["w0_2"][0]),
             subkeys=i["peer_sub_keys"][0].transpose(2, 0, 1), peer_u=i["peer_u"][0], peer_v=i["peer_v"][0],
             mem=i["mem_2"][0], lora=np.concatenate([i["w2_2"][0], i["a2_2"][0]], 0),
             positions=np.broadcast_to(i["positions_2"].reshape(1, T), (P, T)))
    return {k: np.ascontiguousarray(v) for k, v in a.items()}


def kernel(**inputs):
    import concourse.bacc as bacc
    from concourse.bass_utils import run_bass_kernel_spmd

    arrays = lay_out(inputs)
    nc = bacc.Bacc("TRN2", target_bir_lowering=False, num_devices=1)
    a = {k: nc.dram_tensor(f"in_{k}", v.shape, mybir.dt.from_np(v.dtype), kind="ExternalInput").ap()
         for k, v in arrays.items()}
    out = nc.dram_tensor("out", (T, D), F32, kind="ExternalOutput").ap()
    program(nc, a, out)
    r = run_bass_kernel_spmd(nc, [{f"in_{k}": v for k, v in arrays.items()}], core_ids=[0])
    return r.results[0]["out"].reshape(1, T, D)
```

```python
from contextlib import ExitStack
from itertools import zip_longest

import numpy as np

import concourse.bass as bass
from concourse import mybir

F32 = mybir.dt.float32
F32R = mybir.dt.float32r
U32 = mybir.dt.uint32
I32 = mybir.dt.int32
ALU = mybir.AluOpType
ACT = mybir.ActivationFunctionType
AXX = mybir.AxisListType.X

P = 128
T = 512
TT = T // P
D = 1024
DT = D // P
TAPS = 31
PAD = TAPS // 2
EPS = 1e-6
RING = 4

H1, KV1, HD = 16, 4, 64
SLOPES = [2.0 ** (-8.0 * (h + 1) / H1) for h in range(H1)]
FAR = 1e33
PH, TOPK, NKEYS = 8, 16, 128
PICKS = PH * TOPK

MEM = 256
LNX_EPS = 64e-5
DECAY = float(np.exp(-0.5))
CH = 64
LEVELS = 6

HEADS1 = [[4 * (2 * (i // 4) + e) + i % 4 for e in range(2)] for i in range(8)]
HEADS2 = [[i, 4 + i] for i in range(4)]

COLS1 = dict(norm1=8, conv_w=TAPS * 8, conv_b=8, ln_g=8, ln_b=8, sink=16)
COLS2 = dict(norm=8, memnorm=8, mu=13, a0=4, k_k=4, k_a=4, r_k=4, lnx_g=4, lnx_b=4, q_g=1, k_g=1,
             xq_g=1, xk_g=1, inv=1, sinks=8)
CONST1 = dict(ident=P, ones=P, dist=3 * P, iota=TOPK * TOPK)
CONST2 = dict(ident=P, ones=P, halves=P, swap=P, band=2 * P, strict=P, incl=P, level=LEVELS * P, eye2=CH)

FILL1, FILL2 = 24, 46
FILL2_BEFORE_MEM = 40
UNITS = [("z1", 28), ("fill1", FILL1), ("wo", 8), ("wout1", 8), ("query", 16), ("rwkv", 13), ("fill2", FILL2_BEFORE_MEM),
         ("mem", 8), ("fill2_rest", FILL2 - FILL2_BEFORE_MEM), ("merge", 12), ("wout2", 8)]


def first_unit(name):
    at = 0
    for n, count in UNITS:
        if n == name:
            return at
        at += count
    return at


TOTAL = sum(n for _, n in UNITS)


def offsets(widths):
    at, out = 0, {}
    for name, w in widths.items():
        out[name] = (at, at + w)
        at += w
    return out, at


class Columns:

    def __init__(self, tensor, widths):
        self.tensor, (self.at, self.width) = tensor, offsets(widths)

    def __call__(self, name, i=0, n=1):
        a = self.at[name][0] + i
        return self.tensor[:, a:a + n]

    def whole(self, name):
        a, b = self.at[name]
        return self.tensor[:, a:b]


class Chain:

    def __init__(self, eng, sem):
        self.eng, self.sem, self.count = eng, sem, 0

    def __call__(self, ins):
        self.count += 1
        ins.then_inc(self.sem, 1)
        self.eng.wait_ge(self.sem, self.count)


class Split:

    def __init__(self, high, low):
        self.high, self.low = high, low

    def __getitem__(self, at):
        return self.high[at].bitcast(F32R), self.low[at].bitcast(F32R)

    @property
    def width(self):
        return self.high.shape[-1]


def placed(nc, ctx, name, shape):
    tensor = ctx.enter_context(nc.sbuf_tensor(name, shape, F32))
    return tensor, nc.sbuf_base - 4 * int(np.prod(shape[1:]))


def same_place(nc, name, shape, offset):
    return nc.alloc_sbuf_tensor_at(name, shape, F32, offset=offset)


def split_tensor(nc, ctx, name, shape):
    high = ctx.enter_context(nc.sbuf_tensor(f"{name}_high", shape, F32))
    whole, offset = placed(nc, ctx, f"{name}_whole", shape)
    split = Split(high, same_place(nc, f"{name}_low", shape, offset))
    split.whole = whole
    return split


def product(nc, to, left, right, start, stop):
    nc.tensor.matmul(to, left[0], right[0], start=start, stop=False)
    nc.tensor.matmul(to, left[0], right[1], start=False, stop=False)
    return nc.tensor.matmul(to, left[1], right[0], start=False, stop=stop)


class Weights:

    def __init__(self, nc, ctx, dram):
        self.nc, self.dram = nc, dram
        self.ring, offset = placed(nc, ctx, "weight_ring", [P, RING, DT, P])
        self.low = same_place(nc, "weight_low", [P, RING, DT, P], offset)
        self.high, self.high_offset = placed(nc, ctx, "weight_high", [P, 2, DT, P])
        self.arrived = [ctx.enter_context(nc.semaphore(f"weights_arrived{s}")) for s in range(RING)]
        self.high_ready = ctx.enter_context(nc.semaphore("weights_high_ready"))
        self.split = ctx.enter_context(nc.semaphore("weights_split"))
        self.done = ctx.enter_context(nc.semaphore("unit_done"))
        self.issued = self.highs = self.lows = 0

    def units(self, eng, start, upto, one):
        u, n = start, upto - start
        while u < RING and n > 0:
            one(u, 0)
            u, n = u + 1, n - 1
        if n >= 2 * RING:
            with eng.Fori(0, n // RING) as i:
                for j in range(RING):
                    one(u + j, i)
            u, n = u + n // RING * RING, n % RING
        for j in range(n):
            one(u + j, 0)

    def load(self, sp, upto):
        upto = max(min(upto, TOTAL), self.issued)

        def one(u, i):
            if u >= RING:
                sp.wait_ge(self.done, RING * i + (u - RING + 1))
            sp.dma_start(self.ring[:, u % RING], self.dram[u + RING * i]).then_inc(self.arrived[u % RING], 16)
        self.units(sp, self.issued, upto, one)
        self.issued = upto

    def high_part(self, act, u, i=0):
        if u < TOTAL:
            act.wait_ge(self.arrived[u % RING], 16 * i + 16 * (u // RING + 1))
            self.nc.scalar.activation(self.high[:, u % 2].bitcast(F32R), self.ring[:, u % RING], ACT.Copy
                                      ).then_inc(self.high_ready, 1)
            self.highs = u + 1

    def finished(self, act, u, i=0):
        act.wait_ge(self.done, RING * i + (u + 1))
        if not (isinstance(i, int) and 0 <= RING * i + u + 2 - first_unit("rwkv") < 2):
            self.high_part(act, u + 2, i)

    def low_parts(self, pool, upto=None):
        upto = self.highs if upto is None else min(upto, TOTAL)

        def one(u, i):
            slot = u % RING
            pool.wait_ge(self.high_ready, RING * i + (u + 1))
            self.nc.gpsimd.tensor_tensor(self.low[:, slot].bitcast(F32R), self.ring[:, slot], self.high[:, u % 2],
                                         ALU.subtract).then_inc(self.split, 1)
        self.units(pool, self.lows, upto, one)
        self.lows = self.highs = upto

    def wait(self, pe, u, i=0):
        pe.wait_ge(self.split, RING * i + (u + 1))
        return Split(self.high[:, u % 2], self.low[:, u % RING])


class Filler:

    def __init__(self, nc, st, w, banks, unit, items, store):
        self.nc, self.w, self.banks, self.unit, self.items, self.store = nc, w, banks, unit, items, store
        self.kept = st.sem("kept")
        self.stored = [st.sem(f"stored{i}") for i in range(2)]
        self.stage = st.sb("stage", [P, 2, T])
        self.step = self.taken = self.sent = self.early = self.before = 0
        self.limit = len(items)
        self.marks = []

    @property
    def done(self):
        return self.step // DT

    def pe(self, pe, steps):
        self.early = self.done
        for _ in range(min(steps, DT * self.limit - self.step)):
            n, k = divmod(self.step, DT)
            src = self.items[n][0]
            if k == 0:
                self.ring = self.w.wait(pe, self.unit(n))
                if n >= len(self.banks):
                    pe.wait_ge(self.kept, n - len(self.banks) + 1)
            mm = product(self.nc, self.banks[n % len(self.banks)][:], self.ring[:, k], src[:, k], k == 0, k == DT - 1)
            if k == DT - 1:
                mm.then_inc(self.w.done, 1)
            self.step += 1

    def mark(self):
        self.marks.append(self.done)

    def begin(self, act):
        self.act(act, self.before)

    def act(self, act, upto=None):
        if upto is None:
            upto = max(self.early, (self.step - 6) // DT)
        while self.taken < upto:
            n = self.taken
            _, func, scale = self.items[n]
            self.w.finished(act, self.unit(n))
            if n >= 2:
                act.wait_ge(self.stored[n % 2], 16 * (n // 2))
            self.nc.scalar.activation(self.stage[:, n % 2], self.banks[n % len(self.banks)][:], func, scale=scale).then_inc(self.kept, 1)
            self.taken += 1

    def sp(self, sp):
        while self.sent < self.taken:
            n = self.sent
            self.w.load(sp, self.unit(n) + RING + 1)
            sp.wait_ge(self.kept, n + 1)
            sp.dma_start(self.store[n], self.stage[:, n % 2]).then_inc(self.stored[n % 2], 16)
            self.sent += 1
        self.marks, self.before = [], self.done

    def wait_stored(self, sp):
        for i in range(2):
            sp.wait_ge(self.stored[i], 16 * ((self.sent + 1 - i) // 2))


def catch_up(nc, fill):
    with nc.Block() as block:
        @block.tensor
        def _(pe):
            fill.pe(pe, DT * FILL2)

        @block.scalar
        def _(act):
            fill.act(act, fill.done)

        @block.sync
        def _(sp):
            fill.sp(sp)
            fill.wait_stored(sp)

        @block.gpsimd
        def _(pool):
            fill.w.low_parts(pool)


def rounds(eng, n, body):
    body(0, True)
    if n > 1:
        with eng.Fori(1, n) as i:
            body(i, False)


class Stage:

    owner, free = None, []

    def __init__(self, nc, name):
        self.nc, self.name, self.ctx, self.sems = nc, name, ExitStack(), []
        if Stage.owner is not nc:
            Stage.owner, Stage.free = nc, list(nc.free_semaphores)

    def __enter__(self):
        self.ctx.__enter__()
        return self

    def __exit__(self, *e):
        if self.sems:
            numbers = [s.num for s in self.sems]
            self.nc.clear_and_free_semaphores(self.sems)
            Stage.free += numbers
        return self.ctx.__exit__(*e)

    def sb(self, name, shape, dt=F32):
        return self.ctx.enter_context(self.nc.sbuf_tensor(f"{self.name}_{name}", shape, dt))

    def sem(self, name):
        self.sems.append(self.nc.alloc_semaphore(name=f"{self.name}_{name}", num=Stage.free.pop(0)))
        return self.sems[-1]

    def block(self):
        return self.nc.Block()


def norm_to_T(nc, w, bank, name, x, tiles, gain, ident, xT, prefetch, scaled=None, row_gain=None, fill=None,
              steps=0):
    width = tiles * P
    per_bank = 512 // width

    def place(f):
        at = f % per_bank * width
        return bank[f // per_bank][:, at:at + width]

    def whole_bank(f):
        return (f // per_bank + 1) * per_bank

    with Stage(nc, name) as st:
        junk = st.sb("junk", [P, D])
        ss = st.sb("ss", [P, tiles])
        ms = st.sb("ms", [P, tiles])
        rms = st.sb("rms", [P, tiles])
        rstd = st.sb("rstd", [P, tiles])
        xn = scaled if scaled is not None else st.sb("xn", [P, tiles, D])
        squared, mean_ready, root_ready = st.sem("squared"), st.sem("mean_ready"), st.sem("root_ready")
        rstd_ready, normed, turned, kept = st.sem("rstd_ready"), st.sem("normed"), st.sem("turned"), st.sem("kept")
        with st.block() as block:
            @block.tensor
            def _(pe):
                if fill is not None:
                    fill.pe(pe, steps)
                pe.wait_ge(normed, tiles)
                for f in range(DT):
                    for t in range(tiles):
                        mm = nc.tensor.transpose(place(f)[:, t * P:(t + 1) * P], xn[:, t, f * P:(f + 1) * P], ident)
                    mm.then_inc(turned, 1)

            @block.scalar
            def _(act):
                for t in range(tiles):
                    if t:
                        act.wait_ge(squared, t)
                    nc.scalar.activation(junk[:], x[:, t], ACT.Square, accum_out=ss[:, t:t + 1]).then_inc(squared, 1)
                act.wait_ge(mean_ready, 1)
                nc.scalar.activation(rms[:], ms[:], ACT.Sqrt).then_inc(root_ready, 1)
                if fill is not None:
                    fill.act(act, fill.done)
                for f in range(DT):
                    act.wait_ge(turned, whole_bank(f))
                    scale = 1.0 if gain is None else gain[:, f:f + 1]
                    nc.scalar.activation(xT.high[:, f].bitcast(F32R), place(f), ACT.Copy, scale=scale
                                         ).then_inc(kept, 1)

            @block.vector
            def _(dve):
                dve.wait_ge(squared, tiles)
                nc.vector.tensor_scalar(ms[:], ss[:], 1.0 / D, EPS, ALU.mult, ALU.add).then_inc(mean_ready, 1)
                dve.wait_ge(root_ready, 1)
                nc.vector.reciprocal(rstd[:], rms[:]).then_inc(rstd_ready, 1)
                dve.wait_ge(rstd_ready, 1)
                for t in range(tiles):
                    if row_gain is None:
                        nc.vector.tensor_scalar(xn[:, t], x[:, t], rstd[:, t:t + 1], None, ALU.mult).then_inc(normed, 1)
                    else:
                        nc.vector.scalar_tensor_tensor(xn[:, t], x[:, t], rstd[:, t:t + 1], row_gain, ALU.mult,
                                                       ALU.mult).then_inc(normed, 1)
                for f in range(DT):
                    dve.wait_ge(kept, whole_bank(f))
                    nc.vector.scalar_tensor_tensor(xT.low[:, f].bitcast(F32R), place(f),
                                                   1.0 if gain is None else gain[:, f:f + 1], xT.high[:, f], ALU.mult,
                                                   ALU.subtract)

            @block.sync
            def _(sp):
                if fill is None:
                    w.load(sp, prefetch)
                else:
                    fill.sp(sp)

            @block.gpsimd
            def _(pool):
                if fill is not None:
                    w.low_parts(pool)


def attention(nc, bank, name, units, *, scale, sink, ident, out, group, dim,
              fill, fill_steps, out_low=None):
    B = 4
    n = len(units)
    width = max(u["k"].shape[-1] for u in units)
    per = P // dim
    with Stage(nc, name) as st:
        logit = st.sb("logit", [P, B, width])
        prob = st.sb("prob", [P, B, width])
        probT = st.sb("probT", [P, 2, width])
        diag = st.sb("diag", [P, B, P])
        top = st.sb("top", [P, B])
        negtop = st.sb("negtop", [P, B])
        total = st.sb("total", [P, B])
        sinkexp = st.sb("sinkexp", [P, B])
        full = st.sb("full", [P, B])
        recip = st.sb("recip", [P, B])
        scores_ready, biased, top_ready = st.sem("scores_ready"), st.sem("biased"), st.sem("top_ready")
        negtop_ready, exp_ready, full_ready = st.sem("negtop_ready"), st.sem("exp_ready"), st.sem("full_ready")
        recip_ready, diag_ready, turned = st.sem("recip_ready"), st.sem("diag_ready"), st.sem("turned")
        turned_kept, out_ready, out_kept = st.sem("turned_kept"), st.sem("out_ready"), st.sem("out_kept")
        high_kept = st.sem("high_kept")
        has_bias, has_sink = units[0]["bias"] is not None, sink is not None
        with st.block() as block:
            @block.tensor
            def _(pe):
                def scores(i):
                    if i >= 2:
                        pe.wait_ge(biased if has_bias else exp_ready, i - 1)
                        if not has_bias:
                            pe.wait_ge(top_ready, i - 1)
                    u = units[i]
                    nc.tensor.matmul(bank[i % 2][:, 0:u["k"].shape[-1]], u["q"], u["k"], start=True,
                                     stop=True).then_inc(scores_ready, 1)

                def turn(i):
                    pe.wait_ge(exp_ready, i + 1)
                    pe.wait_ge(diag_ready, i + 1)
                    if i >= 2:
                        pe.wait_ge(turned_kept, i - 1)
                    for c in range(len(units[i]["v"])):
                        mm = nc.tensor.matmul(bank[2 + i % 2][:, c * P:(c + 1) * P], prob[:, i % B, c * P:(c + 1) * P],
                                              diag[:, i % B], start=True, stop=True)
                    mm.then_inc(turned, 1)

                def values(i):
                    u, g = units[i], i // group
                    pe.wait_ge(turned_kept, i + 1)
                    if g >= 2:
                        pe.wait_ge(out_kept, g - 1)
                    at = u["half"] * dim
                    col = (i % group) // per * P
                    for c, v in enumerate(u["v"]):
                        mm = nc.tensor.matmul(bank[4 + g % 2][at:at + dim, col:col + P], v,
                                              probT[:, i % 2, c * P:(c + 1) * P], start=(c == 0),
                                              stop=(c == len(u["v"]) - 1))
                    mm.then_inc(out_ready, 1)

                for i in range(n + 5):
                    if i < n:
                        scores(i)
                    if 3 <= i < n + 3:
                        turn(i - 3)
                    if i >= 5:
                        values(i - 5)
                    fill.pe(pe, fill_steps)
                    fill.mark()

            @block.vector
            def _(dve):
                def maximum(i):
                    u, b = units[i], i % B
                    k = u["k"].shape[-1]
                    dve.wait_ge(scores_ready, i + 1)
                    if i >= B:
                        dve.wait_ge(exp_ready, i - B + 1)
                    src = bank[i % 2][:, 0:k]
                    if has_bias:
                        tile, coef = u["bias"]
                        nc.vector.scalar_tensor_tensor(logit[:, b, 0:k], tile, coef, src, ALU.mult,
                                                       ALU.add).then_inc(biased, 1)
                        yield
                        dve.wait_ge(biased, i + 1)
                        src = logit[:, b, 0:k]
                    nc.vector.tensor_reduce(top[:, b:b + 1], src, AXX, ALU.max).then_inc(top_ready, 1)
                    yield
                    dve.wait_ge(top_ready, i + 1)
                    if has_sink:
                        nc.vector.tensor_scalar(negtop[:, b:b + 1], top[:, b:b + 1], u["sink_scaled"], -scale, ALU.max,
                                                ALU.mult).then_inc(negtop_ready, 1)
                    else:
                        nc.vector.tensor_scalar(negtop[:, b:b + 1], top[:, b:b + 1], -scale, None,
                                                ALU.mult).then_inc(negtop_ready, 1)
                    yield

                def divisor(i):
                    b = i % B
                    dve.wait_ge(exp_ready, i + 1)
                    src = total[:, b:b + 1]
                    if has_sink:
                        nc.vector.tensor_tensor(full[:, b:b + 1], src, sinkexp[:, b:b + 1], ALU.add).then_inc(full_ready, 1)
                        yield
                        dve.wait_ge(full_ready, i + 1)
                        src = full[:, b:b + 1]
                    nc.vector.reciprocal(recip[:, b:b + 1], src).then_inc(recip_ready, 1)
                    yield
                    dve.wait_ge(recip_ready, i + 1)
                    if i >= B:
                        dve.wait_ge(turned, i - B + 1)
                    nc.vector.tensor_scalar(diag[:, b], ident, recip[:, b:b + 1], None, ALU.mult).then_inc(diag_ready, 1)
                    yield

                def keep(g):
                    dve.wait_ge(out_ready, group * (g + 1))
                    src = bank[4 + g % 2][:].rearrange("p (a t) -> p a t", t=P)[:, 0:group // per]
                    if out_low is None:
                        nc.vector.tensor_copy(out(g), src).then_inc(out_kept, 1)
                    else:
                        nc.vector.tensor_copy(out(g).bitcast(F32R), src).then_inc(high_kept, 1)
                        dve.wait_ge(high_kept, g + 1)
                        nc.vector.tensor_tensor(out_low(g).bitcast(F32R), src, out(g), ALU.subtract).then_inc(out_kept, 1)

                for i in range(n + 6):
                    rows = [maximum(i)] if i < n else []
                    if 2 <= i < n + 2:
                        rows.append(divisor(i - 2))
                    for _ in zip_longest(*rows):
                        pass
                    if i >= 6 and (i - 6) % group == group - 1:
                        keep((i - 6) // group)

            @block.scalar
            def _(act):
                def exps(i):
                    u, b = units[i], i % B
                    k = u["k"].shape[-1]
                    act.wait_ge(negtop_ready, i + 1)
                    if i >= B:
                        act.wait_ge(turned, i - B + 1)
                        act.wait_ge(recip_ready, i - B + 1)
                    if has_sink:
                        nc.scalar.activation(sinkexp[:, b:b + 1], u["sink"], ACT.Exp, bias=negtop[:, b:b + 1])
                    nc.scalar.activation(prob[:, b, 0:k], logit[:, b, 0:k] if has_bias else bank[i % 2][:, 0:k], ACT.Exp,
                                         bias=negtop[:, b:b + 1], scale=scale,
                                         accum_out=total[:, b:b + 1]).then_inc(exp_ready, 1)

                def keep(i):
                    k = units[i]["k"].shape[-1]
                    act.wait_ge(turned, i + 1)
                    if i >= 2:
                        act.wait_ge(out_ready, i - 1)
                    nc.scalar.activation(probT[:, i % 2, 0:k], bank[2 + i % 2][:, 0:k], ACT.Copy).then_inc(turned_kept, 1)

                for i in range(n + 4):
                    if i >= 4:
                        keep(i - 4)
                    if i < n:
                        exps(i)
                    if i:
                        fill.act(act, fill.marks[i - 1])
                fill.act(act)

            @block.sync
            def _(sp):
                fill.sp(sp)

            @block.gpsimd
            def _(pool):
                fill.w.low_parts(pool)


def turn_tiles(nc, w, bank, name, pairs, ident, prefetch):
    with Stage(nc, name) as st:
        turned, kept = st.sem("turned"), st.sem("kept")
        with st.block() as block:
            @block.sync
            def _(sp):
                w.load(sp, prefetch)

            @block.tensor
            def _(pe):
                for n, (sources, _) in enumerate(pairs):
                    if n >= 6:
                        pe.wait_ge(kept, n - 5)
                    for j, s in enumerate(sources):
                        mm = nc.tensor.transpose(bank[n % 6][:, j * P:(j + 1) * P], s, ident)
                    mm.then_inc(turned, 1)

            @block.scalar
            def _(act):
                for n, (sources, to) in enumerate(pairs):
                    act.wait_ge(turned, n + 1)
                    if n:
                        act.wait_ge(kept, n)
                    src = bank[n % 6][:, 0:len(sources) * P]
                    if len(to.shape) == 3:
                        src = src.rearrange("p (a t) -> p a t", a=to.shape[1])
                    nc.scalar.activation(to, src, ACT.Copy).then_inc(kept, 1)


def first_block(nc, w, bank, cols, const, rows, subkeys, peer_u, peer_v, x, dump):
    ident, ones = const.whole("ident"), const.whole("ones")
    with ExitStack() as outer:
        attnT = split_tensor(nc, outer, "attnT", [P, DT, T])
        z_store = nc.dram_tensor("z1_store", (FILL1, P, T), F32, kind="Internal").ap()
        with ExitStack() as inner:
            conv = split_tensor(nc, inner, "convT", [P, DT, T])
            convT = conv.whole
            qkvT = inner.enter_context(nc.sbuf_tensor("qkvT", [P, 12, T], F32))
            hT = split_tensor(nc, inner, "hT", [P, DT, T])
            norm_to_T(nc, w, bank, "norm1", x, TT, cols.whole("norm1"), ident, hT, first_unit("z1") + RING)
            fill = Filler(nc, inner.enter_context(Stage(nc, "fill1")), w, bank[6:8], lambda n: first_unit("fill1") + n,
                          [(hT, ACT.Tanh, 0.5)] * 16 + [(conv, ACT.Copy, 1.0)] * DT, z_store)
            project_first(nc, w, bank, cols, hT, qkvT, convT, fill)
            dump("conv", convT)
            dump("qkv", qkvT)
            conv_norm(nc, bank, cols, ones, conv, fill)
            v_tok = inner.enter_context(nc.sbuf_tensor("v_tok", [P, TT, KV1 * HD], F32))
            sink8 = inner.enter_context(nc.sbuf_tensor("sink8", [P, H1], F32))
            scale_sinks(nc, "sink1", sink8, cols.whole("sink"))
            turn_tiles(nc, w, bank, "turn_v",
                       [([qkvT[:, 10 + a, t * P:(t + 1) * P] for a in range(2)], v_tok[:, t]) for t in range(TT)],
                       ident, 0)
            units = []
            for b in range(TT):
                lo, hi = max(b - 1, 0), min(b + 2, TT)
                for i in range(8):
                    for e in range(2):
                        h = HEADS1[i][e]
                        a, part = i // 4, slice(e * HD, (e + 1) * HD)
                        kv = 2 * a + e
                        units.append(dict(
                            q=qkvT[part, i, b * P:(b + 1) * P], k=qkvT[part, 8 + a, lo * P:hi * P],
                            bias=(const.whole("dist")[:, (lo - b + 1) * P:(hi - b + 1) * P], -SLOPES[h] * HD ** 0.5),
                            v=[v_tok[:, c, kv * HD:(kv + 1) * HD] for c in range(lo, hi)],
                            sink=cols("sink", h), sink_scaled=sink8[:, h:h + 1], half=e))
            at = lambda g: (slice(None), slice(4 * (g % 2), 4 * (g % 2) + 4), slice((g // 2) * P, (g // 2 + 1) * P))
            attention(nc, bank, "attn1", units, scale=HD ** -0.5, sink=True, ident=ident,
                      out=lambda g: attnT.high[at(g)], out_low=lambda g: attnT.low[at(g)], group=8, dim=HD, fill=fill,
                      fill_steps=2)
            catch_up(nc, fill)
            assert fill.done == FILL1
        with ExitStack() as inner:
            mergedT = split_tensor(nc, inner, "mergedT", [P, DT, T])
            merge_first(nc, w, bank, z_store, attnT, mergedT)
            out_residual(nc, w, bank, "wout1", mergedT, x, first_unit("query") + RING, 0.5)
    dump("x1", x)
    with ExitStack() as inner:
        h2 = inner.enter_context(nc.sbuf_tensor("h2", [P, TT, D], F32))
        scores = inner.enter_context(nc.sbuf_tensor("scores", [P, TT, 2 * PH, NKEYS], F32))
        with ExitStack() as s:
            h2T = split_tensor(nc, s, "h2T", [P, DT, T])
            norm_to_T(nc, w, bank, "norm2", x, TT, None, ident, h2T, first_unit("query") + RING, scaled=h2,
                      row_gain=rows[:, 0:D])
            query_scores(nc, w, bank, h2T, subkeys, scores)
        dump("scores", scores)
        experts(nc, w, bank, const, ident, scores, h2, peer_u, peer_v, x)
    dump("x2", x)
    final_norm(nc, w, x, rows[:, D:2 * D])
    dump("y", x)


def scale_sinks(nc, name, to, sink):
    with Stage(nc, name) as st, st.block() as block:
        @block.vector
        def _(dve):
            nc.vector.tensor_scalar(to[:], sink, float(HD ** 0.5), None, ALU.mult)


def project_first(nc, w, bank, cols, hT, qkvT, convT, fill):
    with Stage(nc, "z1") as st:
        sig = st.sb("sig", [P, T])
        u = st.sb("u", [P, DT, T + 2 * PAD])
        sig_ready, z_kept = st.sem("sig_ready"), st.sem("z_kept")
        u0 = first_unit("z1")
        u_zero, gated, tap_done = st.sem("u_zero"), st.sem("gated"), st.sem("tap_done")
        with st.block() as block:
            @block.tensor
            def _(pe):
                def four_tiles(i):
                    for j in range(RING):
                        ring = w.wait(pe, u0 + j, i)
                        first = isinstance(i, int)
                        if j < 2:
                            if first and i == 1:
                                pe.wait_ge(gated, 1)
                            elif not first:
                                pe.wait_ge(z_kept, 2 * i + (j - 3))
                        elif not (first and i == 0):
                            pe.wait_ge(gated, i + 1)
                        for k in range(DT):
                            mm = product(nc, bank[j][:], ring[:, k], hT[:, k], k == 0, k == DT - 1)
                        mm.then_inc(w.done, 1)
                four_tiles(0)
                four_tiles(1)
                with pe.Fori(2, 28 // RING) as i:
                    four_tiles(i)
                fill.pe(pe, 88)

            @block.scalar
            def _(act):
                w.high_part(act, 0)
                w.high_part(act, 1)

                def gate(i, j, c):
                    w.finished(act, u0 + j, i)
                    if c is not None:
                        act.wait_ge(gated, c)
                    nc.scalar.activation(sig[:], bank[j][:], ACT.Sigmoid).then_inc(sig_ready, 1)
                    w.finished(act, u0 + j + 1, i)
                gate(0, 0, None)
                gate(0, 2, 1)
                with act.Fori(1, 28 // RING) as i:
                    for j in range(2):
                        w.finished(act, u0 + j, i)
                        nc.scalar.activation(qkvT[:, 2 * i + (j - 2)], bank[j][:], ACT.Copy).then_inc(z_kept, 1)
                    gate(i, 2, i + 1)
                fill.act(act)

            @block.sync
            def _(sp):
                w.load(sp, first_unit("fill1") + RING)
                fill.sp(sp)

            @block.gpsimd
            def _(pool):
                nc.gpsimd.memset(u[:, :, 0:PAD], 0.0).then_inc(u_zero, 1)
                nc.gpsimd.memset(u[:, :, T + PAD:T + 2 * PAD], 0.0).then_inc(u_zero, 1)
                w.low_parts(pool)

            @block.vector
            def _(dve):
                dve.wait_ge(u_zero, 2)
                for c in range(DT):
                    dve.wait_ge(w.done, u0 + (2 * c + 2 if c < 2 else RING * c))
                    dve.wait_ge(sig_ready, c + 1)
                    nc.vector.tensor_tensor(u[:, c, PAD:PAD + T], bank[3 if c else 1][:], sig[:], ALU.mult
                                            ).then_inc(gated, 1)
                    dve.wait_ge(gated, c + 1)
                    nc.vector.tensor_scalar(convT[:, c], u[:, c, 0:T], cols("conv_w", c), cols("conv_b", c), ALU.mult,
                                            ALU.add).then_inc(tap_done, 1)
                    for k in range(1, TAPS):
                        dve.wait_ge(tap_done, TAPS * c + k)
                        nc.vector.scalar_tensor_tensor(convT[:, c], u[:, c, k:k + T], cols("conv_w", k * DT + c),
                                                       convT[:, c], ALU.mult, ALU.add).then_inc(tap_done, 1)


def conv_norm(nc, bank, cols, ones, conv, fill):
    convT = conv.whole
    with Stage(nc, "convnorm") as st:
        mean = st.sb("mean", [P, T])
        sq = st.sb("sq", [P, DT, T])
        var = st.sb("var", [P, T])
        std = st.sb("std", [P, T])
        rstd = st.sb("rstd", [P, T])
        sum_ready, mean_ready, centred, squared = st.sem("sum_ready"), st.sem("mean_ready"), st.sem("centred"), st.sem("squared")
        var_ready, std_ready, rstd_ready, scaled, done = st.sem("var_ready"), st.sem("std_ready"), st.sem("rstd_ready"), st.sem("scaled"), st.sem("done")
        high_ready = st.sem("high_ready")
        with st.block() as block:
            @block.tensor
            def _(pe):
                for c in range(DT):
                    mm = nc.tensor.matmul(bank[0][:], ones, convT[:, c], start=(c == 0), stop=(c == DT - 1))
                mm.then_inc(sum_ready, 1)
                for c in range(DT):
                    pe.wait_ge(squared, c + 1)
                    mm = nc.tensor.matmul(bank[1][:], ones, sq[:, c], start=(c == 0), stop=(c == DT - 1))
                mm.then_inc(sum_ready, 1)
                fill.pe(pe, 26)

            @block.vector
            def _(dve):
                dve.wait_ge(sum_ready, 1)
                nc.vector.tensor_scalar(mean[:], bank[0][:], 1.0 / D, None, ALU.mult).then_inc(mean_ready, 1)
                dve.wait_ge(mean_ready, 1)
                for c in range(DT):
                    nc.vector.tensor_tensor(convT[:, c], convT[:, c], mean[:], ALU.subtract).then_inc(centred, 1)
                dve.wait_ge(sum_ready, 2)
                nc.vector.tensor_scalar(var[:], bank[1][:], 1.0 / D, EPS, ALU.mult, ALU.add).then_inc(var_ready, 1)
                dve.wait_ge(std_ready, 1)
                nc.vector.reciprocal(rstd[:], std[:]).then_inc(rstd_ready, 1)
                dve.wait_ge(rstd_ready, 1)
                for c in range(DT):
                    nc.vector.tensor_tensor(convT[:, c], convT[:, c], rstd[:], ALU.mult).then_inc(scaled, 1)
                for c in range(DT):
                    dve.wait_ge(done, c + 1)
                    nc.vector.tensor_copy(conv.high[:, c].bitcast(F32R), convT[:, c]).then_inc(high_ready, 1)
                    dve.wait_ge(high_ready, c + 1)
                    nc.vector.tensor_tensor(conv.low[:, c].bitcast(F32R), convT[:, c], conv.high[:, c], ALU.subtract)

            @block.scalar
            def _(act):
                fill.begin(act)
                for c in range(DT):
                    act.wait_ge(centred, c + 1)
                    nc.scalar.activation(sq[:, c], convT[:, c], ACT.Square).then_inc(squared, 1)
                act.wait_ge(var_ready, 1)
                nc.scalar.activation(std[:], var[:], ACT.Sqrt).then_inc(std_ready, 1)
                for c in range(DT):
                    act.wait_ge(scaled, c + 1)
                    nc.scalar.activation(convT[:, c], convT[:, c], ACT.Silu, bias=cols("ln_b", c),
                                         scale=cols("ln_g", c)).then_inc(done, 1)
                fill.act(act)

            @block.sync
            def _(sp):
                fill.sp(sp)

            @block.gpsimd
            def _(pool):
                fill.w.low_parts(pool)


def split_merged(nc, dve, mergedT, f, high_ready):
    nc.vector.tensor_copy(mergedT.high[:, f].bitcast(F32R), mergedT.whole[:, f]).then_inc(high_ready, 1)
    dve.wait_ge(high_ready, f + 1)
    nc.vector.tensor_tensor(mergedT.low[:, f].bitcast(F32R), mergedT.whole[:, f], mergedT.high[:, f], ALU.subtract)


def merge_first(nc, w, bank, z_store, attnT, mergedT):
    with Stage(nc, "merge1") as st:
        z = st.sb("z", [P, 3, 3, T])
        part = st.sb("part", [P, 2, 2, T])
        z_arrived = [st.sem(f"z_arrived{i}") for i in range(3)]
        conv_gated, gated, merged, high_ready = (st.sem(n) for n in ("conv_gated", "gated", "merged", "high_ready"))
        u0 = first_unit("wo")
        tiles = z_store.rearrange("(b f) p t -> f p b t", b=3)
        with st.block() as block:
            @block.sync
            def _(sp):
                for f in range(DT):
                    if f >= 3:
                        sp.wait_ge(conv_gated, f - 2)
                        sp.wait_ge(gated, f - 2)
                    sp.dma_start(z[:, f % 3], tiles[f]).then_inc(z_arrived[f % 3], 16)
                    w.load(sp, u0 + RING + max(f - 1, 0))
                w.load(sp, first_unit("wout1") + RING)

            @block.tensor
            def _(pe):
                for n in range(DT):
                    ring = w.wait(pe, u0 + n)
                    if n >= RING:
                        pe.wait_ge(gated, n - RING + 1)
                    for k in range(DT):
                        mm = product(nc, bank[n % RING][:], ring[:, k], attnT[:, k], k == 0, k == DT - 1)
                    mm.then_inc(w.done, 1)

            @block.scalar
            def _(act):
                for n in range(DT):
                    w.finished(act, u0 + n)

            @block.gpsimd
            def _(pool):
                w.low_parts(pool)

            @block.vector
            def _(dve):
                for f in range(DT):
                    dve.wait_ge(z_arrived[f % 3], 16 * (f // 3 + 1))
                    if f >= 2:
                        dve.wait_ge(merged, f - 1)
                    nc.vector.scalar_tensor_tensor(part[:, f % 2, 0], z[:, f % 3, 0], 1.0, z[:, f % 3, 2], ALU.add,
                                                   ALU.mult).then_inc(conv_gated, 1)
                    dve.wait_ge(w.done, u0 + f + 1)
                    nc.vector.scalar_tensor_tensor(part[:, f % 2, 1], z[:, f % 3, 1], 1.0, bank[f % RING][:], ALU.add,
                                                   ALU.mult).then_inc(gated, 1)
                    dve.wait_ge(conv_gated, f + 1)
                    dve.wait_ge(gated, f + 1)
                    nc.vector.tensor_tensor(mergedT.whole[:, f], part[:, f % 2, 0], part[:, f % 2, 1], ALU.add
                                            ).then_inc(merged, 1)
                    dve.wait_ge(merged, f + 1)
                    split_merged(nc, dve, mergedT, f, high_ready)


def out_residual(nc, w, bank, name, mergedT, x, prefetch, scale, store=None):
    with Stage(nc, name) as st:
        ready, added, stored = st.sem("ready"), st.sem("added"), st.sem("stored")
        u0 = first_unit(name)
        with st.block() as block:
            @block.sync
            def _(sp):
                w.load(sp, prefetch)
                if store is not None:
                    for t in range(TT):
                        sp.wait_ge(added, 2 * t + 2)
                        sp.dma_start(store[t * P:(t + 1) * P, :], x[:, t]).then_inc(stored, 16)
                    sp.wait_ge(stored, 16 * TT)

            @block.tensor
            def _(pe):
                for k in range(DT):
                    ring = w.wait(pe, u0 + k)
                    for t in range(TT):
                        for e in range(2):
                            mm = product(nc, bank[2 * t + e][:], mergedT[:, k, t * P:(t + 1) * P],
                                         ring[:, 4 * e:4 * e + 4], k == 0, k == DT - 1)
                            if k == DT - 1 and (t, e) != (TT - 1, 1):
                                mm.then_inc(ready, 1)
                    mm.then_inc(w.done, 1)

            @block.scalar
            def _(act):
                for k in range(DT):
                    w.finished(act, u0 + k)

            @block.gpsimd
            def _(pool):
                w.low_parts(pool)

            @block.vector
            def _(dve):
                for n in range(2 * TT):
                    t, e = n // 2, n % 2
                    if n < 2 * TT - 1:
                        dve.wait_ge(ready, n + 1)
                    else:
                        dve.wait_ge(w.done, u0 + DT)
                    part = x[:, t, e * 512:(e + 1) * 512]
                    nc.vector.scalar_tensor_tensor(part, bank[n][:], scale, part, ALU.mult, ALU.add).then_inc(added, 1)


def query_scores(nc, w, bank, h2T, subkeys, scores):
    with Stage(nc, "query") as st:
        queryT = st.sb("queryT", [P, RING, T])
        query_kept = st.sem("query_kept")
        u0 = first_unit("query")
        scored, score_kept = st.sem("scored"), st.sem("score_kept")
        with st.block() as block:
            @block.sync
            def _(sp):
                w.load(sp, first_unit("rwkv") + RING)

            @block.tensor
            def _(pe):
                def four_tiles(i, first):
                    for j in range(RING):
                        ring = w.wait(pe, u0 + j, i)
                        if not first:
                            pe.wait_ge(query_kept, i * RING + (j - RING + 1))
                        for k in range(DT):
                            mm = product(nc, bank[j][:], ring[:, k], h2T[:, k], k == 0, k == DT - 1)
                        mm.then_inc(w.done, 1)
                    for j in range(RING):
                        pe.wait_ge(query_kept, i * RING + (j + 1))
                        if not first:
                            pe.wait_ge(score_kept, i * RING + (j - RING + 1))
                        for t in range(TT):
                            mm = nc.tensor.matmul(bank[4 + j][:, t * P:(t + 1) * P], queryT[:, j, t * P:(t + 1) * P],
                                                  subkeys[:, j % 2], start=True, stop=True)
                        mm.then_inc(scored, 1)
                rounds(pe, 4, four_tiles)

            @block.scalar
            def _(act):
                def four_tiles(i, first):
                    for j in range(RING):
                        w.finished(act, u0 + j, i)
                        if not first:
                            act.wait_ge(scored, i * RING + (j - RING + 1))
                        nc.scalar.activation(queryT[:, j], bank[j][:], ACT.Copy).then_inc(query_kept, 1)
                rounds(act, 3, four_tiles)
                four_tiles(3, False)

            @block.gpsimd
            def _(pool):
                w.low_parts(pool, first_unit("rwkv"))

            @block.vector
            def _(dve):
                for n in range(16):
                    dve.wait_ge(scored, n + 1)
                    nc.vector.tensor_copy(scores[:, :, n], bank[4 + n % RING][:].rearrange("p (t n) -> p t n", t=TT)
                                          ).then_inc(score_kept, 1)


HEADS = TT * PH
GROUP = 4


def is_first(n, bound=1):
    return isinstance(n, int) and n < bound


def head_rounds(eng, body):
    def pair(i):
        for b in range(2):
            body(2 * i + b, b)
    pair(0)
    with eng.Fori(1, HEADS // 2 - 1) as i:
        pair(i)
    pair(HEADS // 2 - 1)


def experts(nc, w, bank, const, ident, scores, h2, peer_u, peer_v, x):
    HALF = TOPK // 2
    with Stage(nc, "peer") as st:
        ubuf = st.sb("ubuf", [P, 2 * GROUP, D])
        vbuf = st.sb("vbuf", [P, TOPK, D])
        junk = st.sb("junk", [P, D])
        sc = st.sb("sc", [P, 2, 2, NKEYS])
        index = st.sb("index", [P, 2, TOPK], I32)
        dots, gelu, weight = (st.sb(n, [P, TOPK]) for n in ("dots", "gelu", "weight"))
        diag = same_place(nc, "peer_diag", [P, TOPK, P], w.high_offset)
        best, wheref, rcf, key = (st.sb(n, [P, 2, TOPK]) for n in ("best", "wheref", "rcf", "key"))
        where, rc = (st.sb(n, [P, 2, TOPK], U32) for n in ("where", "rc"))
        left = st.sb("left", [P, NKEYS])
        hot = st.sb("hot", [P, 2, TOPK, TOPK])
        pair, pairleft = hot[:, 0], hot[:, 1].rearrange("p a b -> p (a b)")
        top = st.sb("top", [P, TOPK])
        pos = st.sb("pos", [P, TOPK], U32)
        e, s, r = st.sb("e", [P, 2, TOPK]), st.sb("s", [P, 2]), st.sb("r", [P, 2])
        choice_open = st.sem("choice_open")
        scores_ready, step_done, index_ready = st.sem("scores_ready"), st.sem("step_done"), st.sem("index_ready")
        shifted, exped, recip_ready, gathers_open = (st.sem(n) for n in ("shifted", "exped", "recip_ready", "gathers_open"))
        u_arrived = [st.sem(f"u_arrived{q}") for q in range(2)]
        v_arrived = [st.sem(f"v_arrived{q}") for q in range(2)]
        dot_done, gelu_done, weight_ready = st.sem("dot_done"), st.sem("gelu_done"), st.sem("weight_ready")
        diag_ready, summed, added = st.sem("diag_ready"), st.sem("summed"), st.sem("added")
        iota = const.whole("iota").rearrange("p (a b) -> p a b", a=TOPK)
        score_heads = scores[:].rearrange("p t (h e) k -> p (t h) e k", e=2)

        with st.block() as block:
            @block.gpsimd
            def _(pool):
                def head(n, b):
                    pool.wait_ge(index_ready, n + 1)
                    for half in range(2):
                        for q in (2 * half, 2 * half + 1):
                            if not (is_first(n) and q < 2):
                                pool.wait_ge(dot_done, TOPK * n + GROUP * (q - 1))
                            pool.sem_inc(gathers_open, 1)
                            for k in range(GROUP):
                                col = index[:, b, q * GROUP + k:q * GROUP + k + 1]
                                pool.indirect_dma_start(ubuf[:, q % 2 * GROUP + k], None, peer_u,
                                                        bass.IndirectOffsetOnAxis(col, 0)).then_inc(u_arrived[q % 2], 16)
                        for q in (2 * half, 2 * half + 1):
                            if not is_first(n):
                                pool.wait_ge(summed, 4 * n + (q - 3))
                            pool.sem_inc(gathers_open, 1)
                            for k in range(q * GROUP, (q + 1) * GROUP):
                                pool.indirect_dma_start(vbuf[:, k], None, peer_v,
                                                        bass.IndirectOffsetOnAxis(index[:, b, k:k + 1], 0)
                                                        ).then_inc(v_arrived[half], 16)
                head_rounds(pool, head)

            @block.vector
            def _(dve):
                def choose(n, b):
                    count = 0

                    def do(ins):
                        nonlocal count
                        count += 1
                        ins.then_inc(step_done, 1)
                        dve.wait_ge(step_done, count)

                    def top16(src, rest, vals, idx):
                        do(nc.vector.max(vals[:, 0:8], src))
                        do(nc.vector.max_index(idx[:, 0:8], vals[:, 0:8], src))
                        do(nc.vector.match_replace(rest, vals[:, 0:8], src, -3.0e38))
                        do(nc.vector.max(vals[:, 8:16], rest))
                        do(nc.vector.max_index(idx[:, 8:16], vals[:, 8:16], rest))

                    wide = [P, 2, TOPK, TOPK]
                    dve.wait_ge(scores_ready, n + 1)
                    dve.sem_inc(choice_open, 1)
                    dve.sem_clear(step_done)
                    for half in range(2):
                        top16(sc[:, b, half], left[:], best[:, half], where[:, half])
                    do(nc.vector.tensor_tensor(pair, best[:, 0].unsqueeze(2).broadcast_to([P, TOPK, TOPK]),
                                               best[:, 1].unsqueeze(1).broadcast_to([P, TOPK, TOPK]), ALU.add))
                    top16(pair.rearrange("p a b -> p (a b)"), pairleft, top[:], pos[:])
                    nc.vector.tensor_scalar(rc[:, 0], pos[:], 4, None, ALU.logical_shift_right)
                    nc.vector.tensor_copy(wheref[:], where[:])
                    do(nc.vector.tensor_scalar(rc[:, 1], pos[:], 15, None, ALU.bitwise_and))
                    do(nc.vector.tensor_copy(rcf[:], rc[:]))
                    do(nc.vector.tensor_tensor(hot[:], rcf[:].unsqueeze(3).broadcast_to(wide),
                                               iota.unsqueeze(1).broadcast_to(wide), ALU.is_equal))
                    do(nc.vector.tensor_tensor(hot[:], hot[:], wheref[:].unsqueeze(2).broadcast_to(wide), ALU.mult))
                    do(nc.vector.tensor_reduce(key[:], hot[:], AXX, ALU.add))
                    if not is_first(n, 2):
                        for q in range(2):
                            dve.wait_ge(u_arrived[q], 16 * HALF * n - 16 * HALF)
                            dve.wait_ge(v_arrived[q], 16 * HALF * n - 16 * HALF)
                        dve.wait_ge(weight_ready, n - 1)
                    nc.vector.scalar_tensor_tensor(index[:, b], key[:, 0], float(NKEYS), key[:, 1], ALU.mult,
                                                   ALU.add).then_inc(index_ready, 1)
                    nc.vector.tensor_scalar(e[:, b], top[:], top[:, 0:1], None, ALU.subtract).then_inc(shifted, 1)
                    dve.wait_ge(exped, n + 1)
                    nc.vector.reciprocal(r[:, b:b + 1], s[:, b:b + 1]).then_inc(recip_ready, 1)

                def add(n, t, b):
                    dve.wait_ge(summed, 4 * n + 4)
                    if not is_first(n):
                        dve.wait_ge(added, 2 * n)
                    for c in range(2):
                        part = x[:, t, c * 512:(c + 1) * 512]
                        nc.vector.tensor_tensor(part, bank[2 * b + c][:], part, ALU.add).then_inc(added, 1)

                def head(n, b):
                    t = n // PH
                    for q in range(4):
                        dve.wait_ge(u_arrived[q % 2], 16 * HALF * n + 16 * GROUP * (q // 2 + 1))
                        if q == 0 and not is_first(n):
                            dve.wait_ge(gelu_done, n)
                        for k in range(GROUP):
                            if not (is_first(n) and q + k == 0):
                                dve.wait_ge(dot_done, TOPK * n + (GROUP * q + k))
                            nc.vector.scalar_tensor_tensor(junk[:], ubuf[:, q % 2 * GROUP + k], 1.0, h2[:, t], ALU.mult,
                                                           ALU.mult, accum_out=dots[:, GROUP * q + k:GROUP * q + k + 1]
                                                           ).then_inc(dot_done, 1)
                    dve.wait_ge(gelu_done, n + 1)
                    dve.wait_ge(recip_ready, n + 1)
                    if not is_first(n):
                        dve.wait_ge(diag_ready, TOPK * n)
                    nc.vector.scalar_tensor_tensor(weight[:], gelu[:], r[:, b:b + 1], e[:, b], ALU.mult, ALU.mult
                                                   ).then_inc(weight_ready, 1)
                    if not is_first(n):
                        add(n - 1, (n - 1) // PH, 1 - b)
                    if not (isinstance(n, int) and n + 2 >= HEADS):
                        choose(n + 2, b)

                choose(0, 0)
                choose(1, 1)
                head_rounds(dve, head)
                add(HEADS - 1, TT - 1, 1)

            @block.scalar
            def _(act):
                def copy_scores(n, b):
                    if not is_first(n, 2):
                        act.wait_ge(index_ready, n - 1)
                    nc.scalar.activation(sc[:, b], score_heads[:, n], ACT.Copy).then_inc(scores_ready, 1)

                def exps(n, b):
                    act.wait_ge(shifted, n + 1)
                    if not is_first(n, 2):
                        act.wait_ge(recip_ready, n - 1)
                    nc.scalar.activation(e[:, b], e[:, b], ACT.Exp, accum_out=s[:, b:b + 1]).then_inc(exped, 1)

                def head(n, b):
                    if not (isinstance(n, int) and n + 2 >= HEADS):
                        copy_scores(n + 2, b)
                    act.wait_ge(dot_done, TOPK * n + TOPK)
                    if not is_first(n):
                        act.wait_ge(weight_ready, n)
                    nc.scalar.activation(gelu[:], dots[:], ACT.Gelu).then_inc(gelu_done, 1)
                    act.wait_ge(weight_ready, n + 1)
                    for k in range(TOPK):
                        if not is_first(n) and k % GROUP == 0:
                            act.wait_ge(summed, 4 * n + (k // GROUP - 3))
                        nc.scalar.activation(diag[:, k], ident, ACT.Copy, scale=weight[:, k:k + 1]).then_inc(diag_ready, 1)
                    if not (isinstance(n, int) and n + 2 >= HEADS):
                        exps(n + 2, b)

                copy_scores(0, 0)
                copy_scores(1, 1)
                exps(0, 0)
                exps(1, 1)
                head_rounds(act, head)

            @block.tensor
            def _(pe):
                def head(n, b):
                    if not is_first(n, 2):
                        pe.wait_ge(added, 2 * n - 2)
                    for half in range(2):
                        pe.wait_ge(v_arrived[half], 16 * HALF * n + 16 * HALF)
                        for k in range(half * HALF, (half + 1) * HALF):
                            pe.wait_ge(diag_ready, TOPK * n + (k + 1))
                            for c in range(2):
                                mm = nc.tensor.matmul(bank[2 * b + c][:], diag[:, k], vbuf[:, k, c * 512:(c + 1) * 512],
                                                      start=(k == 0), stop=(k == TOPK - 1))
                            if k % GROUP == GROUP - 1:
                                mm.then_inc(summed, 1)
                head_rounds(pe, head)


def final_norm(nc, w, x, gain):
    with Stage(nc, "final") as st:
        junk = st.sb("junk", [P, D])
        ss, ms, rms, rstd = (st.sb(n, [P, TT]) for n in ("ss", "ms", "rms", "rstd"))
        squared, mean_ready, root_ready = st.sem("squared"), st.sem("mean_ready"), st.sem("root_ready")
        rstd_ready, normed = st.sem("rstd_ready"), st.sem("normed")
        with st.block() as block:
            @block.scalar
            def _(act):
                for t in range(TT):
                    if t:
                        act.wait_ge(squared, t)
                    nc.scalar.activation(junk[:], x[:, t], ACT.Square, accum_out=ss[:, t:t + 1]).then_inc(squared, 1)
                act.wait_ge(mean_ready, 1)
                nc.scalar.activation(rms[:], ms[:], ACT.Sqrt).then_inc(root_ready, 1)

            @block.vector
            def _(dve):
                dve.wait_ge(squared, TT)
                nc.vector.tensor_scalar(ms[:], ss[:], 1.0 / D, EPS, ALU.mult, ALU.add).then_inc(mean_ready, 1)
                dve.wait_ge(root_ready, 1)
                nc.vector.reciprocal(rstd[:], rms[:]).then_inc(rstd_ready, 1)
                dve.wait_ge(rstd_ready, 1)
                for t in range(TT):
                    nc.vector.scalar_tensor_tensor(x[:, t], x[:, t], rstd[:, t:t + 1], gain, ALU.mult,
                                                   ALU.mult).then_inc(normed, 1)


def project_tiles(nc, w, bank, name, unit, count, src, takers, prefetch, loads=()):
    width = src.width
    with Stage(nc, name) as st:
        kept, loaded = st.sem("kept"), st.sem("loaded")
        u0 = first_unit(unit)
        with st.block() as block:
            @block.sync
            def _(sp):
                for to, of in loads:
                    sp.dma_start(to, of).then_inc(loaded, 16)
                w.load(sp, prefetch)
                if loads:
                    sp.wait_ge(loaded, 16 * len(loads))

            @block.tensor
            def _(pe):
                def four_tiles(i, first, count=RING):
                    for j in range(count):
                        ring = w.wait(pe, u0 + j, i)
                        if not first:
                            pe.wait_ge(kept, i * RING + (j - RING + 1))
                        for k in range(DT):
                            mm = product(nc, bank[j][:, 0:width], ring[:, k], src[:, k], k == 0, k == DT - 1)
                        mm.then_inc(w.done, 1)
                rounds(pe, count // RING, four_tiles)
                if count % RING:
                    four_tiles(count // RING, False, count % RING)

            @block.scalar
            def _(act):
                if unit == "rwkv":
                    w.high_part(act, u0)
                    w.high_part(act, u0 + 1)
                for n in range(count):
                    func, to = takers[n]
                    w.finished(act, u0 + n)
                    nc.scalar.activation(to, bank[n % RING][:, 0:width], func).then_inc(kept, 1)

            @block.gpsimd
            def _(pool):
                w.low_parts(pool)


def group_sums(nc, to, tile, selector):
    n = selector.shape[-1]
    for t in range(tile.shape[-1] // P):
        mm = nc.tensor.matmul(to[:, t * n:(t + 1) * n], tile[:, t * P:(t + 1) * P], selector, start=True, stop=True)
    return mm


def spread(nc, to, narrow, n, ident):
    per = P // n
    for t in range(narrow.shape[-1] // n):
        for g in range(n):
            mm = nc.tensor.matmul(to[g * per:(g + 1) * per, t * P:(t + 1) * P],
                                  narrow[:, t * n + g:t * n + g + 1].broadcast_to([P, per]), ident, start=True, stop=True)
    return mm


def rms_over_partitions(nc, bank, name, tiles, gains, selector, ident, fill, steps):
    width, n = tiles[0].shape[-1], selector.shape[-1]
    columns = width // P * n
    with Stage(nc, name) as st:
        sq = st.sb("sq", [P, len(tiles), width])
        ms, root, rstd = (st.sb(k, [P, len(tiles) * columns]) for k in ("ms", "root", "rstd"))
        squared, summed, mean_ready, root_ready, rstd_ready, spread_ready, normed = (st.sem(k) for k in (
            "squared", "summed", "mean_ready", "root_ready", "rstd_ready", "spread_ready", "normed"))
        with st.block() as block:
            @block.tensor
            def _(pe):
                for i in range(len(tiles)):
                    pe.wait_ge(squared, i + 1)
                    mm = group_sums(nc, bank[0][:, i * columns:(i + 1) * columns], sq[:, i], selector)
                mm.then_inc(summed, 1)
                fill.pe(pe, steps[0])
                fill.mark()
                pe.wait_ge(rstd_ready, 1)
                for i in range(len(tiles)):
                    spread(nc, bank[1 + i], rstd[:, i * columns:(i + 1) * columns], n, ident).then_inc(spread_ready, 1)
                fill.pe(pe, steps[1])

            @block.scalar
            def _(act):
                for i, tile in enumerate(tiles):
                    nc.scalar.activation(sq[:, i], tile, ACT.Square).then_inc(squared, 1)
                act.wait_ge(mean_ready, 1)
                nc.scalar.activation(root[:], ms[:], ACT.Sqrt).then_inc(root_ready, 1)
                fill.begin(act)
                fill.act(act, fill.marks[0])
                fill.act(act)

            @block.vector
            def _(dve):
                dve.wait_ge(summed, 1)
                nc.vector.tensor_scalar(ms[:], bank[0][:, 0:len(tiles) * columns], n / P, EPS, ALU.mult,
                                        ALU.add).then_inc(mean_ready, 1)
                dve.wait_ge(root_ready, 1)
                nc.vector.reciprocal(rstd[:], root[:]).then_inc(rstd_ready, 1)
                for i, tile in enumerate(tiles):
                    dve.wait_ge(spread_ready, i + 1)
                    nc.vector.scalar_tensor_tensor(tile, tile, gains[i], bank[1 + i][:, 0:width], ALU.mult,
                                                   ALU.mult).then_inc(normed, 1)

            @block.sync
            def _(sp):
                fill.sp(sp)

            @block.gpsimd
            def _(pool):
                fill.w.low_parts(pool)


def second_block(nc, ctx, w, bank, a, x, out, dump, load):
    cols_sb = ctx.enter_context(nc.sbuf_tensor("cols2", [P, sum(COLS2.values())], F32))
    const_sb = ctx.enter_context(nc.sbuf_tensor("const2", [P, sum(CONST2.values())], F32))
    cols, const = Columns(cols_sb, COLS2), Columns(const_sb, CONST2)
    ident = const.whole("ident")
    load("second", [(cols_sb[:], a["cols2"]), (const_sb[:], a["const2"])])

    hT = split_tensor(nc, ctx, "h3T", [P, DT, T])
    y_shape = [P, 4, T]
    tensor, offset = placed(nc, ctx, "yaT", y_shape)
    yT, offsets = [tensor], [offset]
    norm_to_T(nc, w, bank, "norm3", x, TT, cols.whole("norm"), ident, hT, first_unit("rwkv") + RING)
    z_store = nc.dram_tensor("z_store", (FILL2, P, T), F32, kind="Internal").ap()
    st = ctx.enter_context(Stage(nc, "fill2"))
    fill = Filler(nc, st, w, bank[6:8],
                  lambda n: first_unit("fill2") + n if n < FILL2_BEFORE_MEM
                  else first_unit("fill2_rest") + n - FILL2_BEFORE_MEM,
                  [(hT, ACT.Copy, 1.0)] * FILL2, z_store)
    fill.limit = FILL2_BEFORE_MEM
    rwkv_branch(nc, w, bank, a, cols, const, hT, yT[0], dump, load, fill)
    for n in "bc":
        tensor, offset = placed(nc, ctx, f"y{n}T", y_shape)
        yT.append(tensor)
        offsets.append(offset)
    y_low = [same_place(nc, f"y{n}T_low", y_shape, o) for n, o in zip("abc", offsets)]
    sliding_branch(nc, w, bank, a, cols, const, yT[1], dump, load, fill)
    memory_branch(nc, w, bank, a, cols, const, yT[2], dump, load, fill)
    catch_up(nc, fill)
    with ExitStack() as s:
        mergedT = split_tensor(nc, s, "merged2T", [P, DT, T])
        merge_second(nc, w, bank, yT, y_low, z_store, mergedT)
        out_residual(nc, w, bank, "wout2", mergedT, x, sum(n for _, n in UNITS), 1.0, store=out)


def fetch(nc, name, fill, first, z, silu, steps):
    n = z.shape[1]
    with Stage(nc, name) as st, st.block() as block:
        arrived, done = st.sem("arrived"), st.sem("done")

        @block.tensor
        def _(pe):
            fill.pe(pe, steps)

        @block.scalar
        def _(act):
            fill.begin(act)
            act.wait_ge(arrived, 16)
            for k in range(silu, n):
                nc.scalar.activation(z[:, k], z[:, k], ACT.Silu).then_inc(done, 1)
            fill.act(act)

        @block.sync
        def _(sp):
            assert fill.sent >= first + n
            fill.wait_stored(sp)
            sp.dma_start(z, fill.store[first:first + n].rearrange("n p t -> p n t")).then_inc(arrived, 16)
            fill.sp(sp)

        @block.gpsimd
        def _(pool):
            fill.w.low_parts(pool)


def memory_branch(nc, w, bank, a, cols, const, y, dump, load, fill):
    ident, ones = const.whole("ident"), const.whole("ones")
    with ExitStack() as s:
        kT = s.enter_context(nc.sbuf_tensor("kT", [P, 4, MEM], F32))
        v_tok = s.enter_context(nc.sbuf_tensor("vm_tok", [P, 2, 512], F32))
        with ExitStack() as m:
            mem = m.enter_context(nc.sbuf_tensor("mem", [P, 2, D], F32))
            memT = split_tensor(nc, m, "memT", [P, DT, MEM])
            vT = m.enter_context(nc.sbuf_tensor("vT", [P, 4, MEM], F32))
            load("mem", [(mem[:], a["mem"].rearrange("(t p) d -> p t d", p=P))])
            norm_to_T(nc, w, bank, "memnorm", mem, 2, cols.whole("memnorm"), ident, memT, 0, fill=fill,
                      steps=14)
            catch_up(nc, fill)
            project_tiles(nc, w, bank, "memkv", "mem", 8, memT,
                          [(ACT.Copy, kT[:, n]) for n in range(4)] + [(ACT.Copy, vT[:, n]) for n in range(4)],
                          first_unit("fill2_rest") + RING)
            turn_tiles(nc, w, bank, "turn_vm", [([vT[:, n, c * P:(c + 1) * P] for n in range(4)], v_tok[:, c])
                                                for c in range(2)], ident, first_unit("fill2_rest") + RING)
        fill.limit = FILL2
        rms_over_partitions(nc, bank, "knorm", [kT[:, n] for n in range(4)], 4 * [cols.whole("xk_g")], ones[:, 0:1],
                            ident, fill, (3, 6))
        qz = s.enter_context(nc.sbuf_tensor("xqz", [P, 8, T], F32))
        fetch(nc, "xqz", fill, 14, qz[:], 4, 8)
        rms_over_partitions(nc, bank, "xqnorm", [qz[:, n] for n in range(4)], 4 * [cols.whole("xq_g")], ones[:, 0:1],
                            ident, fill, (2, 8))
        units = [dict(q=qz[:, h, b * P:(b + 1) * P], k=kT[:, h], bias=None,
                      v=[v_tok[:, c, h * P:(h + 1) * P] for c in range(2)], half=0) for b in range(TT) for h in range(4)]
        attention(nc, bank, "attn3", units, scale=P ** -0.5, sink=None, ident=ident,
                  out=lambda g: y[:, :, g * P:(g + 1) * P], group=4, dim=P, fill=fill, fill_steps=1)
        multiply(nc, "xgate", y, qz[:, 4:8])
    dump("yc", y)


def multiply(nc, name, to, by):
    with Stage(nc, name) as st, st.block() as block:
        @block.vector
        def _(dve):
            nc.vector.tensor_tensor(to[:], to[:], by, ALU.mult)


def sliding_branch(nc, w, bank, a, cols, const, y, dump, load, fill):
    ident = const.whole("ident")
    with ExitStack() as s:
        z = s.enter_context(nc.sbuf_tensor("swz", [P, 10, T], F32))
        v_tok = s.enter_context(nc.sbuf_tensor("vs_tok", [P, TT, P], F32))
        sink8 = s.enter_context(nc.sbuf_tensor("sink8_2", [P, 8], F32))
        fetch(nc, "swz", fill, 4, z[:], 6, 14)
        rms_over_partitions(nc, bank, "sqknorm", [z[:, n] for n in range(5)], 4 * [cols.whole("q_g")] + [cols.whole("k_g")],
                            const.whole("halves")[:, 0:P:HD], ident, fill, (3, 10))
        turn_tiles(nc, w, bank, "turn_vs", [([z[:, 5, t * P:(t + 1) * P]], v_tok[:, t]) for t in range(TT)], ident, 0)
        rotate(nc, bank, a, cols, const, z, load, fill)
        with Stage(nc, "sink2") as st, st.block() as block:
            @block.vector
            def _(dve):
                nc.vector.tensor_scalar(sink8[:], cols.whole("sinks"), float(HD ** 0.5), None, ALU.mult)
        units = []
        for b in range(TT):
            lo = max(b - 1, 0)
            for i in range(4):
                for e in range(2):
                    h, part = HEADS2[i][e], slice(e * HD, (e + 1) * HD)
                    units.append(dict(q=z[part, i, b * P:(b + 1) * P], k=z[part, 4, lo * P:(b + 1) * P],
                                      bias=(const.whole("band")[:, (lo - b + 1) * P:2 * P], 1.0),
                                      v=[v_tok[:, c, part] for c in range(lo, b + 1)],
                                      sink=cols("sinks", h), sink_scaled=sink8[:, h:h + 1], half=e))
        attention(nc, bank, "attn2", units, scale=HD ** -0.5, sink=True, ident=ident,
                  out=lambda g: y[:, :, g * P:(g + 1) * P], group=8, dim=HD, fill=fill, fill_steps=1)
        multiply(nc, "sgate", y, z[:, 6:10])
    dump("yb", y)


def rotate(nc, bank, a, cols, const, z, load, fill):
    two_pi = 2 * np.pi
    c1 = 6.28125
    c2 = float(np.float32(np.floor((two_pi - c1) * 2 ** 22) / 2 ** 22))
    c3 = float(two_pi - c1 - c2)
    magic = 1.5 * 2 ** 23
    with Stage(nc, "rope") as st:
        pos = st.sb("pos", [P, T], I32)
        angle, turns, count, part, trig = (st.sb(n, [P, T]) for n in ("angle", "turns", "count", "part", "trig"))
        sin, cos = st.sb("sin", [P, T]), st.sb("cos", [P, T])
        straight = st.sb("straight", [P, 2, T])
        crossed = st.sb("crossed", [P, 2, T])
        step_done, reduced, trig_ready, swapped, taken = (st.sem(n) for n in (
            "step_done", "reduced", "trig_ready", "swapped", "taken"))
        load("positions", [(pos[:], a["positions"])])
        with st.block() as block:
            @block.vector
            def _(dve):
                do = Chain(dve, step_done)
                do(nc.vector.tensor_copy(angle[:], pos[:]))
                do(nc.vector.tensor_scalar(angle[:], angle[:], cols("inv"), None, ALU.mult))
                for n, (shift, quarter) in enumerate(((0.0, 0.0), (0.25, np.pi / 2))):
                    do(nc.vector.tensor_scalar(turns[:], angle[:], 1.0 / two_pi, shift, ALU.mult, ALU.add))
                    do(nc.vector.tensor_scalar(count[:], turns[:], magic, None, ALU.add))
                    do(nc.vector.tensor_scalar(count[:], count[:], -magic, None, ALU.add))
                    do(nc.vector.scalar_tensor_tensor(part[:], count[:], -c1, angle[:], ALU.mult, ALU.add))
                    do(nc.vector.scalar_tensor_tensor(part[:], count[:], -c2, part[:], ALU.mult, ALU.add))
                    do(nc.vector.scalar_tensor_tensor(part[:], count[:], -c3, part[:], ALU.mult, ALU.add))
                    if n:
                        dve.wait_ge(trig_ready, n)
                    do(nc.vector.tensor_scalar(trig[:], part[:], float(quarter), 3.1415925, ALU.add, ALU.min))
                    nc.vector.tensor_scalar(trig[:], trig[:], -3.1415925, None, ALU.max).then_inc(reduced, 1)
                for i in range(5):
                    dve.wait_ge(trig_ready, 2)
                    dve.wait_ge(swapped, i + 1)
                    if i >= 2:
                        dve.wait_ge(taken, i - 1)
                    do(nc.vector.tensor_tensor(crossed[:, i % 2], bank[i][:], sin[:], ALU.mult))
                    do(nc.vector.tensor_tensor(straight[:, i % 2], z[:, i], cos[:], ALU.mult))
                    nc.vector.tensor_tensor(z[:, i], straight[:, i % 2], crossed[:, i % 2], ALU.add).then_inc(taken, 1)

            @block.tensor
            def _(pe):
                for i in range(5):
                    nc.tensor.matmul(bank[i][:], const.whole("swap"), z[:, i], start=True, stop=True).then_inc(swapped, 1)
                fill.pe(pe, 18)

            @block.scalar
            def _(act):
                fill.begin(act)
                for n, to in enumerate((sin, cos)):
                    act.wait_ge(reduced, n + 1)
                    nc.scalar.activation(to[:], trig[:], ACT.Sin).then_inc(trig_ready, 1)
                fill.act(act)

            @block.sync
            def _(sp):
                fill.sp(sp)

            @block.gpsimd
            def _(pool):
                fill.w.low_parts(pool)


def rwkv_branch(nc, w, bank, a, cols, const, hT, y, dump, load, fill):
    ident, halves = const.whole("ident"), const.whole("halves")
    with ExitStack() as s:
        sb = lambda n, shape: s.enter_context(nc.sbuf_tensor(f"rw_{n}", shape, F32))
        bonus = sb("bonus", [P, 4, T])
        r_end = sb("r_end", [P, 4, T // CH])
        R = sb("R", [P, 4, T])
        A = sb("A", [P, 4, T])
        B = sb("B", [P, 4, T])
        Kt = sb("K", [P, 4, T])
        toks = {n: sb(f"{n}_tok", [P, TT, 512]) for n in "ABKV"}
        with ExitStack() as s2:
            z = s2.enter_context(nc.sbuf_tensor("rwz", [P, 13, T + 1], F32))
            project_tiles(nc, w, bank, "rwz", "rwkv", 13, hT, [(ACT.Copy, z[:, n, 1:T + 1]) for n in range(13)],
                          first_unit("fill2") + RING, [(toks["V"][:, 0], a["lora"]), (toks["V"][:, 1], a["rows2"])])
            rwkv_prepare(nc, bank, a, cols, const, z, R, A, B, Kt, bonus, r_end, toks, load, fill)
            turn_tiles(nc, w, bank, "turn_rw",
                       [([m[:, n, o + t * P:o + (t + 1) * P] for n in range(4)], toks[name][:, t])
                        for name, m, o in (("A", A, 0), ("B", B, 0), ("K", Kt, 0), ("V", z[:, 8:12], 1))
                        for t in range(TT)], ident, 0)
        ZW = sb("ZW", [P, TT, 8, 2 * CH])
        WT = sb("WT", [P, TT, 4, P])
        for t in range(TT):
            rwkv_solve(nc, bank, const, t, A, B, Kt, toks, ZW, WT, y, fill)
        S = sb("S", [P, T // CH + 1, 4, CH])
        rwkv_chain(nc, bank, const, toks, ZW, r_end, S, fill)
        for t in range(TT):
            rwkv_output(nc, bank, const, t, R, B, Kt, toks, ZW, WT, S, y, fill)
        gate = toks["A"]
        fetch(nc, "rwgate", fill, 0, gate[:], 0, 3)
        rwkv_finish(nc, bank, cols, halves, ident, y, bonus, gate, toks["B"], dump, fill)


def rwkv_prepare(nc, bank, a, cols, const, z, R, A, B, Kt, bonus, r_end, toks, load, fill):
    halves = const.whole("halves")
    with Stage(nc, "rwprep") as st:
        lora, w0, tl, tmp = toks["V"][:, 0], toks["V"][:, 1], toks["V"][:, 2], toks["K"][:, 0:2]
        rate, aa = toks["A"], toks["B"]
        inv = Kt
        zero, step_done, mixed, tanh_ready = st.sem("zero"), st.sem("step_done"), st.sem("mixed"), st.sem("tanh_ready")
        lora_ready, biased, rate_ready, a_ready = st.sem("lora_ready"), st.sem("biased"), st.sem("rate_ready"), st.sem("a_ready")
        with st.block() as block:
            @block.vector
            def _(dve):
                do = Chain(dve, step_done)
                do(nc.vector.memset(z[:, :, 0:1], 0.0))
                for n in [12] + list(range(12)):
                    do(nc.vector.tensor_tensor(tmp[:, n % 2], z[:, n, 0:T], z[:, n, 1:T + 1], ALU.subtract))
                    ins = nc.vector.scalar_tensor_tensor(z[:, n, 1:T + 1], tmp[:, n % 2], cols("mu", n), z[:, n, 1:T + 1],
                                                         ALU.mult, ALU.add)
                    if n == 12:
                        ins.then_inc(mixed, 1)
                        dve.wait_ge(mixed, 1)
                    else:
                        do(ins)
                    if n == 2:
                        for t in range(TT):
                            dve.wait_ge(lora_ready, t + 1)
                            nc.vector.tensor_tensor(rate[:, t], bank[t][:], w0, ALU.add).then_inc(biased, 1)

            @block.tensor
            def _(pe):
                pe.wait_ge(tanh_ready, 1)
                for t in range(TT):
                    nc.tensor.matmul(bank[t][:], tl[0:CH, t * P:(t + 1) * P], lora[0:CH, :], start=True,
                                     stop=True).then_inc(lora_ready, 1)
                fill.pe(pe, 6)
                for c in range(4):
                    if c >= 2:
                        pe.wait_ge(a_ready, c - 1)
                    nc.tensor.matmul(bank[4 + c % 2][:], lora[CH:P, c * P:(c + 1) * P], z[CH:P, 12, 1:T + 1], start=True,
                                     stop=True).then_inc(lora_ready, 1)
                fill.pe(pe, 19)

            @block.scalar
            def _(act):
                fill.begin(act)
                act.wait_ge(mixed, 1)
                nc.scalar.activation(tl[0:CH], z[0:CH, 12, 1:T + 1], ACT.Tanh).then_inc(tanh_ready, 1)
                for t in range(TT):
                    act.wait_ge(biased, t + 1)
                    nc.scalar.activation(rate[:, t], rate[:, t], ACT.Sigmoid).then_inc(rate_ready, 1)
                for c in range(4):
                    act.wait_ge(lora_ready, TT + c + 1)
                    nc.scalar.activation(aa[:, c], bank[4 + c % 2][:], ACT.Sigmoid, bias=cols("a0", c)).then_inc(a_ready, 1)
                fill.act(act)

            @block.sync
            def _(sp):
                fill.sp(sp)

            @block.gpsimd
            def _(pool):
                fill.w.low_parts(pool)
        cum_ready, exp_ready = st.sem("cum_ready"), st.sem("exp_ready")
        with st.block() as block:
            @block.tensor
            def _(pe):
                for e, mask in enumerate(("incl", "strict")):
                    for c in range(4):
                        if e and c >= 2:
                            pe.wait_ge(exp_ready, 8 + c - 1)
                        for t in range(TT):
                            mm = nc.tensor.matmul(bank[4 * e + (c % 2 if e else c)][:, t * P:(t + 1) * P], rate[:, t, c * P:(c + 1) * P],
                                                  const.whole(mask), start=True, stop=True)
                        mm.then_inc(cum_ready, 1)
                fill.pe(pe, 6)

            @block.scalar
            def _(act):
                fill.begin(act)
                for c in range(4):
                    act.wait_ge(cum_ready, c + 1)
                    nc.scalar.activation(R[:, c], bank[c][:], ACT.Exp, scale=-DECAY).then_inc(exp_ready, 1)
                    nc.scalar.activation(inv[:, c], bank[c][:], ACT.Exp, scale=DECAY).then_inc(exp_ready, 1)
                for c in range(4):
                    act.wait_ge(cum_ready, 4 + c + 1)
                    nc.scalar.activation(A[:, c], bank[4 + c % 2][:], ACT.Exp, scale=-DECAY).then_inc(exp_ready, 1)
                fill.act(act)

            @block.sync
            def _(sp):
                fill.sp(sp)

            @block.gpsimd
            def _(pool):
                fill.w.low_parts(pool)
        kk_ready, squared, norm_ready, root_ready, k_done, rk_ready, bonus_ready = (st.sem(n) for n in (
            "kk_ready", "squared", "norm_ready", "root_ready", "k_done", "rk_ready", "bonus_ready"))
        inv_norm_ready, spread_ready = st.sem("inv_norm_ready"), st.sem("spread_ready")
        root, norm, inv_norm = (st.sb(n, [P, 4 * 2 * TT]) for n in ("root", "norm", "inv_norm"))
        with st.block() as block:
            @block.vector
            def _(dve):
                do = Chain(dve, k_done)
                zr, zk, zv = ([z[:, n + c, 1:T + 1] for c in range(4)] for n in (0, 4, 8))
                do(nc.vector.tensor_copy(r_end[:], R[:, :, CH - 1:T:CH]))
                for c in range(4):
                    nc.vector.tensor_scalar(B[:, c], zk[c], cols("k_k", c), None, ALU.mult).then_inc(kk_ready, 1)
                dve.wait_ge(root_ready, 1)
                do(nc.vector.tensor_scalar(norm[:], root[:], 1e-12, None, ALU.max))
                nc.vector.reciprocal(inv_norm[:], norm[:]).then_inc(inv_norm_ready, 1)
                for c in range(4):
                    dve.wait_ge(spread_ready, c + 1)
                    do(nc.vector.tensor_tensor(B[:, c], B[:, c], bank[c][:], ALU.mult))
                    do(nc.vector.scalar_tensor_tensor(A[:, c], B[:, c], -1.0, A[:, c], ALU.mult, ALU.mult))
                    do(nc.vector.tensor_tensor(B[:, c], B[:, c], aa[:, c], ALU.mult))
                    do(nc.vector.tensor_tensor(B[:, c], B[:, c], inv[:, c], ALU.mult))
                    do(nc.vector.tensor_scalar(aa[:, c], aa[:, c], -1.0, cols("k_a", c), ALU.add, ALU.mult))
                    do(nc.vector.scalar_tensor_tensor(zk[c], aa[:, c], 1.0, zk[c], ALU.add, ALU.mult))
                    do(nc.vector.tensor_tensor(Kt[:, c], zk[c], inv[:, c], ALU.mult))
                    do(nc.vector.tensor_tensor(bonus[:, c], zr[c], zk[c], ALU.mult))
                    nc.vector.tensor_scalar(bonus[:, c], bonus[:, c], cols("r_k", c), None, ALU.mult).then_inc(rk_ready, 1)
                    do(nc.vector.tensor_tensor(R[:, c], zr[c], R[:, c], ALU.mult))
                for c in range(4):
                    dve.wait_ge(bonus_ready, c + 1)
                    do(nc.vector.tensor_tensor(bonus[:, c], bank[c][:], zv[c], ALU.mult))

            @block.tensor
            def _(pe):
                for c in range(4):
                    pe.wait_ge(squared, c + 1)
                    mm = group_sums(nc, bank[4][:, c * 2 * TT:(c + 1) * 2 * TT], rate[:, c], halves[:, 0:P:HD])
                mm.then_inc(norm_ready, 1)
                fill.pe(pe, 3)
                pe.wait_ge(inv_norm_ready, 1)
                for c in range(4):
                    spread(nc, bank[c], inv_norm[:, c * 2 * TT:(c + 1) * 2 * TT], 2, const.whole("ident")
                           ).then_inc(spread_ready, 1)
                fill.pe(pe, 5)
                for c in range(4):
                    pe.wait_ge(rk_ready, c + 1)
                    nc.tensor.matmul(bank[c][:], halves, bonus[:, c], start=True, stop=True).then_inc(bonus_ready, 1)
                    fill.pe(pe, 11 if c < 3 else 4)

            @block.scalar
            def _(act):
                fill.begin(act)
                for c in range(4):
                    act.wait_ge(kk_ready, c + 1)
                    nc.scalar.activation(rate[:, c], B[:, c], ACT.Square).then_inc(squared, 1)
                act.wait_ge(norm_ready, 1)
                nc.scalar.activation(root[:], bank[4][:, 0:4 * 2 * TT], ACT.Sqrt).then_inc(root_ready, 1)
                fill.act(act)

            @block.sync
            def _(sp):
                fill.sp(sp)

            @block.gpsimd
            def _(pool):
                fill.w.low_parts(pool)


def head(o):
    half, c = o // 4, o % 4
    return slice(half * HD, (half + 1) * HD), c, slice((2 * c + half) * HD, (2 * c + half + 1) * HD)


def by_head(tok):
    return tok.rearrange("p (c e v) -> p e c v", c=4, e=2)


def over_heads(mask, n=4):
    return mask.unsqueeze(1).broadcast_to([P, n, P])


def rwkv_solve(nc, bank, const, t, A, B, Kt, toks, ZW, WT, y, fill):
    ident = const.whole("ident")
    here = slice(t * P, (t + 1) * P)
    with Stage(nc, f"solve{t}") as st:
        AB, AK = st.sb("AB", [P, 8, P]), st.sb("AK", [P, 8, P])
        Tm, TmT, G = (st.sb(n, [P, 8, P]) for n in ("T", "TT", "G"))
        E, QA = (y[:, 2 * n:2 * n + 2].rearrange("p a (b c) -> p (a b) c", c=P) for n in range(2))
        step_done, products, turned, g_kept, filled = (st.sem(n) for n in (
            "step_done", "products", "turned", "g_kept", "filled"))
        with st.block() as block:
            @block.tensor
            def _(pe):
                for e, left in enumerate((B, Kt)):
                    for h in range(8):
                        part, c, cols = head(h)
                        mm = nc.tensor.matmul(bank[2 * e + h // 4][:, h % 4 * P:(h % 4 + 1) * P], left[part, c, here],
                                              A[part, c, here], start=True, stop=True)
                        if h % 4 == 3:
                            mm.then_inc(products, 1)
                fill.pe(pe, 5)
                fill.mark()
                pe.wait_ge(step_done, 6)
                for h in range(8):
                    mm = nc.tensor.transpose(bank[4 + h // 4][:, h % 4 * P:(h % 4 + 1) * P], TmT[:, h], ident)
                mm.then_inc(turned, 1)
                for h in range(8):
                    _, _, cols = head(h)
                    mm = nc.tensor.matmul(bank[0][:, h * CH:(h + 1) * CH], AK[:, h], toks["V"][:, t, cols],
                                          start=True, stop=True)
                mm.then_inc(turned, 1)
                fill.pe(pe, 3)

            @block.vector
            def _(dve):
                do = Chain(dve, step_done)
                for n, to in enumerate((AB, AB, AK, AK)):
                    dve.wait_ge(products, n + 1)
                    g = n % 2
                    do(nc.vector.tensor_tensor(to[:, 4 * g:4 * g + 4], bank[n][:].rearrange("p (h t) -> p h t", h=4),
                                               over_heads(const.whole("strict")), ALU.mult))
                do(nc.vector.tensor_tensor(TmT[:], AB[:], over_heads(const("level", 0, P), 8), ALU.mult))
                do(nc.vector.tensor_tensor(TmT[:], TmT[:], over_heads(ident, 8), ALU.add))

            @block.scalar
            def _(act):
                fill.begin(act)
                fill.act(act, fill.marks[0])
                act.wait_ge(turned, 1)
                for g in range(2):
                    nc.scalar.activation(Tm[:, 4 * g:4 * g + 4], bank[4 + g][:].rearrange("p (h t) -> p h t", h=4),
                                         ACT.Copy).then_inc(filled, 1)
                act.wait_ge(turned, 2)
                nc.scalar.activation(QA[:, :, 0:CH], bank[0][:].rearrange("p (h t) -> p h t", h=8), ACT.Copy
                                     ).then_inc(filled, 1)
                for e in range(2):
                    nc.scalar.activation(QA[:, 4 * e:4 * e + 4, CH:2 * CH], by_head(toks["A"][:, t])[:, e], ACT.Copy
                                         ).then_inc(filled, 1)
                fill.act(act)

            @block.sync
            def _(sp):
                fill.sp(sp)

            @block.gpsimd
            def _(pool):
                fill.w.low_parts(pool)
        g_ready, d_ready, added, masked = (st.sem(n) for n in ("g_ready", "d_ready", "added", "masked"))
        with st.block() as block:
            @block.tensor
            def _(pe):
                for m in range(1, LEVELS):
                    for g in range(2):
                        pe.wait_ge(masked, m)
                        if m > 1:
                            pe.wait_ge(added, 2 * (m - 2) * 2 + 2 * g + 2)
                        for h in range(4 * g, 4 * g + 4):
                            mm = nc.tensor.matmul(bank[g][:, h % 4 * P:(h % 4 + 1) * P], E[:, h], Tm[:, h], start=True,
                                                  stop=True)
                        mm.then_inc(g_ready, 1)
                    fill.pe(pe, 1)
                    for g in range(2):
                        pe.wait_ge(g_kept, 2 * (m - 1) + g + 1)
                        for e in range(m == LEVELS - 1, 2):
                            for h in range(4 * g, 4 * g + 4):
                                mm = nc.tensor.matmul(bank[2 + 2 * g + e][:, h % 4 * P:(h % 4 + 1) * P],
                                                      G[:, h] if e else TmT[:, h], TmT[:, h] if e else G[:, h],
                                                      start=True, stop=True)
                            mm.then_inc(d_ready, 1)
                    fill.pe(pe, 3)
                    fill.mark()

            @block.vector
            def _(dve):
                for m in range(1, LEVELS):
                    if m > 1:
                        dve.wait_ge(g_ready, 2 * (m - 1))
                    nc.vector.tensor_tensor(E, AB[:], over_heads(const("level", m * P, P), 8), ALU.mult
                                            ).then_inc(masked, 1)
                    for g in range(2):
                        for e, to in enumerate((Tm, TmT)):
                            if m == LEVELS - 1 and e == 0:
                                continue
                            dve.wait_ge(d_ready, 4 * (m - 1) + (g + 1 if m == LEVELS - 1 else 2 * g + 2))
                            if m > 1:
                                dve.wait_ge(added, 4 * (m - 2) + 2 * g + e + 1)
                            nc.vector.tensor_tensor(to[:, 4 * g:4 * g + 4], to[:, 4 * g:4 * g + 4],
                                                    bank[2 + 2 * g + e][:].rearrange("p (h t) -> p h t", h=4), ALU.add
                                                    ).then_inc(added, 1)

            @block.scalar
            def _(act):
                fill.begin(act)
                for m in range(1, LEVELS):
                    for g in range(2):
                        act.wait_ge(g_ready, 2 * (m - 1) + g + 1)
                        if m > 1:
                            act.wait_ge(d_ready, 4 * (m - 2) + 2 * g + 2)
                        nc.scalar.activation(G[:, 4 * g:4 * g + 4], bank[g][:].rearrange("p (h t) -> p h t", h=4),
                                             ACT.Copy).then_inc(g_kept, 1)
                    if m > 1:
                        fill.act(act, fill.marks[m - 2])
                fill.act(act)

            @block.sync
            def _(sp):
                fill.sp(sp)

            @block.gpsimd
            def _(pool):
                fill.w.low_parts(pool)
        zw_ready, zw_kept = st.sem("zw_ready"), st.sem("zw_kept")
        with st.block() as block:
            @block.tensor
            def _(pe):
                for g in range(2):
                    for h in range(4 * g, 4 * g + 4):
                        mm = nc.tensor.matmul(bank[g][:, h % 4 * P:(h % 4 + 1) * P], TmT[:, h], QA[:, h], start=True,
                                              stop=True)
                    mm.then_inc(zw_ready, 1)
                for h in range(8):
                    part, c, cols = head(h)
                    mm = nc.tensor.matmul(bank[2][part, c * P:(c + 1) * P], toks["A"][:, t, cols],
                                          TmT[:, h], start=True, stop=True)
                mm.then_inc(zw_ready, 1)
                fill.pe(pe, 1)

            @block.scalar
            def _(act):
                fill.begin(act)
                for g in range(2):
                    act.wait_ge(zw_ready, g + 1)
                    nc.scalar.activation(ZW[:, t, 4 * g:4 * g + 4], bank[g][:].rearrange("p (h t) -> p h t", h=4), ACT.Copy
                                         ).then_inc(zw_kept, 1)
                act.wait_ge(zw_ready, 3)
                nc.scalar.activation(WT[:, t], bank[2][:].rearrange("p (c t) -> p c t", c=4), ACT.Copy).then_inc(zw_kept, 1)
                fill.act(act)

            @block.sync
            def _(sp):
                fill.sp(sp)

            @block.gpsimd
            def _(pool):
                fill.w.low_parts(pool)


def rwkv_chain(nc, bank, const, toks, ZW, r_end, S, fill):
    n = T // CH
    with Stage(nc, "chain") as st:
        H = st.sb("H", [P, 2, 4, CH])
        new = st.sb("new", [P, 2, 4, CH])
        old = st.sb("old", [P, 4, CH])
        parts_ready, h_kept, new_kept, s_sum, scaled, s_ready = (st.sem(n) for n in (
            "parts_ready", "h_kept", "new_kept", "s_sum", "scaled", "s_ready"))
        tiles = lambda b, at: b[:, at:at + 4 * CH].rearrange("p (c k) -> p c k", c=4)
        with st.block() as block:
            @block.tensor
            def _(pe):
                def parts(ch):
                    rows, t = slice(ch % 2 * CH, (ch % 2 + 1) * CH), ch // 2
                    if ch >= 2:
                        pe.wait_ge(new_kept, ch - 1)
                    for o in range(8):
                        part, c, cols = head(o)
                        nc.tensor.matmul(bank[ch % 2][part, c * CH:(c + 1) * CH], ZW[rows, t, o, CH:2 * CH],
                                         toks["B"][rows, t, cols], start=True, stop=True)
                        to = bank[ch % 2][part, (4 + c) * CH:(5 + c) * CH]
                        nc.tensor.matmul(to, toks["B"][rows, t, cols], ZW[rows, t, o, 0:CH], start=True, stop=False)
                        mm = nc.tensor.matmul(to, toks["K"][rows, t, cols], toks["V"][rows, t, cols], start=False, stop=True)
                    mm.then_inc(parts_ready, 1)

                parts(0)
                for ch in range(n):
                    if ch + 1 < n:
                        parts(ch + 1)
                    fill.pe(pe, 1)
                    pe.wait_ge(h_kept, ch + 1)
                    pe.wait_ge(s_ready, ch + 1)
                    for o in range(8):
                        part, c, _ = head(o)
                        mm = nc.tensor.matmul(bank[2 + ch % 2][part, c * CH:(c + 1) * CH], H[part, ch % 2, c],
                                              S[part, ch, c], start=True, stop=True)
                    mm.then_inc(s_sum, 1)

            @block.vector
            def _(dve):
                def keep(ch):
                    dve.wait_ge(parts_ready, ch + 1)
                    if ch >= 2:
                        dve.wait_ge(s_sum, ch - 1)
                        dve.wait_ge(s_ready, ch)
                    nc.vector.tensor_tensor(H[:, ch % 2], tiles(bank[ch % 2], 0),
                                            const.whole("eye2").unsqueeze(1).broadcast_to([P, 4, CH]), ALU.add
                                            ).then_inc(h_kept, 1)
                    nc.vector.tensor_tensor(new[:, ch % 2], tiles(bank[ch % 2], 4 * CH),
                                            r_end[:, :, ch:ch + 1].broadcast_to([P, 4, CH]), ALU.mult).then_inc(new_kept, 1)

                nc.vector.memset(S[:, 0], 0.0).then_inc(s_ready, 1)
                keep(0)
                for ch in range(n):
                    if ch + 1 < n:
                        keep(ch + 1)
                    dve.wait_ge(s_sum, ch + 1)
                    if ch:
                        dve.wait_ge(s_ready, ch + 1)
                    nc.vector.tensor_tensor(old[:], tiles(bank[2 + ch % 2], 0),
                                            r_end[:, :, ch:ch + 1].broadcast_to([P, 4, CH]), ALU.mult).then_inc(scaled, 1)
                    dve.wait_ge(scaled, ch + 1)
                    dve.wait_ge(new_kept, ch + 1)
                    nc.vector.tensor_tensor(S[:, ch + 1], old[:], new[:, ch % 2], ALU.add).then_inc(s_ready, 1)

            @block.scalar
            def _(act):
                fill.begin(act)
                fill.act(act)

            @block.sync
            def _(sp):
                fill.sp(sp)

            @block.gpsimd
            def _(pool):
                fill.w.low_parts(pool)


def rwkv_output(nc, bank, const, t, R, B, Kt, toks, ZW, WT, S, y, fill):
    here = slice(t * P, (t + 1) * P)
    with Stage(nc, f"rwout{t}") as st:
        RB, RK = st.sb("RB", [P, 8, P]), st.sb("RK", [P, 8, P])
        U = st.sb("U", [P, 8, CH])
        products, masked, u_sum, u_ready, y_ready, y_kept = (st.sem(n) for n in (
            "products", "masked", "u_sum", "u_ready", "y_ready", "y_kept"))
        with st.block() as block:
            @block.tensor
            def _(pe):
                for h in range(8):
                    part, c, cols = head(h)
                    for e in range(2):
                        mm = nc.tensor.matmul(bank[4 + h // 4][e * CH:(e + 1) * CH, c * CH:(c + 1) * CH],
                                              WT[part, t, c, e * CH:(e + 1) * CH], S[part, 2 * t + e, c], start=True,
                                              stop=True)
                mm.then_inc(u_sum, 1)
                for e, left in enumerate((B, Kt)):
                    for h in range(8):
                        part, c, cols = head(h)
                        mm = nc.tensor.matmul(bank[2 * e + h // 4][:, h % 4 * P:(h % 4 + 1) * P], left[part, c, here],
                                              R[part, c, here], start=True, stop=True)
                        if h % 4 == 3:
                            mm.then_inc(products, 1)
                fill.pe(pe, 3)
                pe.wait_ge(u_ready, 2)
                pe.wait_ge(masked, 4)
                for h in range(8):
                    part, c, cols = head(h)
                    nc.tensor.matmul(bank[4][part, c * P:(c + 1) * P], U[:, h], RB[:, h], start=True, stop=False)
                    nc.tensor.matmul(bank[4][part, c * P:(c + 1) * P], toks["V"][:, t, cols], RK[:, h],
                                     start=False, stop=False)
                    for e in range(2):
                        mm = nc.tensor.matmul(bank[4][part, c * P + e * CH:c * P + (e + 1) * CH], S[part, 2 * t + e, c],
                                              R[part, c, t * P + e * CH:t * P + (e + 1) * CH], start=False, stop=(e == 1))
                mm.then_inc(y_ready, 1)
                fill.pe(pe, 1)

            @block.vector
            def _(dve):
                dve.wait_ge(u_sum, 1)
                for e in range(2):
                    nc.vector.tensor_tensor(U[:, 4 * e:4 * e + 4],
                                            bank[4 + e][:, 0:4 * CH].rearrange("p (h v) -> p h v", h=4),
                                            ZW[:, t, 4 * e:4 * e + 4, 0:CH], ALU.add).then_inc(u_ready, 1)
                for n, to in enumerate((RB, RB, RK, RK)):
                    dve.wait_ge(products, n + 1)
                    g = n % 2
                    nc.vector.tensor_tensor(to[:, 4 * g:4 * g + 4], bank[n][:].rearrange("p (h t) -> p h t", h=4),
                                            over_heads(const.whole("incl")), ALU.mult).then_inc(masked, 1)

            @block.scalar
            def _(act):
                fill.begin(act)
                act.wait_ge(y_ready, 1)
                nc.scalar.activation(y[:, :, here], bank[4][:].rearrange("p (c t) -> p c t", c=4), ACT.Copy
                                     ).then_inc(y_kept, 1)
                fill.act(act)

            @block.sync
            def _(sp):
                fill.sp(sp)

            @block.gpsimd
            def _(pool):
                fill.w.low_parts(pool)


def rwkv_finish(nc, bank, cols, halves, ident, y, bonus, gate, sq, dump, fill):
    with Stage(nc, "rwfin") as st:
        mean = st.sb("mean", [P, T])
        var, root, rstd = (st.sb(n, [P, 4 * 2 * TT]) for n in ("var", "root", "rstd"))
        selector = halves[:, 0:P:HD]
        rstd_ready, spread_ready = st.sem("rstd_ready"), st.sem("spread_ready")
        step_done, summed, centred, squared, var_ready, root_ready = (st.sem(n) for n in (
            "step_done", "summed", "centred", "squared", "var_ready", "root_ready"))
        with st.block() as block:
            @block.tensor
            def _(pe):
                for c in range(4):
                    nc.tensor.matmul(bank[c][:], halves, y[:, c], start=True, stop=True).then_inc(summed, 1)
                fill.pe(pe, 1)
                for c in range(4):
                    pe.wait_ge(squared, c + 1)
                    mm = group_sums(nc, bank[4][:, c * 2 * TT:(c + 1) * 2 * TT], sq[:, c], selector)
                mm.then_inc(summed, 1)
                fill.pe(pe, 5)
                fill.mark()
                pe.wait_ge(rstd_ready, 1)
                for c in range(4):
                    spread(nc, bank[c], rstd[:, c * 2 * TT:(c + 1) * 2 * TT], 2, ident).then_inc(spread_ready, 1)
                fill.pe(pe, 14)

            @block.scalar
            def _(act):
                fill.begin(act)
                for c in range(4):
                    act.wait_ge(centred, c + 1)
                    nc.scalar.activation(sq[:, c], y[:, c], ACT.Square).then_inc(squared, 1)
                act.wait_ge(var_ready, 1)
                nc.scalar.activation(root[:], var[:], ACT.Sqrt).then_inc(root_ready, 1)
                fill.act(act, fill.marks[0])
                fill.act(act)

            @block.vector
            def _(dve):
                do = Chain(dve, step_done)
                for c in range(4):
                    dve.wait_ge(summed, c + 1)
                    do(nc.vector.tensor_scalar(mean[:], bank[c][:], 1.0 / HD, None, ALU.mult))
                    nc.vector.tensor_tensor(y[:, c], y[:, c], mean[:], ALU.subtract).then_inc(centred, 1)
                    dve.wait_ge(centred, c + 1)
                dve.wait_ge(summed, 5)
                nc.vector.tensor_scalar(var[:], bank[4][:, 0:4 * 2 * TT], 1.0 / HD, LNX_EPS, ALU.mult, ALU.add
                                        ).then_inc(var_ready, 1)
                dve.wait_ge(root_ready, 1)
                nc.vector.reciprocal(rstd[:], root[:]).then_inc(rstd_ready, 1)
                for c in range(4):
                    dve.wait_ge(spread_ready, c + 1)
                    do(nc.vector.scalar_tensor_tensor(y[:, c], y[:, c], cols("lnx_g", c), bank[c][:], ALU.mult, ALU.mult))
                    do(nc.vector.scalar_tensor_tensor(y[:, c], y[:, c], cols("lnx_b", c), bonus[:, c], ALU.add, ALU.add))
                    do(nc.vector.tensor_tensor(y[:, c], y[:, c], gate[:, c], ALU.mult))
            @block.sync
            def _(sp):
                fill.sp(sp)

            @block.gpsimd
            def _(pool):
                fill.w.low_parts(pool)
    dump("ya", y)


def merge_second(nc, w, bank, yT, y_low, z_store, mergedT):
    u0, g0 = first_unit("merge"), FILL2 - 24

    def adds(n):
        return 2 * (n - (n + 2) // 3)

    with Stage(nc, "merge2") as st:
        z = st.sb("z", [P, 3, 2, T])
        y = [Split(st.sb(f"y{b}_high", [P, 4, T]), y_low[b]) for b in range(3)]
        gate = st.sb("gate", [P, 2, 2, T])
        part = st.sb("part", [P, 2, 2, T])
        z_arrived = [st.sem(f"z_arrived{i}") for i in range(3)]
        gate_ready, parts, merged = st.sem("gate_ready"), st.sem("parts"), st.sem("merged")
        y_high, y_split, high_ready = st.sem("y_high"), st.sem("y_split"), st.sem("high_ready")
        with st.block() as block:
            @block.sync
            def _(sp):
                for n in range(12):
                    if n >= 3:
                        sp.wait_ge(gate_ready, n - 2)
                    at = g0 + 2 * n
                    sp.dma_start(z[:, n % 3], z_store[at:at + 2].rearrange("e p t -> p e t")
                                 ).then_inc(z_arrived[n % 3], 16)
                    w.load(sp, u0 + RING + max(n - 1, 0))
                w.load(sp, first_unit("wout2") + RING)

            @block.tensor
            def _(pe):
                for n in range(12):
                    ring = w.wait(pe, u0 + n)
                    if n >= 2:
                        pe.wait_ge(parts, 2 * (n - 1))
                    if n < 3:
                        pe.wait_ge(y_split, n + 1)
                    for e in range(2):
                        for k in range(4):
                            mm = product(nc, bank[2 * (n % 2) + e][:], ring[:, 4 * e + k], y[n % 3][:, k], k == 0, k == 3)
                    mm.then_inc(w.done, 1)

            @block.scalar
            def _(act):
                for n in range(12):
                    if n >= 2:
                        w.finished(act, u0 + n - 2)
                    act.wait_ge(z_arrived[n % 3], 16 * (n // 3 + 1))
                    if n >= 2:
                        act.wait_ge(parts, 2 * (n - 1))
                    nc.scalar.activation(gate[:, n % 2], z[:, n % 3], ACT.Sigmoid).then_inc(gate_ready, 1)
                for n in range(10, 12):
                    w.finished(act, u0 + n)

            @block.gpsimd
            def _(pool):
                w.low_parts(pool)

            @block.vector
            def _(dve):
                for b in range(3):
                    nc.vector.tensor_copy(y[b].high[:].bitcast(F32R), yT[b][:]).then_inc(y_high, 1)
                    dve.wait_ge(y_high, b + 1)
                    nc.vector.tensor_tensor(y_low[b][:].bitcast(F32R), yT[b][:], y[b].high[:], ALU.subtract
                                            ).then_inc(y_split, 1)
                for n in range(12):
                    f = n // 3 * 2
                    dve.wait_ge(gate_ready, n + 1)
                    dve.wait_ge(w.done, u0 + n + 1)
                    for e in range(2):
                        to = mergedT.whole[:, f + e] if n % 3 == 0 else part[:, n % 2, e]
                        if adds(n - 1) > 0:
                            dve.wait_ge(merged, adds(n - 1))
                        nc.vector.tensor_tensor(to, bank[2 * (n % 2) + e][:], gate[:, n % 2, e], ALU.mult
                                                ).then_inc(parts, 1)
                        if n % 3:
                            dve.wait_ge(parts, 2 * n + e + 1)
                            if n % 3 == 2:
                                dve.wait_ge(merged, adds(n))
                            nc.vector.tensor_tensor(mergedT.whole[:, f + e], mergedT.whole[:, f + e], part[:, n % 2, e], ALU.add
                                                    ).then_inc(merged, 1)
                            if n % 3 == 2:
                                dve.wait_ge(merged, adds(n) + e + 1)
                                split_merged(nc, dve, mergedT, f + e, high_ready)


def program(nc, a, out, dump_to=None):
    dumped = []
    with ExitStack() as ctx:
        bank = [ctx.enter_context(nc.psum_tensor(f"bank{i}", [P, 512], F32)) for i in range(8)]
        w = Weights(nc, ctx, a["weights"])
        x = ctx.enter_context(nc.sbuf_tensor("x", [P, TT, D], F32))

        def dump(name, tensor):
            if dump_to is None or name not in dump_to:
                return
            with Stage(nc, f"dump_{name}") as st, st.block() as block:
                s = st.sem("s")

                @block.sync
                def _(sp):
                    sp.dma_start(dump_to[name], tensor[:]).then_inc(s, 16)
                    sp.wait_ge(s, 16)

        def load(name, pairs):
            with Stage(nc, name) as st, st.block() as block:
                s = st.sem("arrived")

                @block.sync
                def _(sp):
                    for to, of in pairs:
                        sp.dma_start(to, of).then_inc(s, 16)
                    sp.wait_ge(s, 16 * len(pairs))

        with ExitStack() as one:
            cols_sb = one.enter_context(nc.sbuf_tensor("cols1", [P, sum(COLS1.values())], F32))
            const_sb = one.enter_context(nc.sbuf_tensor("const1", [P, sum(CONST1.values())], F32))
            rows = one.enter_context(nc.sbuf_tensor("rows1", [P, 2 * D], F32))
            subkeys = one.enter_context(nc.sbuf_tensor("subkeys", [P, 2, NKEYS], F32))
            load("first", [(x[:], a["x"].rearrange("(t p) d -> p t d", p=P)), (cols_sb[:], a["cols1"]),
                           (const_sb[:], a["const1"]), (rows[:], a["rows1"]), (subkeys[:], a["subkeys"])])
            first_block(nc, w, bank, Columns(cols_sb, COLS1), Columns(const_sb, CONST1), rows, subkeys,
                        a["peer_u"], a["peer_v"], x, dump)
        second_block(nc, ctx, w, bank, a, x, out, dump, load)


def constants():
    p, c = np.arange(P)[:, None], np.arange(P)[None, :]
    ident = np.eye(P)
    r, s3 = np.arange(P)[:, None], np.arange(3 * P)[None, :]
    dist = np.abs(r + P - s3).astype(np.float64)
    dist[dist > P] = FAR
    iota = np.broadcast_to(np.tile(np.arange(TOPK), TOPK), (P, TOPK * TOPK))
    const1 = np.concatenate([ident, np.ones((P, P)), dist, iota], 1).astype(np.float32)
    halves = (p // 64 == c // 64)
    swap = np.zeros((P, P))
    for o in range(P):
        if o % 64 < 32:
            swap[o + 32, o] = -1
        else:
            swap[o - 32, o] = 1
    s2 = np.arange(2 * P)[None, :]
    rel = r - s2 + P
    band = np.where((rel >= 0) & (rel < P), 0.0, -1e31)
    same = p // CH == c // CH
    strict, incl = same & (p < c), same & (p <= c)
    levels = [(p // (2 * m) == c // (2 * m)) & (p % (2 * m) < m) & (c % (2 * m) >= m) for m in (1, 2, 4, 8, 16, 32)]
    eye2 = np.concatenate([np.eye(CH), np.eye(CH)], 0)
    const2 = np.concatenate([ident, np.ones((P, P)), halves, swap, band, strict, incl, *levels, eye2], 1).astype(np.float32)
    inv = (10000.0 ** (-np.arange(32) / 32)).astype(np.float32)
    return const1, const2, np.tile(inv, 4)[:, None]


def unit_columns(mat, cols):
    m = mat[:, cols] if cols is not None else mat
    k, n = m.shape[0] // P, m.shape[1] // P
    return m.reshape(k, P, n, P).transpose(2, 1, 0, 3)


def lay_out(i):
    i = {k: np.asarray(v) for k, v in i.items()}
    col = lambda v: v.reshape(-1, P).T
    rep = lambda v: np.broadcast_to(v.reshape(1, -1), (P, v.size))
    full = lambda u: u.reshape(u.shape[0], P, DT * P)
    order1 = np.concatenate([np.arange(HD) + HD * h for pair in HEADS1 for h in pair])
    order2 = np.concatenate([np.arange(HD) + HD * h for pair in HEADS2 for h in pair])

    w_in = i["w_in"][0]
    tile = lambda n: np.arange(P) + n * P
    qkv = np.concatenate([2 * D + order1, np.arange(3 * D, 3 * D + 512)]).reshape(-1, P)
    z1 = [tile(DT), tile(0)]
    for t in range(1, DT):
        if t >= 2:
            z1 += [qkv[2 * t - 4], qkv[2 * t - 3]]
        z1 += [tile(DT + t), tile(t)]
    z1 = np.concatenate(z1)
    gate1 = np.arange(3 * D + 512, 5 * D + 512)
    w2 = i["w_in_2"][0]
    at = np.cumsum([0, 512, 512, 512, 64, 64, 512, 512, 128, 128, 512, 512, 512, 3072])
    rng = lambda a, b: np.arange(at[a], at[b])
    rwkv, rwkv_gate = rng(0, 5), rng(5, 6)
    sw = np.concatenate([at[6] + order2, rng(7, 9), at[9] + order2])
    xq = rng(10, 12)
    proj = [i["w_proj_a_2"][0], i["w_proj_b_2"][0][order2], i["w_proj_c_2"][0]]
    merge, beside = [], [unit_columns(w2, c) for c in (rwkv_gate, sw, xq)]
    gates = [unit_columns(w2, at[12] + D * b + np.arange(D)) for b in range(3)]
    proj = [unit_columns(m, None) for m in proj]
    for f in range(0, DT, 2):
        for b in range(3):
            merge.append(np.concatenate([proj[b][f], proj[b][f + 1]], 1)[None])
            beside.append(gates[b][f:f + 2])
    beside = np.concatenate(beside)
    rows_of = lambda m: m.reshape(DT, P, D)
    weights = np.concatenate([
        full(unit_columns(w_in, z1)), full(unit_columns(w_in, gate1)), full(unit_columns(i["conv_w_pw"][0], None)),
        full(unit_columns(i["attn_w_o"][0][order1], None)), rows_of(i["w_out"][0]),
        full(unit_columns(i["peer_w_query"][0], None)), full(unit_columns(w2, rwkv)),
        full(beside[:FILL2_BEFORE_MEM]), full(unit_columns(i["w_mem_kv_2"][0], None)), full(beside[FILL2_BEFORE_MEM:]),
        *[full(m) for m in merge], rows_of(i["w_out_2"][0])], 0)
    const1, const2, inv = constants()
    two = lambda v: np.concatenate([v, v])[:, None]
    cols1 = np.concatenate([col(i["norm1_g"][0]), col(i["conv_dw_w"][0]), col(i["conv_dw_b"][0]),
                            col(i["conv_ln_g"][0]), col(i["conv_ln_b"][0]), rep(i["attn_sink"][0])], 1)
    cols2 = np.concatenate([
        col(i["norm_g_2"][0]), col(i["mem_norm_g_2"][0]), col(i["mu_rkv_2"][0]), i["mu_wa_2"][0].reshape(P, 1),
        col(i["a0_2"][0]), col(i["k_k_2"][0]), col(i["k_a_2"][0]), col(i["r_k_2"][0]), col(i["lnx_g_2"][0]),
        col(i["lnx_b_2"][0]), two(i["q_norm_g_2"][0]), two(i["k_norm_g_2"][0]), i["xq_norm_g_2"][0][:, None],
        i["xk_norm_g_2"][0][:, None], inv, rep(i["sinks_2"][0])], 1)
    a = dict(x=i["x"][0], weights=weights.reshape(-1, P, DT * P), cols1=cols1, cols2=cols2, const1=const1, const2=const2,
             rows1=np.concatenate([rep(i["norm2_g"][0]), rep(i["final_g"])], 1), rows2=rep(i["w0_2"][0]),
             subkeys=i["peer_sub_keys"][0].transpose(2, 0, 1), peer_u=i["peer_u"][0], peer_v=i["peer_v"][0],
             mem=i["mem_2"][0], lora=np.concatenate([i["w2_2"][0], i["a2_2"][0]], 0),
             positions=np.broadcast_to(i["positions_2"].reshape(1, T), (P, T)))
    return {k: np.ascontiguousarray(v) for k, v in a.items()}


def kernel(**inputs):
    import concourse.bacc as bacc
    from concourse.bass_utils import run_bass_kernel_spmd

    arrays = lay_out(inputs)
    nc = bacc.Bacc("TRN2", target_bir_lowering=False, num_devices=1)
    a = {k: nc.dram_tensor(f"in_{k}", v.shape, mybir.dt.from_np(v.dtype), kind="ExternalInput").ap()
         for k, v in arrays.items()}
    out = nc.dram_tensor("out", (T, D), F32, kind="ExternalOutput").ap()
    program(nc, a, out)
    r = run_bass_kernel_spmd(nc, [{f"in_{k}": v for k, v in arrays.items()}], core_ids=[0])
    return r.results[0]["out"].reshape(1, T, D)
```
